# Optimizing a Trainium2 kernel written in Bass

```python
import math
import jax, jax.numpy as jnp
from jax import lax
import numpy as np

D_MODEL = 2048
BATCH = 1
SEQ = 256
DEPTH = 1

CHUNK = 64
N_META = 16
MIX_WIDTH = D_MODEL
LRU_WIDTH = MIX_WIDTH // 2
LRU_BLOCKS = 8
LRU_BLOCK_W = LRU_WIDTH // LRU_BLOCKS
CONV_W = 4
LRU_C = 8.0
ATT_HEADS = 8
ATT_QK_DIM = (MIX_WIDTH - LRU_WIDTH) // (2 * ATT_HEADS)
ATT_V_DIM = 2 * ATT_QK_DIM
ATT_WIDTH = ATT_HEADS * ATT_V_DIM
QK_WIDTH = ATT_HEADS * 2 * ATT_QK_DIM
IN_PROJ_WIDTH = 2 * LRU_WIDTH + 2 * QK_WIDTH + ATT_WIDTH
Q_BLOCK = 128
N_GROUPS = 4
EXPERTS_PER_GROUP = 4
N_EXPERTS = N_GROUPS * EXPERTS_PER_GROUP
TOP_K_INNER = 2
D_EXPERT = 512
RMS_EPS = 1e-6

kernel_name = "hybrid_rglru_diffattn_hmoe_block"

def rmsnorm(x, g):
    xf = x.astype(jnp.float32)
    y = xf * lax.rsqrt(jnp.mean(xf * xf, axis=-1, keepdims=True) + RMS_EPS)
    return (y * g.astype(jnp.float32)).astype(x.dtype)

def chunk_id(pos):
    return jnp.where(pos < N_META, 0, 1 + (pos - N_META) // CHUNK)

def alibi_slopes(n_heads):
    return jnp.exp2(-8.0 * jnp.arange(1, n_heads + 1, dtype=jnp.float32) / n_heads)

def rg_lru_mixer(u, yg, conv_w, conv_b, wa, ba, wx, bx, lru_a_param):
    B, T, W = u.shape
    up = jnp.pad(u, ((0, 0), (CONV_W - 1, 0), (0, 0)))
    xc = conv_b
    for k in range(CONV_W):
        xc = xc + conv_w[k] * up[:, CONV_W - 1 - k: CONV_W - 1 - k + T]
    xh = xc.reshape(B, T, LRU_BLOCKS, LRU_BLOCK_W)
    r = jax.nn.sigmoid(jnp.einsum('btgi,gij->btgj', xh, wa).reshape(B, T, W) + ba)
    i = jax.nn.sigmoid(jnp.einsum('btgi,gij->btgj', xh, wx).reshape(B, T, W) + bx)
    log_a = (-LRU_C * r.astype(jnp.float32)) * jax.nn.softplus(-lru_a_param.astype(jnp.float32))
    a = jnp.exp(log_a)
    b = jnp.sqrt(-jnp.expm1(2.0 * log_a)) * (i * xc).astype(jnp.float32)

    def combine(left, right):
        a_l, b_l = left
        a_r, b_r = right
        return a_l * a_r, a_r * b_l + b_r

    _, h = lax.associative_scan(combine, (a, b), axis=1)
    return h.astype(u.dtype) * jax.nn.gelu(yg)

def diff_attention(q, k, v, lam, lam_init, subln_g):
    B, T, _ = q.shape
    H, Dh, Dv = ATT_HEADS, ATT_QK_DIM, ATT_V_DIM
    q = q.reshape(B, T, H, 2, Dh).transpose(0, 2, 3, 1, 4)
    k = k.reshape(B, T, H, 2, Dh).transpose(0, 2, 3, 1, 4)
    v = v.reshape(B, T, H, Dv).transpose(0, 2, 1, 3)
    n_blk = -(-T // Q_BLOCK)
    t_pad = n_blk * Q_BLOCK
    qp = jnp.pad(q, ((0, 0), (0, 0), (0, 0), (0, t_pad - T), (0, 0)))
    q_blocks = qp.reshape(B, H, 2, n_blk, Q_BLOCK, Dh).transpose(3, 0, 1, 2, 4, 5)
    pos_blocks = jnp.arange(t_pad).reshape(n_blk, Q_BLOCK)
    pos_k = jnp.arange(T)
    cid_k = chunk_id(pos_k)
    slopes = alibi_slopes(H)
    scale = Dh ** -0.5

    def block(args):
        q_blk, pos_q = args
        visible = chunk_id(pos_q)[:, None] >= cid_k[None, :]
        dist = jnp.abs(pos_q[:, None] - pos_k[None, :]).astype(jnp.float32)
        bias = jnp.where(visible[None], -slopes[:, None, None] * dist[None], -jnp.inf)
        s = jnp.einsum('bhmqd,bhmkd->bhmqk', q_blk, k).astype(jnp.float32) * scale + bias[None, :, None]
        p = jax.nn.softmax(s, axis=-1)
        a = (p[:, :, 0] - lam * p[:, :, 1]).astype(v.dtype)
        return jnp.einsum('bhqk,bhkd->bhqd', a, v)

    o = lax.map(block, (q_blocks, pos_blocks))
    o = o.transpose(1, 2, 0, 3, 4).reshape(B, H, t_pad, Dv)[:, :, :T]
    o = rmsnorm(o, subln_g) * (1.0 - lam_init)
    return o.transpose(0, 2, 1, 3).reshape(B, T, H * Dv)

def hier_moe(x, rg_w, rg_b, re_w, re_b, w_gate, w_up, w_down):
    shape = x.shape
    xt = x.reshape(-1, shape[-1])
    n = xt.shape[0]
    lg_g = (xt @ rg_w + rg_b).astype(jnp.float32)
    p_g = jax.nn.softmax(lg_g, axis=-1)
    _, g_idx = lax.top_k(lg_g, 1)
    g_prob = jnp.take_along_axis(p_g, g_idx, axis=1)
    lg_e = (xt @ re_w + re_b).astype(jnp.float32).reshape(n, N_GROUPS, EXPERTS_PER_GROUP)
    lg_in = jnp.take_along_axis(lg_e, g_idx[:, :, None], axis=1)[:, 0]
    top_v, top_i = lax.top_k(lg_in, TOP_K_INNER)
    p_in = jax.nn.softmax(top_v, axis=-1)
    w_in = jnp.sum(jax.nn.one_hot(top_i, EXPERTS_PER_GROUP, dtype=jnp.float32) * p_in[..., None], axis=1)
    gate = (jax.nn.one_hot(g_idx[:, 0], N_GROUPS, dtype=jnp.float32)[:, :, None]
            * w_in[:, None, :]).reshape(n, N_EXPERTS) * g_prob
    gate = gate.astype(xt.dtype)
    y = jnp.zeros_like(xt)
    for e in range(N_EXPERTS):
        he = jax.nn.silu(xt @ w_gate[e]) * (xt @ w_up[e])
        y = y + gate[:, e:e + 1] * (he @ w_down[e])
    return y.reshape(shape)

def setup_inputs(seed: int = 0) -> dict:
    key = jax.random.key(seed)
    ks = jax.random.split(key, 28)
    f32 = jnp.float32

    def nrm(k, shape, scale):
        return jax.random.normal(k, shape, f32) * scale

    rad = jax.random.uniform(ks[10], (DEPTH, LRU_WIDTH), f32, 0.9, 0.999)
    s = rad ** (1.0 / LRU_C)
    lru_a_param = jnp.log(s) - jnp.log1p(-s)
    return {
        "x": nrm(ks[0], (BATCH, SEQ, D_MODEL), 1.0),
        "meta_tokens": nrm(ks[1], (N_META, D_MODEL), 1.0),
        "norm1_g": 1.0 + nrm(ks[2], (DEPTH, D_MODEL), 0.02),
        "w_in": nrm(ks[3], (DEPTH, D_MODEL, IN_PROJ_WIDTH), D_MODEL ** -0.5),
        "conv_w": nrm(ks[4], (DEPTH, CONV_W, LRU_WIDTH), CONV_W ** -0.5),
        "conv_b": nrm(ks[5], (DEPTH, LRU_WIDTH), 0.02),
        "gate_a_w": nrm(ks[6], (DEPTH, LRU_BLOCKS, LRU_BLOCK_W, LRU_BLOCK_W), LRU_BLOCK_W ** -0.5),
        "gate_a_b": nrm(ks[7], (DEPTH, LRU_WIDTH), 0.02),
        "gate_x_w": nrm(ks[8], (DEPTH, LRU_BLOCKS, LRU_BLOCK_W, LRU_BLOCK_W), LRU_BLOCK_W ** -0.5),
        "gate_x_b": nrm(ks[9], (DEPTH, LRU_WIDTH), 0.02),
        "lru_a_param": lru_a_param,
        "lambda_q1": nrm(ks[11], (DEPTH, ATT_QK_DIM), 0.1),
        "lambda_k1": nrm(ks[12], (DEPTH, ATT_QK_DIM), 0.1),
        "lambda_q2": nrm(ks[13], (DEPTH, ATT_QK_DIM), 0.1),
        "lambda_k2": nrm(ks[14], (DEPTH, ATT_QK_DIM), 0.1),
        "subln_g": 1.0 + nrm(ks[15], (DEPTH, ATT_V_DIM), 0.02),
        "w_out": nrm(ks[16], (DEPTH, MIX_WIDTH, D_MODEL), MIX_WIDTH ** -0.5),
        "norm2_g": 1.0 + nrm(ks[17], (DEPTH, D_MODEL), 0.02),
        "router_g_w": nrm(ks[18], (DEPTH, D_MODEL, N_GROUPS), D_MODEL ** -0.5),
        "router_g_b": nrm(ks[19], (DEPTH, N_GROUPS), 0.01),
        "router_e_w": nrm(ks[20], (DEPTH, D_MODEL, N_EXPERTS), D_MODEL ** -0.5),
        "router_e_b": nrm(ks[21], (DEPTH, N_EXPERTS), 0.01),
        "exp_w_gate": nrm(ks[22], (DEPTH, N_EXPERTS, D_MODEL, D_EXPERT), D_MODEL ** -0.5),
        "exp_w_up": nrm(ks[23], (DEPTH, N_EXPERTS, D_MODEL, D_EXPERT), D_MODEL ** -0.5),
        "exp_w_down": nrm(ks[24], (DEPTH, N_EXPERTS, D_EXPERT, D_MODEL), D_EXPERT ** -0.5),
        "final_norm_g": 1.0 + nrm(ks[25], (D_MODEL,), 0.02),
    }

def reference(x, meta_tokens, norm1_g, w_in, conv_w, conv_b, gate_a_w, gate_a_b, gate_x_w, gate_x_b,
              lru_a_param, lambda_q1, lambda_k1, lambda_q2, lambda_k2, subln_g, w_out, norm2_g,
              router_g_w, router_g_b, router_e_w, router_e_b, exp_w_gate, exp_w_up, exp_w_down,
              final_norm_g):
    B = x.shape[0]
    meta = jnp.broadcast_to(meta_tokens[None].astype(x.dtype), (B, N_META, D_MODEL))
    h = jnp.concatenate([meta, x], axis=1)
    splits = [LRU_WIDTH, 2 * LRU_WIDTH, 2 * LRU_WIDTH + QK_WIDTH, 2 * LRU_WIDTH + 2 * QK_WIDTH]
    for l in range(DEPTH):
        lam_init = 0.8 - 0.6 * math.exp(-0.3 * l)
        hn = rmsnorm(h, norm1_g[l])
        proj = hn @ w_in[l]
        u, yg, q, k, v = jnp.split(proj, splits, axis=-1)
        lru_out = rg_lru_mixer(u, yg, conv_w[l], conv_b[l], gate_a_w[l], gate_a_b[l],
                               gate_x_w[l], gate_x_b[l], lru_a_param[l])
        lam = (jnp.exp(jnp.sum(lambda_q1[l].astype(jnp.float32) * lambda_k1[l].astype(jnp.float32)))
               - jnp.exp(jnp.sum(lambda_q2[l].astype(jnp.float32) * lambda_k2[l].astype(jnp.float32)))
               + lam_init)
        att_out = diff_attention(q, k, v, lam, lam_init, subln_g[l])
        h = h + jnp.concatenate([lru_out, att_out], axis=-1) @ w_out[l]
        h = h + hier_moe(rmsnorm(h, norm2_g[l]), router_g_w[l], router_g_b[l], router_e_w[l],
                         router_e_b[l], exp_w_gate[l], exp_w_up[l], exp_w_down[l])
    out = rmsnorm(h, final_norm_g)
    return out[:, N_META:]


_drawn_inputs = setup_inputs


def setup_inputs(seed=0):
    import zlib

    import numpy as np

    out = dict(_drawn_inputs(seed))
    spreads = {}
    factors = {'gate_a_b': 8.0,
     'gate_x_b': 8.0,
     'subln_g': 3.583,
     'norm2_g': 3.93,
     'router_g_b': 8.0,
     'router_e_b': 8.0,
     'final_norm_g': 2.721}
    for name, (base, spread) in spreads.items():
        noise = np.random.default_rng([zlib.crc32(name.encode()), seed]).standard_normal(out[name].shape)
        drawn = base * np.exp(spread * noise) if base else spread * noise
        out[name] = __import__('jax').numpy.asarray(drawn.astype(out[name].dtype))
    for name, factor in factors.items():
        out[name] = (out[name] * factor).astype(out[name].dtype)
    return out
```

```python
from contextlib import ExitStack

import concourse.bass as bass
from concourse import mybir

P = 128
D = 2048
KC = D // P
TX = 256
NM = 16
T = NM + TX
NT = TX // P
HEADS = 8
DH = 64
CHUNK = 64
LW = 1024
LB = LW // P
CONVW = 4
NG, EPG = 4, 4
NE = NG * EPG
F = 512
FC = F // P
C = 80
ROUNDS = -(-TX // C)
EPS = 1e-6
LAM_INIT = 0.8 - 0.6
BIG = 4096.0
K0, K1 = NM + P, T
S0, S1 = 0, K0
SW = K0 + K1

N_QKV = 3 * HEADS
N_LRU = 2 * LB
N_OUT = D // P
LRU0 = N_QKV
OUT0 = N_QKV + N_LRU
N_CHUNKS = OUT0 + N_OUT
QKV_RING = 3
RING = 4

F32 = mybir.dt.float32
F32R = mybir.dt.float32r
I32 = mybir.dt.int32
U32 = mybir.dt.uint32
ALU = mybir.AluOpType
ACT = mybir.ActivationFunctionType
AX = mybir.AxisListType

ROW_G1, ROW_G2, ROW_CB, ROW_CW, ROW_BA, ROW_BX, ROW_LA, ROW_SG = 0, 16, 32, 40, 72, 80, 88, 96
N_ROWS = 97


def ds(start, size):
    return bass.ds(start, size)


class Steps:

    def __init__(self, eng, sem):
        self.eng, self.sem, self.base, self.k = eng, sem, 0, 0

    def mark(self, ins):
        self.k += 1
        ins.then_inc(self.sem, 1)

    def wait(self):
        self.eng.wait_ge(self.sem, self.base + self.k)

    def done(self, ins):
        self.mark(ins)
        self.wait()

    def begin(self, base):
        self.base, self.k = base, 0


def looped(eng, steps, first, count, body, per_body, ticks=None):
    start = steps.base + steps.k
    with eng.Fori(first, first + count) as i:
        steps.begin((i - first) * per_body + start)
        body(i)
        assert steps.k == per_body, (steps.k, per_body)
    steps.begin(start + count * per_body)


def at_least(eng, sem, value):
    if isinstance(value, int) and value <= 0:
        return
    eng.wait_ge(sem, value)


def build(nc, x, meta_tokens, norm1_g, w_in, conv_w, conv_b, gate_a_w, gate_a_b, gate_x_w, gate_x_b,
          lru_a_param, lambda_q1, lambda_k1, lambda_q2, lambda_k2, subln_g, w_out, norm2_g,
          router_g_w, router_g_b, router_e_w, router_e_b, exp_w_gate, exp_w_up, exp_w_down,
          final_norm_g, out):
    with ExitStack() as ctx:
        ctx.enter_context(nc.allow_non_contiguous_dma("small parameter loads"))

        def sem(name):
            return ctx.enter_context(nc.semaphore(name))

        base = [(nc.sbuf_base + 31) // 32 * 32]
        arena = nc.alloc_sbuf_tensor("arena", [P, (nc.sbuf_usable_end - base[0] - 64) // 4], F32)
        first_byte = base[0]
        limit = nc.sbuf_usable_end

        def place(name, shape, dt, offset=None):
            n = 4
            for s in shape[1:]:
                n *= s
            n = (n + 31) // 32 * 32
            if offset is None:
                offset = base[0]
                base[0] += n
                assert base[0] <= limit, (name, base[0], limit)
            return nc.alloc_sbuf_tensor_at(name, shape, dt, offset=offset), offset, offset + n

        def region(start, end, *parts):
            o = start
            got = []
            for name, shape, dt in parts:
                t, _, o = place(name, shape, dt, o)
                got.append(t)
            assert o <= end, (parts[-1][0], o, end)
            return got

        h_res, _, _ = place("h_res", [P, NT, D], F32)
        mix_hi, MIX, _ = place("mix_hi", [P, KC, TX], F32R)
        mix_lo, _, MIX_END = place("mix_lo", [P, KC, TX], F32R)
        hn_hi, hn_lo = region(MIX, MIX_END, ("hn_hi", [P, NT, KC, P], F32R), ("hn_lo", [P, NT, KC, P], F32R))
        xn, metan, junk = region(MIX, MIX_END, ("xn", [P, NT, D], F32), ("metan", [NM, D], F32), ("junk", [P, D], F32))
        STAGE = base[0]
        raw, w_lo, w_hi = [], [], []
        for s in range(RING):
            t, o, _ = place(f"raw{s}", [P, KC, P], F32)
            raw.append(t)
            w_lo.append(place(f"w_lo{s}", [P, KC, P], F32R, o)[0])
            w_hi.append(place(f"w_hi{s}", [P, KC, P], F32R)[0])
        STAGE_END = base[0]
        WREG = base[0]
        slots = []
        for s in range(10):
            slots.append(place(f"slot{s}", [P, D], F32)[0])
        WREG_END = base[0]
        (s10, s11, sel, x_e, h_e, e_neg, e_rec, y_t, y_e) = region(
            STAGE, STAGE_END, ("slot10", [P, D], F32), ("slot11", [P, D], F32),
            ("sel", [P, NT, NE, C], F32R), ("x_e", [P, KC, C], F32), ("h_e", [P, FC, C], F32),
            ("e_neg", [P, FC, C], F32), ("e_rec", [P, FC, C], F32), ("y_t", [P, KC, C], F32), ("y_e", [C, D], F32))
        (rt,) = region(STAGE_END - 20 * NT * NE * 4, STAGE_END, ("rt", [P, 20, NT, NE], F32))
        slots += [s10, s11]
        (xt_hi, xt_lo, q_t, k_t, v_t, v_tm, v_meta, s_sb, a_sb, at_x, at_m, o_sb, u_pad, yg_t, xc, e_ri, r_ri, a_t, tg,
         lr1, lr2, lr3, gl1, gl2, hs_t, g_w, lru_f, mix_f) = region(
            WREG, WREG_END, ("xt_hi", [P, KC, T], F32R), ("xt_lo", [P, KC, T], F32R),
            ("q_t", [P, TX], F32), ("k_t", [P, T], F32), ("v_t", [P, T], F32), ("v_tm", [P, NT, P], F32),
            ("v_meta", [NM, P], F32), ("s_sb", [P, 2, SW], F32), ("a_sb", [P, SW], F32),
            ("at_x", [P, NT, TX], F32), ("at_m", [NM, TX], F32), ("o_sb", [P, NT, P], F32),
            ("u_pad", [P, CONVW - 1 + T], F32), ("yg_t", [P, TX], F32), ("xc", [P, T], F32),
            ("e_ri", [P, 2, T], F32), ("r_ri", [P, 2, T], F32), ("a_t", [P, T], F32), ("tg", [P, T], F32),
            ("lr1", [P, T], F32), ("lr2", [P, T], F32), ("lr3", [P, T], F32), ("gl1", [P, TX], F32),
            ("gl2", [P, TX], F32), ("hs_t", [P, T], F32), ("g_w", [P, 2, 2, P], F32), ("lru_f", [P, TX], F32),
            ("mix_f", [P, TX], F32))
        y_rows, ysum, yout, fgain = region(WREG, WREG_END, ("y_rows", [P, 2, NT, D], F32), ("ysum", [P, NT, D], F32),
                                           ("yout", [P, NT, D], F32), ("fgain", [P, D], F32))
        def small(name, shape, dt=F32):
            return place(name, shape, dt)[0]

        ident = small("ident", [P, P])
        ltri = small("ltri", [P, P])
        ones = small("ones", [P, P])
        params = small("params", [P, P])
        col = small("col", [P, N_ROWS])
        g2e = small("g2e", [P, KC])
        lam_in = small("lam_in", [P, 4, DH])
        bias = small("bias", [P, SW])
        rw = small("rw", [P, KC, NG + NE])
        rb = small("rb", [P, NG + NE])
        slot_no = small("slot_no", [P, C])
        stat = small("stat", [P, 96])
        negb = small("negb", [P, 3 * LB])
        sp = small("sp", [P, 8, LB])
        half = small("half", [P, T])
        o_t = [small(f"o_t{i}", [P, TX]) for i in range(2)]
        idx_f = small("idx_f", [C, NE])
        idx_i = small("idx_i", [C, NE], I32)
        idx_1 = small("idx_1", [C, 1], I32)
        cnt = small("cnt", [P, 2], I32)
        h_s = [small(f"h_s{i}", [P, NT, P]) for i in range(2)]
        h_tt = [small(f"h_t{i}", [P, TX]) for i in range(2)]
        sg = small("sg", [P, 1])
        junk_a = small("junk_a", [P, NT, P])

        ps = ctx.enter_context(nc.psum_tensor("ps", [P, 8, 512], F32))

        y_dram = nc.dram_tensor("expert_rows", [2 * TX, D], F32, kind="Internal").ap()
        x_rows = x.rearrange("b (t p) d -> p (b t) d", p=P)
        out_rows = out.rearrange("b (t p) d -> p (b t) d", p=P)
        w_in_rows = w_in[0].rearrange("(c p) n -> p c n", p=P)
        w_out_rows = w_out[0].rearrange("(c p) n -> p c n", p=P)
        wg_rows = exp_w_gate[0].rearrange("e (p c) f -> e p (c f)", c=KC)
        wu_rows = exp_w_up[0].rearrange("e (p c) f -> e p (c f)", c=KC)
        wd_rows = exp_w_down[0].rearrange("e (c p) d -> e c p d", p=P)

        x_in = [sem(f"x_in{i}") for i in range(3)]
        params_in = sem("params_in")
        misc_in = sem("misc_in")
        gates_in = [sem(f"gates_in{i}") for i in range(2)]
        raw_in = [sem(f"raw_in{i}") for i in range(RING)]
        slot_in = [sem(f"slot_in{i}") for i in range(12)]
        fgain_in, y_in, out_done = sem("fgain_in"), sem("y_in"), sem("out_done")
        carried = sem("carried")
        consts_ready, act_step, dve_step, pool_step = sem("consts_ready"), sem("act_step"), sem("dve_step"), sem("pool_step")
        sq_ready, xn_ready = sem("sq_ready"), sem("xn_ready")
        params_turned, cols_ready = sem("params_turned"), sem("cols_ready")
        xt_turned, xt_hi_ready, xt_lo_ready = sem("xt_turned"), sem("xt_hi_ready"), sem("xt_lo_ready")
        ms_ready, rstd_ready = sem("ms_ready"), sem("rstd_ready")
        sp_e_in, sp_e_out = sem("sp_e_in"), sem("sp_e_out")
        hi_ready, lo_ready, chunk_done, acc_out = sem("hi_ready"), sem("lo_ready"), sem("chunk_done"), sem("acc_out")
        v_turned, v_out = sem("v_turned"), sem("v_out")
        scores_done, biased = sem("scores_done"), sem("biased")
        max_ready, probs_ready, a_ready = sem("max_ready"), sem("probs_ready"), sem("a_ready")
        a_turned, a_out = sem("a_turned"), sem("a_out")
        o_done, o_sq, o_ms, o_rstd, o_out, o_turned = (sem("o_done"), sem("o_sq"), sem("o_ms"), sem("o_rstd"),
                                                       sem("o_out"), sem("o_turned"))
        mix_hi_ready, mix_lo_ready = sem("mix_hi_ready"), sem("mix_lo_ready")
        xc_ready, gates_done, e_ready, r_ready, at_ready = (sem("xc_ready"), sem("gates_done"), sem("e_ready"),
                                                            sem("r_ready"), sem("at_ready"))
        q_ready, sqrt_ready, lru_ready = sem("q_ready"), sem("sqrt_ready"), sem("lru_ready")
        gelu_in, gelu_th, gelu_ready = sem("gelu_in"), sem("gelu_th"), sem("gelu_ready")
        o_back, h_ready, h_kept, h_turned, h_t_ready, logits_done = (
            sem("o_back"), sem("h_ready"), sem("h_kept"), sem("h_turned"), sem("h_t_ready"), sem("logits_done"))
        h_sq = sem("h_sq")
        h_ms, h_rstd, hn_hi_ready, hn_lo_ready = sem("h_ms"), sem("h_rstd"), sem("hn_hi_ready"), sem("hn_lo_ready")
        rt_max, rt_exp = sem("rt_max"), sem("rt_exp")
        members, ranks_done, sel_ready, lists_done, lists_ready, cnt_ready = (
            sem("members"), sem("ranks_done"), sem("sel_ready"), sem("lists_done"), sem("lists_ready"),
            sem("cnt_ready"))
        slot_used, gathered, x_e_ready = sem("slot_used"), sem("gathered"), sem("x_e_ready")
        e_neg_ready, h_e_ready, y_t_act, y_t_dve = (
            sem("e_neg_ready"), sem("h_e_ready"), sem("y_t_act"), sem("y_t_dve"))
        y_back, y_out, scattered = sem("y_back"), sem("y_out"), sem("scattered")
        y_half = sem("y_half")
        ysum_ready, y_sq, y_ms, y_rstd, yout_ready = (sem("ysum_ready"), sem("y_sq"), sem("y_ms"), sem("y_rstd"),
                                                      sem("yout_ready"))

        def chunk_use(n_slot, phase, i):
            before = {"qkv": 0, "lru": HEADS, "out": HEADS + N_LRU // RING}[phase]
            if n_slot == RING - 1 and phase != "qkv":
                before -= HEADS
            return before + i + 1

        def is0(i):
            return isinstance(i, int) and i == 0

        def apart(eng):
            eng.sem_inc(carried, 1)

        SQ, RSTD = 0, 4
        LAM, NLAM = 8, 9
        NMAX, L, RL, CM = 12, 16, 20, 24
        OSQ, ORS = 28, 30
        W12 = 32
        HRS, YSQ, YRS = 36, 38, 40
        HSQ = 48
        NH = 80
        LP = 84

        def qkv_src(h, j):
            return w_in_rows[:, :, ds(2 * LW + j * 1024 + h * P, P)]

        def lru_src(g, j):
            return w_in_rows[:, :, ds(j * LW + g * P, P)]

        block = ctx.enter_context(nc.Block())

        @block.sync
        def _(sp_e):
            eng = sp_e
            eng.dma_start(h_res[:, 0, :], x_rows[:, 0, :]).then_inc(x_in[0], 16)
            eng.dma_start(h_res[:, 1, :], x_rows[:, 1, :]).then_inc(x_in[1], 16)
            eng.dma_start(metan[:, :], meta_tokens).then_inc(x_in[2], 16)

            def load_qkv(h, j, first=False):
                n = 3 * h + j
                if not is0(h):
                    eng.wait_ge(chunk_done, n - QKV_RING + 1)
                eng.dma_start(raw[j][:, :, :], qkv_src(h, j)).then_inc(raw_in[j], 16)

            for j in range(3):
                load_qkv(0, j)
                if j == 0:
                    for r, src in ((ROW_G1, norm1_g[0].rearrange("(c p) -> c p", p=P)),
                                   (ROW_G2, norm2_g[0].rearrange("(c p) -> c p", p=P)),
                                   (ROW_CB, conv_b[0].rearrange("(c p) -> c p", p=P)),
                                   (ROW_CW, conv_w[0].rearrange("k (c p) -> (k c) p", p=P)),
                                   (ROW_BA, gate_a_b[0].rearrange("(c p) -> c p", p=P)),
                                   (ROW_BX, gate_x_b[0].rearrange("(c p) -> c p", p=P)),
                                   (ROW_LA, lru_a_param[0].rearrange("(c p) -> c p", p=P)),
                                   (ROW_SG, subln_g)):
                        eng.dma_start(params[r:r + src.shape[0], :], src).then_inc(params_in, 16)
            for k, lam in enumerate((lambda_q1, lambda_q2, lambda_k1, lambda_k2)):
                eng.dma_start(lam_in[:, k, :], lam.partition_broadcast(P)).then_inc(misc_in, 16)
            eng.dma_start(g2e[:, :], norm2_g[0].rearrange("(p c) -> p c", c=KC)).then_inc(misc_in, 16)
            eng.dma_start(rw[:, :, 0:NG], router_g_w[0].rearrange("(c p) g -> p c g", p=P)).then_inc(misc_in, 16)
            eng.dma_start(rw[:, :, NG:], router_e_w[0].rearrange("(c p) g -> p c g", p=P)).then_inc(misc_in, 16)
            eng.dma_start(rb[:, 0:NG], router_g_b.partition_broadcast(P)).then_inc(misc_in, 16)
            eng.dma_start(rb[:, NG:], router_e_b.partition_broadcast(P)).then_inc(misc_in, 16)
            with eng.Fori(1, HEADS) as h:
                for j in range(3):
                    load_qkv(h, j)

            def load_lru(i):
                for s in range(RING):
                    if is0(i):
                        if s < QKV_RING:
                            eng.wait_ge(chunk_done, LRU0 - QKV_RING + s + 1)
                    else:
                        eng.wait_ge(chunk_done, LRU0 + RING * i + s - RING + 1)
                    eng.dma_start(raw[s][:, :, :], lru_src(2 * i + s // 2, s % 2)).then_inc(raw_in[s], 16)
                    if s % 2 == 0:
                        g = 2 * i + s // 2
                        if not is0(i):
                            eng.wait_ge(gates_done, g - 1)
                        eng.dma_start(g_w[:, s // 2, 0, :], gate_a_w[0, ds(g, 1)].rearrange("g i j -> i (g j)"))\
                           .then_inc(gates_in[s // 2], 16)
                        eng.dma_start(g_w[:, s // 2, 1, :], gate_x_w[0, ds(g, 1)].rearrange("g i j -> i (g j)"))\
                           .then_inc(gates_in[s // 2], 16)

            load_lru(0)
            with eng.Fori(1, LB // 2) as i:
                load_lru(i)

            def load_out(m, s):
                eng.wait_ge(chunk_done, OUT0 + m - RING + 1)
                eng.dma_start(raw[s][:, :, :], w_out_rows[:, :, ds(m * P, P)]).then_inc(raw_in[s], 16)

            def load_slot(e, s):
                if s < 8:
                    rows = (wg_rows if s < 4 else wu_rows)[ds(e, 1), :, (s % 4) * D:(s % 4 + 1) * D]
                    rows = rows.rearrange("e p n -> (e p) n")
                else:
                    rows = wd_rows[ds(e, 1), s - 8].rearrange("e p n -> (e p) n")
                eng.dma_start(slots[s][:, :], rows).then_inc(slot_in[s], 16)

            for s in range(RING):
                load_out(s, s)
            eng.wait_ge(mix_hi_ready, KC)
            eng.wait_ge(mix_lo_ready, KC)
            for s in range(RING):
                load_out(RING + s, s)
                load_slot(0, 2 * s)
                load_slot(0, 2 * s + 1)
            for s in range(RING):
                load_out(2 * RING + s, s)
            load_slot(0, 8)
            load_slot(0, 9)
            for s in range(RING):
                load_out(3 * RING + s, s)
            eng.wait_ge(chunk_done, OUT0 + 3 * RING + 1)
            load_slot(0, 10)
            load_slot(0, 11)

            def load_expert(i, e):
                for s in range(12):
                    eng.wait_ge(slot_used, 12 * (i - 1) + s + 1)
                    load_slot(e, s)

            with eng.Fori(1, NE) as e:
                load_expert(e, e)
            eng.wait_ge(cnt_ready, 1)
            most = eng.value_load(cnt[0:1, 0:1], min_val=0, max_val=TX)
            with eng.Fori(1, ROUNDS) as r:
                with eng.If(most > r * C):
                    with eng.Fori(0, NE) as e:
                        load_expert(r * NE + e, e)
                    eng.wait_ge(scattered, 16 * NE * (r + 1))
                    apart(eng)
            eng.wait_ge(scattered, 16 * NE)
            eng.dma_start(fgain[:, :], final_norm_g.rearrange("(a d) -> a d", a=1).partition_broadcast(P)
                          if False else final_norm_g.partition_broadcast(P)).then_inc(fgain_in, 16)
            yr = y_dram.rearrange("(k t p) d -> p k t d", p=P, t=NT)
            for t in range(NT):
                eng.dma_start(y_rows[:, :, t, :], yr[:, :, t, :]).then_inc(y_in, 16)
            for t in range(NT):
                eng.wait_ge(yout_ready, t + 1)
                eng.dma_start(out_rows[:, t, :], yout[:, t, :]).then_inc(out_done, 16)
            eng.wait_ge(out_done, 16 * NT)

        @block.gpsimd
        def _(eng):
            step = Steps(eng, pool_step)
            step.done(eng.memset(ident[:, :], 0.0))
            eng.affine_select(out=ident[:, :], in_=ident[:, :], compare_op=ALU.not_equal, fill=1.0, base=0,
                              pattern=[[-1, P]], channel_multiplier=1).then_inc(consts_ready, 1)
            step.done(eng.memset(ones[:, :], 1.0))
            step.mark(eng.affine_select(out=ltri[:, :], in_=ones[:, :], compare_op=ALU.is_gt, fill=0.0, base=0,
                                        pattern=[[1, P]], channel_multiplier=-1))
            step.mark(eng.iota(slot_no[:, :], [[1, C]], base=0, channel_multiplier=0,
                               allow_small_or_imprecise_dtypes=True))
            step.mark(eng.memset(half[:, :], 0.5))
            step.mark(eng.memset(stat[:, NH:NH + 4], -0.5))
            for t, c0, w in ((0, S0, K0), (1, S1, K1)):
                b = bias[:, c0:c0 + w]
                step.done(eng.iota(b, [[1, w]], base=-(NM + P * t), channel_multiplier=-1,
                                   allow_small_or_imprecise_dtypes=True))
            step.done(eng.tensor_scalar(s_sb[:, 0, :], bias[:, :], 0.0, -2.0, ALU.max, ALU.mult))
            step.done(eng.tensor_tensor(bias[:, :], bias[:, :], s_sb[:, 0, :], ALU.add))
            for t, c0 in ((0, S0), (1, S1)):
                late = c0 + NM + P * t + CHUNK
                step.done(eng.memset(bias[0:CHUNK, late:late + CHUNK], -1e30))
            step.mark(eng.memset(u_pad[:, 0:CONVW - 1], 0.0))
            step.mark(eng.iota(stat[:, 86:88], [[P, NT]], base=0, channel_multiplier=1,
                               allow_small_or_imprecise_dtypes=True))
            step.mark(eng.iota(stat[:, 88:92], [[-1, 4]], base=4, channel_multiplier=0,
                               allow_small_or_imprecise_dtypes=True))
            step.wait()
            eng.memset(stat[:, 92:93], 0.0).then_inc(consts_ready, 1)
            eng.wait_ge(ms_ready, 1)
            eng.tensor_tensor(stat[:, RSTD:RSTD + 2], stat[:, RSTD:RSTD + 2], stat[:, NH:NH + 2], ALU.pow)\
               .then_inc(rstd_ready, 1)
            eng.tensor_tensor(stat[0:NM, RSTD + 2:RSTD + 3], stat[0:NM, RSTD + 2:RSTD + 3], stat[0:NM, NH:NH + 1],
                              ALU.pow).then_inc(rstd_ready, 1)

            def o_power(h):
                eng.wait_ge(o_ms, h + 1)
                eng.tensor_tensor(stat[:, ORS:ORS + NT], stat[:, ORS:ORS + NT], stat[:, NH:NH + NT], ALU.pow)\
                   .then_inc(o_rstd, 1)

            with eng.Fori(0, HEADS) as h:
                o_power(h)

            def lru(g):
                yg = yg_t[:, :]
                eng.wait_ge(acc_out, LRU0 + 2 * g + 2)
                at_least(eng, lru_ready, g)
                step.done(eng.tensor_tensor(gl1[:, :], yg, yg, ALU.mult))
                apart(eng)
                step.done(eng.tensor_scalar(gl1[:, :], gl1[:, :], 0.044715, 1.0, ALU.mult, ALU.add))
                eng.tensor_tensor(gl1[:, :], gl1[:, :], yg, ALU.mult).then_inc(gelu_in, 1)
                eng.wait_ge(q_ready, g + 1)
                eng.tensor_tensor(lr3[:, :], lr2[:, :], half[:, :], ALU.pow).then_inc(sqrt_ready, 1)
                eng.wait_ge(gelu_th, g + 1)
                apart(eng)
                step.done(eng.tensor_scalar(gl2[:, :], gl2[:, :], 1.0, 0.5, ALU.add, ALU.mult))
                eng.tensor_tensor(gl1[:, :], gl2[:, :], yg, ALU.mult).then_inc(gelu_ready, 1)

            lru(0)
            looped(eng, step, 1, LB - 1, lru, 3)

            def keep(m, b):
                eng.wait_ge(h_ready, m + 1)
                eng.tensor_copy(h_res[:, :, ds(m * P, P)], h_s[b][:, :, :]).then_inc(h_kept, 1)

            with eng.Fori(0, N_OUT // 2) as i:
                for b in range(2):
                    keep(2 * i + b, b)
            eng.wait_ge(h_ms, 1)
            eng.tensor_tensor(stat[:, HRS:HRS + NT], stat[:, HRS:HRS + NT], stat[:, NH:NH + NT], ALU.pow)\
               .then_inc(h_rstd, 1)

            def scatter(i, e):
                at_least(eng, scattered, 16 * i)
                step.done(eng.tensor_copy(idx_1[:, 0:1], idx_i[:, ds(e, 1)]))
                eng.wait_ge(y_out, 4 * (i + 1))
                apart(eng)
                eng.indirect_dma_start(out=y_dram[:, :], out_offset=bass.IndirectOffsetOnAxis(ap=idx_1[:, 0:1], axis=0),
                                       in_=y_e[:, :], in_offset=None, bounds_check=2 * TX - 1, oob_is_err=False)\
                   .then_inc(scattered, 16)

            def scatter_round(r):
                eng.wait_ge(lists_ready, r + 1)
                apart(eng)
                looped(eng, step, 0, NE, lambda e: scatter(r * NE + e, e), 1)

            eng.wait_ge(lists_ready, 1)
            scatter(0, 0)
            looped(eng, step, 1, NE - 1, lambda e: scatter(e, e), 1)
            k0 = step.k + step.base
            eng.wait_ge(cnt_ready, 1)
            most = eng.value_load(cnt[0:1, 0:1], min_val=0, max_val=TX)
            with eng.Fori(1, ROUNDS) as r:
                with eng.If(most > r * C):
                    step.begin(k0 + (r - 1) * NE)
                    scatter_round(r)
            eng.wait_ge(y_ms, 1)
            eng.tensor_tensor(stat[:, YRS:YRS + NT], stat[:, YRS:YRS + NT], stat[:, NH:NH + NT], ALU.pow)\
               .then_inc(y_rstd, 1)

        @block.scalar
        def _(eng):
            step = Steps(eng, act_step)
            for t in range(NT):
                eng.wait_ge(x_in[t], 16)
                step.mark(eng.activation(junk[:, :], h_res[:, t, :], ACT.Square, accum_out=stat[:, SQ + t:SQ + t + 1]))
                step.wait()
            eng.wait_ge(x_in[2], 16)
            eng.activation(junk[0:NM, :], metan[:, :], ACT.Square, accum_out=stat[0:NM, SQ + 2:SQ + 3])\
               .then_inc(sq_ready, 1)

            def hi(n, s, use):
                eng.wait_ge(raw_in[s], 16 * use)
                eng.activation(w_hi[s][:, :, :], raw[s][:, :, :], ACT.Copy).then_inc(hi_ready, 1)

            hi(0, 0, 1)
            hi(1, 1, 1)
            eng.wait_ge(cols_ready, 1)
            for c in range(KC):
                eng.wait_ge(xt_turned, c + 1)
                eng.activation(xt_hi[:, c, :], ps[:, 3 + c % 4, 0:T], ACT.Copy,
                               scale=col[:, ROW_G1 + c:ROW_G1 + c + 1]).then_inc(xt_hi_ready, 1)
            eng.wait_ge(sp_e_in, 1)
            eng.activation(sp[:, 1, :], sp[:, 0, :], ACT.Exp).then_inc(sp_e_out, 1)
            eng.activation(stat[:, LP:LP + 2], stat[:, LP:LP + 2], ACT.Exp).then_inc(sp_e_out, 1)

            def o_squares(h):
                eng.wait_ge(o_done, h + 1)
                for t in range(NT):
                    ins = eng.activation(junk_a[:, t, :], ps[:, 7, TX + t * P:TX + (t + 1) * P], ACT.Square,
                                         accum_out=stat[:, OSQ + t:OSQ + t + 1])
                    ins.then_inc(o_sq, 1)

            def mix_high(h):
                eng.wait_ge(o_turned, h + 1)
                eng.activation(mix_hi[:, ds(LB + h, 1), :].rearrange("p a t -> p (a t)"), ps[:, 6, 0:TX], ACT.Copy,
                               scale=sg[:, 0:1]).then_inc(mix_hi_ready, 1)

            def probs(h):
                for m in range(2):
                    for t, c0, w in ((0, S0, K0), (1, S1, K1)):
                        eng.wait_ge(max_ready, 2 * h + t + 1)
                        k = 2 * m + t
                        eng.activation(s_sb[:, m, c0:c0 + w], s_sb[:, m, c0:c0 + w], ACT.Exp,
                                       bias=stat[:, NMAX + k:NMAX + k + 1],
                                       accum_out=stat[:, L + k:L + k + 1]).then_inc(probs_ready, 1)

            def qkv(h):
                n = 3 * h
                hi(n + 2, 2, h + 1)
                eng.wait_ge(chunk_done, n + 1)
                eng.activation(q_t[:, :], ps[:, 0, 0:TX], ACT.Copy).then_inc(acc_out, 1)
                if not is0(h):
                    o_squares(h - 1)
                eng.wait_ge(chunk_done, n + 2)
                eng.activation(k_t[:, :], ps[:, 1, 0:T], ACT.Copy).then_inc(acc_out, 1)
                hi(n + 3, 0, h + 2)
                probs(h)
                if not is0(h):
                    mix_high(h - 1)
                hi(n + 4, 1, h + 2)
                eng.wait_ge(chunk_done, n + 3)
                eng.activation(v_t[:, :], ps[:, 2, 0:T], ACT.Copy).then_inc(acc_out, 1)

            qkv(0)
            with eng.Fori(1, HEADS) as h:
                qkv(h)

            def lru(i, b):
                g = 2 * i + b
                n = LRU0 + 2 * g
                s = 2 * b
                eng.wait_ge(chunk_done, n + 1)
                at_least(eng, xc_ready, g)
                eng.activation(u_pad[:, CONVW - 1:], ps[:, 0, 0:T], ACT.Copy).then_inc(acc_out, 1)
                if is0(i) and b == 0:
                    o_squares(HEADS - 1)
                for j in (2, 3):
                    if b == 0:
                        hi(n + j, s + j, chunk_use(s + j, "lru", i))
                    elif isinstance(i, int) and i == LB // 2 - 1:
                        hi(n + j, j - 2, chunk_use(j - 2, "out", 0))
                    else:
                        hi(n + j, j - 2, chunk_use(j - 2, "lru", i + 1))
                    if is0(i) and b == 0 and j == 2:
                        mix_high(HEADS - 1)
                eng.wait_ge(gates_done, g + 1)
                at_least(eng, r_ready, g)
                eng.activation(e_ri[:, 0, :], ps[:, 3, 0:T], ACT.Exp, bias=negb[:, ds(g, 1)], scale=-1.0)\
                   .then_inc(e_ready, 1)
                eng.activation(e_ri[:, 1, :], ps[:, 4, 0:T], ACT.Exp, bias=negb[:, ds(LB + g, 1)], scale=-1.0)\
                   .then_inc(e_ready, 1)
                eng.wait_ge(chunk_done, n + 2)
                at_least(eng, gelu_ready, g)
                eng.activation(yg_t[:, :], ps[:, 1, 0:TX], ACT.Copy).then_inc(acc_out, 1)
                eng.wait_ge(r_ready, g + 1)
                at_least(eng, lru_ready, g)
                eng.activation(a_t[:, :], r_ri[:, 0, :], ACT.Exp, scale=sp[:, 6, ds(g, 1)]).then_inc(at_ready, 1)
                eng.activation(tg[:, :], r_ri[:, 0, :], ACT.Tanh, scale=sp[:, 7, ds(g, 1)]).then_inc(at_ready, 1)
                eng.wait_ge(gelu_in, g + 1)
                eng.activation(gl2[:, :], gl1[:, :], ACT.Tanh, scale=0.7978845608028654).then_inc(gelu_th, 1)
                eng.wait_ge(lru_ready, g + 1)
                eng.activation(mix_hi[:, ds(g, 1), :].rearrange("p a t -> p (a t)"), lru_f[:, :], ACT.Copy)\
                   .then_inc(mix_hi_ready, 1)

            lru(0, 0)
            lru(0, 1)
            with eng.Fori(1, LB // 2 - 1) as i:
                lru(i, 0)
                lru(i, 1)
            lru(LB // 2 - 1, 0)
            lru(LB // 2 - 1, 1)

            def h_squares(m, b):
                eng.wait_ge(h_ready, m + 1)
                for t in range(NT):
                    eng.activation(ps[:, 7, (NT * b + t) * P:(NT * b + t + 1) * P], h_s[b][:, t, :], ACT.Square,
                                   accum_out=stat[:, ds(HSQ + t * N_OUT + m, 1)]).then_inc(h_sq, 1)

            def project(i, s, last=False):
                m = RING * i + s
                n = OUT0 + m
                eng.wait_ge(chunk_done, n + 1)
                at_least(eng, o_back, m - 1)
                eng.activation(o_t[s % 2][:, :], ps[:, s % 2, 0:TX], ACT.Copy).then_inc(acc_out, 1)
                if s < 2:
                    hi(n + 2, s + 2, chunk_use(s + 2, "out", i))
                elif not last:
                    hi(n + 2, s - 2, chunk_use(s - 2, "out", i + 1))
                if not (is0(i) and s == 0):
                    h_squares(m - 1, (s - 1) % 2)

            for s in range(RING):
                project(0, s)
            with eng.Fori(1, N_OUT // RING - 1) as i:
                for s in range(RING):
                    project(i, s)
            for s in range(RING):
                project(N_OUT // RING - 1, s, last=True)
            h_squares(N_OUT - 1, 1)
            eng.wait_ge(h_rstd, 1)
            eng.wait_ge(h_kept, N_OUT)
            for t in range(NT):
                eng.activation(hn_hi[:, t, :, :], h_res[:, t, :].rearrange("p (q c) -> p c q", c=KC), ACT.Copy,
                               scale=stat[:, HRS + t:HRS + t + 1]).then_inc(hn_hi_ready, 1)
            eng.wait_ge(rt_max, 1)
            eng.activation(rt[:, 2, :, 0:NG], rt[:, 1, :, 0:NG], ACT.Exp).then_inc(rt_exp, 1)
            eng.wait_ge(rt_max, 2)
            eng.activation(rt[:, 10, :, 1:2], rt[:, 10, :, 0:1], ACT.Exp).then_inc(rt_exp, 1)

            def expert(i):
                eng.wait_ge(slot_used, 12 * i + 4)
                at_least(eng, h_e_ready, i)
                eng.activation(e_neg[:, :, :].rearrange("p f c -> p (f c)"), ps[:, 0, 0:FC * C], ACT.Exp, scale=-1.0)\
                   .then_inc(e_neg_ready, 1)
                eng.wait_ge(slot_used, 12 * i + 12)
                for j in range(2):
                    eng.activation(y_t[:, 6 * j:6 * j + 6, :].rearrange("p f c -> p (f c)"), ps[:, 2 + j, 0:6 * C],
                                   ACT.Copy).then_inc(y_t_act, 1)
                for j in range(4):
                    eng.wait_ge(y_back, 4 * i + j + 1)
                    if j == 0:
                        at_least(eng, scattered, 16 * i)
                    eng.activation(y_e[:, 512 * j:512 * (j + 1)], ps[0:C, 5 + j % 3, :], ACT.Copy).then_inc(y_out, 1)

            expert(0)
            with eng.Fori(1, NE) as e:
                expert(e)
            eng.wait_ge(cnt_ready, 1)
            most = eng.value_load(cnt[0:1, 0:1], min_val=0, max_val=TX)
            with eng.Fori(1, ROUNDS) as r:
                with eng.If(most > r * C):
                    with eng.Fori(0, NE) as e:
                        expert(r * NE + e)
            for t in range(NT):
                eng.wait_ge(ysum_ready, t + 1)
                eng.activation(yout[:, t, :], ysum[:, t, :], ACT.Square,
                               accum_out=stat[:, YSQ + t:YSQ + t + 1]).then_inc(y_sq, 1)

        @block.vector
        def _(eng):
            step = Steps(eng, dve_step)
            eng.wait_ge(sq_ready, 1)
            eng.wait_ge(act_step, 2)
            step.mark(eng.tensor_scalar(stat[:, RSTD:RSTD + 2], stat[:, SQ:SQ + 2], 1.0 / D, EPS, ALU.mult, ALU.add))
            step.mark(eng.tensor_scalar(stat[0:NM, RSTD + 2:RSTD + 3], stat[0:NM, SQ + 2:SQ + 3], 1.0 / D, EPS,
                                        ALU.mult, ALU.add))
            step.wait()
            eng.memset(stat[:, 94:95], 0.0).then_inc(ms_ready, 1)
            eng.wait_ge(params_turned, 1)
            eng.tensor_copy(col[:, :], ps[:, 7, 0:N_ROWS]).then_inc(cols_ready, 1)
            eng.wait_ge(rstd_ready, 2)
            eng.tensor_scalar(metan[:, :], metan[:, :], stat[0:NM, RSTD + 2:RSTD + 3], None, ALU.mult)\
               .then_inc(xn_ready, 1)
            for t in range(NT):
                eng.tensor_scalar(xn[:, t, :], h_res[:, t, :], stat[:, RSTD + t:RSTD + t + 1], None, ALU.mult)\
                   .then_inc(xn_ready, 1)

            def lo(n, s):
                eng.wait_ge(hi_ready, n + 1)
                eng.tensor_tensor(w_lo[s][:, :, :], raw[s][:, :, :], w_hi[s][:, :, :].bitcast(F32), ALU.subtract)\
                   .then_inc(lo_ready, 1)

            lo(0, 0)
            for c in range(KC):
                eng.wait_ge(xt_hi_ready, c + 1)
                eng.wait_ge(cols_ready, 1)
                eng.scalar_tensor_tensor(out=xt_lo[:, c, :], in0=ps[:, 3 + c % 4, 0:T],
                                         scalar=col[:, ROW_G1 + c:ROW_G1 + c + 1],
                                         in1=xt_hi[:, c, :].bitcast(F32), op0=ALU.mult, op1=ALU.subtract)\
                   .then_inc(xt_lo_ready, 1)
            lo(1, 1)
            p = col[:, ROW_LA:ROW_LA + LB]
            step.done(eng.tensor_scalar(sp[:, 5, :], p, -1.0, None, ALU.mult))
            step.done(eng.tensor_tensor(sp[:, 0, :], p, sp[:, 5, :], ALU.min))
            eng.wait_ge(misc_in, 16 * 9)
            step.done(eng.tensor_tensor(lam_in[:, 0:2, :], lam_in[:, 0:2, :], lam_in[:, 2:4, :], ALU.mult))
            step.done(eng.tensor_reduce(stat[:, LP:LP + 2], lam_in[:, 0:2, :], AX.X, ALU.add))
            eng.tensor_scalar(sg[:, 0:1], col[:, ROW_SG:ROW_SG + 1], 1.0 - LAM_INIT, None, ALU.mult).then_inc(sp_e_in, 1)
            step.done(eng.tensor_scalar(negb[:, 0:2 * LB], col[:, ROW_BA:ROW_BA + 2 * LB], -1.0, None, ALU.mult))
            eng.wait_ge(sp_e_out, 2)
            step.done(eng.tensor_tensor(stat[:, LAM:LAM + 1], stat[:, LP + 1:LP + 2], stat[:, LP:LP + 1], ALU.subtract))
            step.done(eng.tensor_scalar(stat[:, NLAM:NLAM + 1], stat[:, LAM:LAM + 1], -LAM_INIT, None, ALU.add))
            step.done(eng.tensor_scalar(sp[:, 2, :], sp[:, 1, :], 2.0, None, ALU.add))
            step.done(eng.reciprocal(sp[:, 3, :], sp[:, 2, :]))
            step.done(eng.tensor_tensor(sp[:, 2, :], sp[:, 1, :], sp[:, 3, :], ALU.mult))
            step.done(eng.tensor_tensor(sp[:, 3, :], sp[:, 2, :], sp[:, 2, :], ALU.mult))
            step.done(eng.tensor_scalar(sp[:, 4, :], sp[:, 3, :], 1.0 / 17, 1.0 / 15, ALU.mult, ALU.add))
            for k in (13, 11, 9, 7, 5, 3, 1):
                step.done(eng.tensor_tensor(sp[:, 4, :], sp[:, 4, :], sp[:, 3, :], ALU.mult))
                step.done(eng.tensor_scalar(sp[:, 4, :], sp[:, 4, :], 1.0 / k, None, ALU.add))
            step.done(eng.tensor_tensor(sp[:, 4, :], sp[:, 4, :], sp[:, 2, :], ALU.mult))
            step.done(eng.tensor_scalar(sp[:, 5, :], sp[:, 5, :], 0.0, None, ALU.max))
            step.done(eng.scalar_tensor_tensor(out=sp[:, 5, :], in0=sp[:, 4, :], scalar=2.0, in1=sp[:, 5, :],
                                               op0=ALU.mult, op1=ALU.add))
            step.done(eng.tensor_scalar(sp[:, 6, :], sp[:, 5, :], -8.0, None, ALU.mult))
            step.done(eng.tensor_scalar(sp[:, 7, :], sp[:, 5, :], 8.0, None, ALU.mult))
            eng.wait_ge(consts_ready, 2)

            def v_rows(h):
                eng.wait_ge(v_turned, h + 1)
                eng.tensor_copy(v_tm[:, :, :], ps[:, 6, 0:TX].rearrange("p (t d) -> p t d", t=NT)).then_inc(v_out, 1)
                eng.tensor_copy(v_meta[:, :], ps[0:NM, 6, TX:TX + P]).then_inc(v_out, 1)

            def a_turn(h):
                eng.wait_ge(a_turned, h + 1)
                eng.tensor_copy(at_x[:, 0, :], ps[:, 5, 0:TX]).then_inc(a_out, 1)
                eng.tensor_copy(at_x[:, 1, P:TX], ps[:, 5, TX + P:2 * TX]).then_inc(a_out, 1)
                eng.tensor_copy(at_m[:, :], ps[0:NM, 7, 0:TX]).then_inc(a_out, 1)

            def o_norm(h):
                eng.wait_ge(o_sq, 2 * h + 2)
                eng.tensor_scalar(stat[:, ORS:ORS + NT], stat[:, OSQ:OSQ + NT], 1.0 / P, EPS, ALU.mult, ALU.add)\
                   .then_inc(o_ms, 1)
                eng.wait_ge(o_rstd, h + 1)
                eng.tensor_tensor(o_sb[:, :, :], ps[:, 7, TX:2 * TX].rearrange("p (t d) -> p t d", t=NT),
                                  stat[:, ORS:ORS + NT].unsqueeze(2).to_broadcast([P, NT, P]), ALU.mult)\
                   .then_inc(o_out, 1)

            def softmax_in(h):
                step.done(eng.tensor_scalar(bias[:, :], bias[:, :], 0.5, None, ALU.mult))
                eng.wait_ge(scores_done, h + 1)
                eng.scalar_tensor_tensor(out=s_sb[:, :, :], in0=ps[:, 3:5, 0:SW], scalar=DH ** -0.5,
                                         in1=bias[:, :].unsqueeze(1).to_broadcast([P, 2, SW]), op0=ALU.mult,
                                         op1=ALU.add).then_inc(biased, 1)
                eng.wait_ge(biased, h + 1)
                for t, c0, w in ((0, S0, K0), (1, S1, K1)):
                    eng.tensor_reduce(stat[:, NMAX + t:NMAX + t + 3:2], s_sb[:, :, c0:c0 + w], AX.X, ALU.max,
                                      negate=True).then_inc(max_ready, 1)

            def softmax_out(h):
                eng.wait_ge(probs_ready, 4 * h + 4)
                step.done(eng.reciprocal(stat[:, RL:RL + 4], stat[:, L:L + 4]))
                step.done(eng.tensor_scalar(stat[:, CM:CM + 2], stat[:, RL + 2:RL + 4], stat[:, NLAM:NLAM + 1], None,
                                            ALU.mult))
                for t, c0, w in ((0, S0, K0), (1, S1, K1)):
                    step.mark(eng.tensor_scalar(a_sb[:, c0:c0 + w], s_sb[:, 0, c0:c0 + w],
                                                stat[:, RL + t:RL + t + 1], None, ALU.mult))
                step.wait()
                for t, c0, w in ((0, S0, K0), (1, S1, K1)):
                    eng.scalar_tensor_tensor(out=a_sb[:, c0:c0 + w], in0=s_sb[:, 1, c0:c0 + w],
                                             scalar=stat[:, CM + t:CM + t + 1], in1=a_sb[:, c0:c0 + w],
                                             op0=ALU.mult, op1=ALU.add).then_inc(a_ready, 1)

            def mix_low(h):
                eng.wait_ge(mix_hi_ready, h + 1)
                eng.scalar_tensor_tensor(out=mix_lo[:, ds(LB + h, 1), :].rearrange("p a t -> p (a t)"),
                                         in0=ps[:, 6, 0:TX], scalar=sg[:, 0:1],
                                         in1=mix_hi[:, ds(LB + h, 1), :].rearrange("p a t -> p (a t)").bitcast(F32),
                                         op0=ALU.mult, op1=ALU.subtract).then_inc(mix_lo_ready, 1)

            def qkv(h):
                n = 3 * h
                if not is0(h):
                    v_rows(h - 1)
                lo(n + 2, 2)
                if not is0(h):
                    a_turn(h - 1)
                    o_norm(h - 1)
                lo(n + 3, 0)
                softmax_in(h)
                if not is0(h):
                    mix_low(h - 1)
                lo(n + 4, 1)
                softmax_out(h)

            qkv(0)
            looped(eng, step, 1, HEADS - 1, qkv, 5)

            def lru(i, b):
                g = 2 * i + b
                n = LRU0 + 2 * g
                s = 2 * b
                if is0(i) and b == 0:
                    v_rows(HEADS - 1)
                eng.wait_ge(acc_out, n + 1)
                for k in range(CONVW):
                    src = u_pad[:, CONVW - 1 - k:CONVW - 1 - k + T]
                    tap = col[:, ds(ROW_CW + k * LB + g, 1)]
                    if k == 0:
                        step.done(eng.tensor_scalar(xc[:, :], src, tap, col[:, ds(ROW_CB + g, 1)], ALU.mult, ALU.add))
                    else:
                        ins = eng.scalar_tensor_tensor(out=xc[:, :], in0=src, scalar=tap, in1=xc[:, :], op0=ALU.mult,
                                                       op1=ALU.add)
                        if k < CONVW - 1:
                            step.done(ins)
                ins.then_inc(xc_ready, 1)
                if is0(i) and b == 0:
                    a_turn(HEADS - 1)
                    o_norm(HEADS - 1)
                lo(n + 2, (s + 2) % RING)
                if is0(i) and b == 0:
                    mix_low(HEADS - 1)
                eng.wait_ge(e_ready, 2 * g + 2)
                at_least(eng, at_ready, 2 * g)
                step.done(eng.tensor_scalar(r_ri[:, :, :], e_ri[:, :, :], 1.0, None, ALU.add))
                eng.reciprocal(r_ri[:, :, :], r_ri[:, :, :]).then_inc(r_ready, 1)
                lo(n + 3, (s + 3) % RING)
                eng.wait_ge(r_ready, g + 1)
                step.done(eng.tensor_tensor(lr1[:, :], r_ri[:, 1, :], xc[:, :], ALU.mult))
                eng.wait_ge(at_ready, 2 * g + 2)
                step.done(eng.tensor_scalar(lr2[:, :], tg[:, :], 1.0, None, ALU.add))
                step.done(eng.reciprocal(lr2[:, :], lr2[:, :]))
                eng.scalar_tensor_tensor(out=lr2[:, :], in0=tg[:, :], scalar=2.0, in1=lr2[:, :], op0=ALU.mult,
                                         op1=ALU.mult).then_inc(q_ready, 1)
                eng.wait_ge(sqrt_ready, g + 1)
                step.done(eng.tensor_tensor(lr3[:, :], lr3[:, :], lr1[:, :], ALU.mult))
                step.done(eng.tensor_tensor_scan(hs_t[:, :], a_t[:, :], lr3[:, :], 0.0, ALU.mult, ALU.add))
                eng.wait_ge(gelu_ready, g + 1)
                eng.tensor_tensor(lru_f[:, :], hs_t[:, NM:T], gl1[:, :], ALU.mult).then_inc(lru_ready, 1)
                eng.wait_ge(mix_hi_ready, HEADS + g + 1)
                eng.tensor_tensor(mix_lo[:, ds(g, 1), :].rearrange("p a t -> p (a t)"), lru_f[:, :],
                                  mix_hi[:, ds(g, 1), :].rearrange("p a t -> p (a t)").bitcast(F32),
                                  ALU.subtract).then_inc(mix_lo_ready, 1)

            lru(0, 0)
            lru(0, 1)

            def lru2(i):
                lru(i, 0)
                lru(i, 1)

            looped(eng, step, 1, LB // 2 - 1, lru2, 18)

            def residual(m, b):
                eng.wait_ge(o_back, m + 1)
                at_least(eng, h_kept, m - 1)
                at_least(eng, h_sq, 2 * (m - 1))
                at_least(eng, h_turned, m - 1)
                eng.tensor_tensor(h_s[b][:, :, :], ps[:, 3, 0:TX].rearrange("p (t d) -> p t d", t=NT),
                                  h_res[:, :, ds(m * P, P)], ALU.add).then_inc(h_ready, 1)
                eng.wait_ge(h_turned, m + 1)
                at_least(eng, logits_done, m - 1)
                eng.tensor_scalar(h_tt[b][:, :], ps[:, 4, 0:TX], col[:, ds(ROW_G2 + m, 1)], None, ALU.mult)\
                   .then_inc(h_t_ready, 1)

            def project(i, s, last=False):
                m = RING * i + s
                if not (is0(i) and s == 0):
                    residual(m - 1, (s - 1) % 2)
                if not (last and s >= 2):
                    lo(OUT0 + m + 2, (s + 2) % RING)

            for s in range(RING):
                project(0, s)
            with eng.Fori(1, N_OUT // RING - 1) as i:
                for s in range(RING):
                    project(i, s)
            for s in range(RING):
                project(N_OUT // RING - 1, s, last=True)
            residual(N_OUT - 1, 1)

            eng.wait_ge(h_sq, 2 * N_OUT)
            step.done(eng.tensor_reduce(stat[:, HRS:HRS + NT],
                                        stat[:, HSQ:HSQ + NT * N_OUT].rearrange("p (t m) -> p t m", t=NT), AX.X, ALU.add))
            eng.tensor_scalar(stat[:, HRS:HRS + NT], stat[:, HRS:HRS + NT], 1.0 / D, EPS, ALU.mult, ALU.add)\
               .then_inc(h_ms, 1)
            eng.wait_ge(h_rstd, 1)
            eng.wait_ge(logits_done, N_OUT)
            lg = rt[:, 0, :, 0:NG]
            le = rt[:, 3, :, :]
            for t in range(NT):
                step.mark(eng.scalar_tensor_tensor(out=rt[:, 0, t, 0:NG], in0=ps[:, 5 + t, 0:NG],
                                                   scalar=stat[:, HRS + t:HRS + t + 1], in1=rb[:, 0:NG],
                                                   op0=ALU.mult, op1=ALU.add))
                step.mark(eng.scalar_tensor_tensor(out=rt[:, 3, t, :], in0=ps[:, 5 + t, NG:NG + NE],
                                                   scalar=stat[:, HRS + t:HRS + t + 1], in1=rb[:, NG:NG + NE],
                                                   op0=ALU.mult, op1=ALU.add))
            step.wait()
            prio = stat[:, 88:92].unsqueeze(1).to_broadcast([P, NT, 4])

            def first_max(v, m, hot, work):
                step.done(eng.tensor_reduce(m, v, AX.X, ALU.max))
                step.done(eng.tensor_tensor(work, v, m.to_broadcast([P, NT, 4]), ALU.is_equal))
                step.done(eng.tensor_tensor(work, work, prio, ALU.mult))
                step.done(eng.tensor_reduce(rt[:, 17, :, 0:1], work, AX.X, ALU.max))
                step.done(eng.tensor_tensor(hot, prio, rt[:, 17, :, 0:1].to_broadcast([P, NT, 4]), ALU.is_equal))

            gmax = rt[:, 4, :, 0:1]
            ghot = rt[:, 5, :, 0:NG]
            first_max(lg, gmax, ghot, rt[:, 6, :, 0:NG])
            eng.tensor_tensor(rt[:, 1, :, 0:NG], lg, gmax.to_broadcast([P, NT, NG]), ALU.subtract).then_inc(rt_max, 1)
            for t in range(NT):
                step.mark(eng.tensor_tensor(rt[:, 7, t, :].rearrange("p (g j) -> p g j", g=NG),
                                            rt[:, 3, t, :].rearrange("p (g j) -> p g j", g=NG),
                                            rt[:, 5, t, 0:NG].unsqueeze(2).to_broadcast([P, NG, EPG]), ALU.mult))
            step.wait()
            lin = rt[:, 8, :, 0:EPG]
            for t in range(NT):
                step.mark(eng.tensor_reduce(rt[:, 8, t, 0:EPG], rt[:, 7, t, :].rearrange("p (g j) -> p j g", g=NG),
                                            AX.X, ALU.add))
            step.wait()
            hot1, hot2 = rt[:, 9, :, 0:EPG], rt[:, 11, :, 0:EPG]
            m1, m2 = rt[:, 12, :, 0:1], rt[:, 12, :, 1:2]
            first_max(lin, m1, hot1, rt[:, 6, :, 0:EPG])
            step.done(eng.scalar_tensor_tensor(out=rt[:, 13, :, 0:EPG], in0=hot1, scalar=-1e30, in1=lin,
                                               op0=ALU.mult, op1=ALU.add))
            first_max(rt[:, 13, :, 0:EPG], m2, hot2, rt[:, 6, :, 0:EPG])
            eng.tensor_tensor(rt[:, 10, :, 0:1], m2, m1, ALU.subtract).then_inc(rt_max, 1)
            for t in range(NT):
                for k, hot in ((14, 9), (15, 11)):
                    step.mark(eng.tensor_tensor(rt[:, k, t, :].rearrange("p (g j) -> p g j", g=NG),
                                                rt[:, 5, t, 0:NG].unsqueeze(2).to_broadcast([P, NG, EPG]),
                                                rt[:, hot, t, 0:EPG].unsqueeze(1).to_broadcast([P, NG, EPG]),
                                                ALU.mult))
            step.wait()
            member = rt[:, 16, :, :]
            eng.tensor_tensor(member, rt[:, 14, :, :], rt[:, 15, :, :], ALU.add).then_inc(members, 1)
            eng.wait_ge(members, 1)
            for t in range(NT):
                step.mark(eng.tensor_scalar(rt[:, 18, t, :], rt[:, 16, t, :], stat[:, 86 + t:87 + t], None, ALU.mult))
            step.wait()
            step.done(eng.scalar_tensor_tensor(out=rt[:, 18, :, :], in0=rt[:, 15, :, :], scalar=float(TX),
                                               in1=rt[:, 18, :, :], op0=ALU.mult, op1=ALU.add))
            step.done(eng.scalar_tensor_tensor(out=rt[:, 18, :, :], in0=member, scalar=-BIG, in1=rt[:, 18, :, :],
                                               op0=ALU.mult, op1=ALU.add))
            eng.wait_ge(ranks_done, 1)
            rank = rt[:, 19, :, :]
            step.done(eng.scalar_tensor_tensor(out=rank, in0=ps[:, 3, 0:NT * NE].rearrange("p (t e) -> p t e", t=NT),
                                               scalar=1.0, in1=member, op0=ALU.add, op1=ALU.mult))
            step.done(eng.tensor_scalar(rank, rank, -1.0, None, ALU.add))

            def select(r):
                at_least(eng, gathered, NE * r)
                for t in range(NT):
                    ins = eng.tensor_tensor(sel[:, t, :, :], rank[:, t, :].unsqueeze(2).to_broadcast([P, NE, C]),
                                            slot_no[:, :].unsqueeze(1).to_broadcast([P, NE, C]), ALU.is_equal)
                    ins.then_inc(sel_ready, 1)

            def row_lists(r):
                eng.wait_ge(lists_done, r + 1)
                at_least(eng, scattered, 16 * NE * r)
                eng.tensor_scalar(idx_i[:, :], ps[0:C, 2, 0:NE], BIG, None, ALU.add).then_inc(lists_ready, 1)

            select(0)
            for t in range(NT):
                eng.wait_ge(hn_hi_ready, t + 1)
                eng.scalar_tensor_tensor(out=hn_lo[:, t, :, :], in0=h_res[:, t, :].rearrange("p (q c) -> p c q", c=KC),
                                         scalar=stat[:, HRS + t:HRS + t + 1], in1=hn_hi[:, t, :, :].bitcast(F32),
                                         op0=ALU.mult, op1=ALU.subtract).then_inc(hn_lo_ready, 1)

            def gathered_x(i):
                eng.wait_ge(gathered, i + 1)
                for j, w in enumerate((6, 6, 4)):
                    ins = eng.tensor_tensor(x_e[:, 6 * j:6 * j + w, :],
                                            ps[:, 5 + j, 0:w * C].rearrange("p (c s) -> p c s", c=w),
                                            g2e[:, 6 * j:6 * j + w].unsqueeze(2).to_broadcast([P, w, C]), ALU.mult)
                    ins.then_inc(x_e_ready, 1)

            gathered_x(0)
            row_lists(0)
            eng.wait_ge(rt_exp, 2)
            step.done(eng.tensor_reduce(rt[:, 17, :, 1:2], rt[:, 2, :, 0:NG], AX.X, ALU.add))
            step.done(eng.tensor_scalar(rt[:, 17, :, 2:3], rt[:, 10, :, 1:2], 1.0, None, ALU.add))
            step.done(eng.tensor_tensor(rt[:, 17, :, 3:4], rt[:, 17, :, 1:2], rt[:, 17, :, 2:3], ALU.mult))
            w12 = stat[:, W12:W12 + 4].rearrange("p (t k) -> p t k", k=2)
            step.done(eng.reciprocal(w12[:, :, 0:1], rt[:, 17, :, 3:4]))
            step.done(eng.tensor_tensor(w12[:, :, 1:2], w12[:, :, 0:1], rt[:, 10, :, 1:2], ALU.mult))
            step.done(eng.tensor_reduce(stat[:, 95:96], ps[:, 4, 0:NE], AX.X, ALU.max))
            eng.tensor_copy(cnt[:, 0:1], stat[:, 95:96]).then_inc(cnt_ready, 1)

            def silu(i):
                gate = ps[:, 0, 0:FC * C]
                flat = e_rec[:, :, :].rearrange("p f c -> p (f c)")
                eng.wait_ge(e_neg_ready, i + 1)
                step.done(eng.tensor_scalar(flat, e_neg[:, :, :].rearrange("p f c -> p (f c)"), 1.0, None, ALU.add))
                step.done(eng.reciprocal(flat, flat))
                step.done(eng.tensor_tensor(flat, gate, flat, ALU.mult))
                eng.wait_ge(slot_used, 12 * i + 8)
                eng.tensor_tensor(h_e[:, :, :].rearrange("p f c -> p (f c)"), ps[:, 1, 0:FC * C], flat, ALU.mult)\
                   .then_inc(h_e_ready, 1)

            def y_turn(i):
                eng.wait_ge(slot_used, 12 * i + 12)
                eng.tensor_copy(y_t[:, 12:16, :].rearrange("p f c -> p (f c)"), ps[:, 4, 0:4 * C]).then_inc(y_t_dve, 1)

            def expert(i):
                silu(i)
                gathered_x(i + 1)
                y_turn(i)

            def last_expert(i):
                silu(i)
                y_turn(i)

            looped(eng, step, 0, NE - 1, expert, 3)
            last_expert(NE - 1)
            k0 = step.base + step.k
            per_round = 1 + 3 * NE
            eng.wait_ge(cnt_ready, 1)
            most = eng.value_load(cnt[0:1, 0:1], min_val=0, max_val=TX)
            with eng.Fori(1, ROUNDS) as r:
                with eng.If(most > r * C):
                    step.begin(k0 + (r - 1) * per_round)
                    step.done(eng.tensor_scalar(rank, rank, float(-C), None, ALU.add))
                    select(r)
                    gathered_x(r * NE)
                    row_lists(r)
                    looped(eng, step, 0, NE - 1, lambda e: expert(r * NE + e), 3)
                    last_expert(r * NE + NE - 1)

            for t in range(NT):
                eng.wait_ge(y_in, 16 * (t + 1)) if False else eng.wait_ge(y_in, 16 * NT)
                eng.scalar_tensor_tensor(out=ysum[:, t, :], in0=y_rows[:, 0, t, :],
                                         scalar=stat[:, W12 + 2 * t:W12 + 2 * t + 1], in1=h_res[:, t, :],
                                         op0=ALU.mult, op1=ALU.add).then_inc(y_half, 1)
                eng.wait_ge(y_half, t + 1)
                eng.scalar_tensor_tensor(out=ysum[:, t, :], in0=y_rows[:, 1, t, :],
                                         scalar=stat[:, W12 + 2 * t + 1:W12 + 2 * t + 2], in1=ysum[:, t, :],
                                         op0=ALU.mult, op1=ALU.add).then_inc(ysum_ready, 1)
            eng.wait_ge(y_sq, NT)
            eng.tensor_scalar(stat[:, YRS:YRS + NT], stat[:, YSQ:YSQ + NT], 1.0 / D, EPS, ALU.mult, ALU.add)\
               .then_inc(y_ms, 1)
            eng.wait_ge(y_rstd, 1)
            eng.wait_ge(fgain_in, 16)
            for t in range(NT):
                eng.scalar_tensor_tensor(out=yout[:, t, :], in0=ysum[:, t, :], scalar=stat[:, YRS + t:YRS + t + 1],
                                         in1=fgain[:, :], op0=ALU.mult, op1=ALU.mult).then_inc(yout_ready, 1)

        @block.tensor
        def _(eng):
            eng.wait_ge(consts_ready, 1)
            eng.wait_ge(params_in, 16 * 8)
            eng.transpose(ps[:, 7, 0:N_ROWS], params[0:N_ROWS, :], ident[0:N_ROWS, 0:N_ROWS]).then_inc(params_turned, 1)
            eng.wait_ge(xn_ready, 3)
            for c in range(KC):
                if c >= 4:
                    eng.wait_ge(xt_lo_ready, c - 3)
                cs = slice(c * P, (c + 1) * P)
                eng.transpose(ps[:, 3 + c % 4, 0:NM], metan[:, cs], ident[0:NM, 0:NM])
                eng.transpose(ps[:, 3 + c % 4, NM:NM + P], xn[:, 0, cs], ident[:, :])
                eng.transpose(ps[:, 3 + c % 4, NM + P:T], xn[:, 1, cs], ident[:, :]).then_inc(xt_turned, 1)

            def chunk(n, s, acc, act_hi, act_lo, t0, extras=(), order=range(KC), ready=None, freed=2):
                eng.wait_ge(lo_ready, n + 1)
                at_least(eng, acc_out, n - freed + 1)
                w = act_hi.shape[2] - t0
                for k, c in enumerate(order):
                    if k in dict(extras):
                        dict(extras)[k]()
                    if ready:
                        ready(c)
                    o = ps[:, acc, 0:w]
                    eng.matmul(o, w_hi[s][:, c, :], act_hi[:, c, t0:], start=(k == 0), stop=False,
                               skip_group_check=True)
                    eng.matmul(o, w_hi[s][:, c, :], act_lo[:, c, t0:], start=False, stop=False, skip_group_check=True)
                    ins = eng.matmul(o, w_lo[s][:, c, :], act_hi[:, c, t0:], start=False, stop=(k == KC - 1),
                                     skip_group_check=True)
                ins.then_inc(chunk_done, 1)

            def turn_v(h):
                eng.wait_ge(acc_out, 3 * h + 3)
                if not is0(h):
                    eng.wait_ge(mix_lo_ready, h)
                eng.transpose(ps[:, 6, 0:P], v_t[:, NM:NM + P], ident[:, :])
                eng.transpose(ps[:, 6, P:TX], v_t[:, NM + P:T], ident[:, :])
                eng.transpose(ps[0:NM, 6, TX:TX + P], v_t[:, 0:NM], ident[:, :]).then_inc(v_turned, 1)

            def score(h):
                eng.wait_ge(acc_out, 3 * h + 2)
                at_least(eng, biased, h)
                for m in range(2):
                    rows = slice(DH * m, DH * (m + 1))
                    for t, c0, w in ((0, S0, K0), (1, S1, K1)):
                        ins = eng.matmul(ps[:, 3 + m, c0:c0 + w], q_t[rows, t * P:(t + 1) * P], k_t[rows, 0:w],
                                         start=True, stop=True)
                ins.then_inc(scores_done, 1)

            def turn_a(h):
                eng.wait_ge(a_ready, 2 * h + 2)
                at_least(eng, a_out, 3 * h)
                eng.transpose(ps[:, 5, 0:P], a_sb[:, S0 + NM:S0 + NM + P], ident[:, :])
                eng.transpose(ps[:, 5, P:TX], a_sb[:, S1 + NM:S1 + NM + P], ident[:, :])
                eng.transpose(ps[:, 5, TX + P:2 * TX], a_sb[:, S1 + NM + P:S1 + T], ident[:, :])
                eng.transpose(ps[0:NM, 7, 0:P], a_sb[:, S0:S0 + NM], ident[:, :])
                eng.transpose(ps[0:NM, 7, P:TX], a_sb[:, S1:S1 + NM], ident[:, :]).then_inc(a_turned, 1)

            def attend(h):
                eng.wait_ge(a_out, 3 * h + 3)
                eng.wait_ge(v_out, 2 * h + 2)
                at_least(eng, o_out, h)
                for t in range(NT):
                    o = ps[:, 7, TX + t * P:TX + (t + 1) * P]
                    q = slice(t * P, (t + 1) * P)
                    eng.matmul(o, at_m[:, q], v_meta[:, :], start=True, stop=False)
                    for k in range(t + 1):
                        ins = eng.matmul(o, at_x[:, k, q], v_tm[:, k, :], start=False, stop=(k == t))
                ins.then_inc(o_done, 1)

            def turn_o(h):
                eng.wait_ge(o_out, h + 1)
                eng.transpose(ps[:, 6, 0:P], o_sb[:, 0, :], ident[:, :])
                eng.transpose(ps[:, 6, P:TX], o_sb[:, 1, :], ident[:, :]).then_inc(o_turned, 1)

            def qkv(h):
                n = 3 * h
                if is0(h):
                    chunk(0, 0, 0, xt_hi, xt_lo, NM, ready=lambda c: eng.wait_ge(xt_lo_ready, c + 1), freed=3)
                    chunk(1, 1, 1, xt_hi, xt_lo, 0, freed=3)
                    chunk(2, 2, 2, xt_hi, xt_lo, 0, extras=[(6, lambda: score(0))], freed=3)
                    return
                chunk(n, 0, 0, xt_hi, xt_lo, NM, extras=[(4, lambda: turn_v(h - 1))], freed=3)
                chunk(n + 1, 1, 1, xt_hi, xt_lo, 0, extras=[(4, lambda: turn_a(h - 1)), (12, lambda: attend(h - 1))],
                      freed=3)
                chunk(n + 2, 2, 2, xt_hi, xt_lo, 0, extras=[(6, lambda: score(h)), (12, lambda: turn_o(h - 1))],
                      freed=3)

            qkv(0)
            with eng.Fori(1, HEADS) as h:
                qkv(h)

            def gates(g, b, i):
                eng.wait_ge(xc_ready, g + 1)
                eng.wait_ge(gates_in[b], 32 * (i + 1))
                at_least(eng, e_ready, 2 * g)
                if is0(i) and b == 0:
                    eng.wait_ge(biased, HEADS)
                eng.matmul(ps[:, 3, 0:T], g_w[:, b, 0, :], xc[:, :], start=True, stop=True)
                eng.matmul(ps[:, 4, 0:T], g_w[:, b, 1, :], xc[:, :], start=True, stop=True).then_inc(gates_done, 1)

            def lru(i, b):
                g = 2 * i + b
                n = LRU0 + 2 * g
                h = HEADS - 1
                first = is0(i) and b == 0
                chunk(n, 2 * b, 0, xt_hi, xt_lo, 0, extras=[(4, lambda: turn_v(h)), (12, lambda: turn_a(h))]
                      if first else ())
                chunk(n + 1, 2 * b + 1, 1, xt_hi, xt_lo, NM,
                      extras=[(3, lambda: attend(h)), (12, lambda: gates(g, b, i)), (15, lambda: turn_o(h))]
                      if first else [(12, lambda: gates(g, b, i))])

            lru(0, 0)
            lru(0, 1)
            with eng.Fori(1, LB // 2) as i:
                lru(i, 0)
                lru(i, 1)

            def turn_back(m, b):
                eng.wait_ge(acc_out, OUT0 + m + 1)
                at_least(eng, h_ready, m)
                for t in range(NT):
                    ins = eng.transpose(ps[:, 3, t * P:(t + 1) * P], o_t[b][:, t * P:(t + 1) * P], ident[:, :])
                ins.then_inc(o_back, 1)

            def turn_h(m, b):
                eng.wait_ge(h_ready, m + 1)
                at_least(eng, h_t_ready, m)
                for t in range(NT):
                    ins = eng.transpose(ps[:, 4, t * P:(t + 1) * P], h_s[b][:, t, :], ident[:, :])
                ins.then_inc(h_turned, 1)

            def logits(m, b, last=False):
                eng.wait_ge(h_t_ready, m + 1)
                for t in range(NT):
                    ins = eng.matmul(ps[:, 5 + t, 0:NG + NE], h_tt[b][:, t * P:(t + 1) * P],
                                     rw[:, ds(m, 1), :].rearrange("p a e -> p (a e)"), start=is0(m), stop=last,
                                     skip_group_check=True)
                ins.then_inc(logits_done, 1)

            heads_first = list(range(LB, KC)) + list(range(LB))

            def mix_ready(c):
                k = HEADS + c + 1 if c < LB else c - LB + 1
                eng.wait_ge(mix_hi_ready, k)
                eng.wait_ge(mix_lo_ready, k)

            def project(i, s):
                m = RING * i + s
                extras = ()
                if not (is0(i) and s == 0):
                    b = (s - 1) % 2
                    extras = [(2, lambda: turn_back(m - 1, b)), (7, lambda: turn_h(m - 1, b)),
                              (13, lambda: logits(m - 1, b))]
                chunk(OUT0 + m, s, s % 2, mix_hi, mix_lo, 0, extras=extras, order=heads_first,
                      ready=mix_ready if (is0(i) and s == 0) else None)

            for s in range(RING):
                project(0, s)
            with eng.Fori(1, N_OUT // RING) as i:
                for s in range(RING):
                    project(i, s)
            turn_back(N_OUT - 1, 1)
            turn_h(N_OUT - 1, 1)
            logits(N_OUT - 1, 1, last=True)

            eng.wait_ge(members, 1)
            m0, m1 = rt[:, 16, 0, :], rt[:, 16, 1, :]
            eng.matmul(ps[:, 3, 0:NE], ltri[:, :], m0, start=True, stop=True)
            eng.matmul(ps[:, 3, NE:2 * NE], ones[:, :], m0, start=True, stop=False)
            eng.matmul(ps[:, 3, NE:2 * NE], ltri[:, :], m1, start=False, stop=True)
            eng.matmul(ps[:, 4, 0:NE], ones[:, :], m0, start=True, stop=False)
            eng.matmul(ps[:, 4, 0:NE], ones[:, :], m1, start=False, stop=True).then_inc(ranks_done, 1)

            def gather(i, e):
                for c in range(KC):
                    o = ps[:, 5 + c // 6, (c % 6) * C:(c % 6 + 1) * C]
                    for k, (part, t) in enumerate(((hn_hi, 0), (hn_hi, 1), (hn_lo, 0), (hn_lo, 1))):
                        if is0(i) and c == 0:
                            eng.wait_ge(hn_hi_ready, NT)
                            eng.wait_ge(hn_lo_ready, NT)
                        pick = sel[:, t, ds(e, 1), :].rearrange("p e s -> p (e s)")
                        ins = eng.matmul(o, part[:, t, c, :], pick, start=(k == 0), stop=(k == 3))
                ins.then_inc(gathered, 1)

            def lists(r):
                for e in range(NE):
                    for t in range(NT):
                        ins = eng.matmul(ps[0:C, 2, e:e + 1], sel[:, t, e, :].bitcast(F32), rt[:, 18, t, e:e + 1],
                                         start=(t == 0), stop=(t == NT - 1))
                ins.then_inc(lists_done, 1)

            def start_round(r):
                eng.wait_ge(sel_ready, NT * (r + 1))
                at_least(eng, y_out, 4 * NE * r)
                gather(r * NE if not isinstance(r, int) else 0, 0)
                lists(r)

            def through(i, s):
                eng.wait_ge(slot_in[s], 16 * (i + 1))

            def up_proj(i, acc, s0):
                for s in range(s0, s0 + 4):
                    through(i, s)
                    w = slots[s][:, :].rearrange("p (c f) -> p c f", c=4)
                    for c in range(4):
                        kc = 4 * (s - s0) + c
                        for f in range(FC):
                            ins = eng.matmul(ps[:, acc, f * C:(f + 1) * C], w[:, c, f * P:(f + 1) * P], x_e[:, kc, :],
                                             start=(kc == 0 and f == 0), stop=(kc == KC - 1), skip_group_check=True)
                    ins.then_inc(slot_used, 1)

            def expert(i, e, last=False):
                eng.wait_ge(x_e_ready, 3 * (i + 1))
                at_least(eng, h_e_ready, i)
                up_proj(i, 0, 0)
                up_proj(i, 1, 4)
                if not last:
                    at_least(eng, y_out, 4 * i)
                    gather(i + 1 if not isinstance(i, int) else i + 1, e + 1)
                eng.wait_ge(h_e_ready, i + 1)
                if is0(i):
                    eng.wait_ge(lists_ready, 1)
                for f in range(FC):
                    through(i, 8 + f)
                    for d in range(KC):
                        ins = eng.matmul(ps[:, 2 + d // 6, (d % 6) * C:(d % 6 + 1) * C],
                                         slots[8 + f][:, d * P:(d + 1) * P], h_e[:, f, :],
                                         start=(f == 0 and d % 6 == 0), stop=(f == FC - 1), skip_group_check=True)
                    ins.then_inc(slot_used, 1)
                eng.wait_ge(y_t_act, 2 * (i + 1))
                eng.wait_ge(y_t_dve, i + 1)
                eng.wait_ge(x_e_ready, 3 * (i + 1) if last else 3 * (i + 2))
                if last:
                    at_least(eng, y_out, 4 * i)
                for j in range(4):
                    if j == 3:
                        eng.wait_ge(y_out, 4 * i + 1)
                    for d in range(4 * j, 4 * j + 4):
                        ins = eng.transpose(ps[0:C, 5 + j % 3, (d % 4) * P:(d % 4 + 1) * P], y_t[:, d, :], ident[:, :])
                    ins.then_inc(y_back, 1)

            start_round(0)
            eng.wait_ge(lists_ready, 1)
            expert(0, 0)
            with eng.Fori(1, NE - 1) as e:
                expert(e, e)
            expert(NE - 1, NE - 1, last=True)
            eng.wait_ge(cnt_ready, 1)
            most = eng.value_load(cnt[0:1, 0:1], min_val=0, max_val=TX)
            with eng.Fori(1, ROUNDS) as r:
                with eng.If(most > r * C):
                    start_round(r)
                    eng.wait_ge(lists_ready, r + 1)
                    apart(eng)
                    with eng.Fori(0, NE - 1) as e:
                        expert(r * NE + e, e)
                    expert(r * NE + NE - 1, NE - 1, last=True)

    return nc


_INS = ["x", "meta_tokens", "norm1_g", "w_in", "conv_w", "conv_b", "gate_a_w", "gate_a_b", "gate_x_w", "gate_x_b",
        "lru_a_param", "lambda_q1", "lambda_k1", "lambda_q2", "lambda_k2", "subln_g", "w_out", "norm2_g",
        "router_g_w", "router_g_b", "router_e_w", "router_e_b", "exp_w_gate", "exp_w_up", "exp_w_down",
        "final_norm_g"]


def kernel(**inputs):
    import numpy as np
    import concourse.bacc as bacc
    from concourse.bass_utils import run_bass_kernel_spmd

    nc = bacc.Bacc("TRN2", target_bir_lowering=False, num_devices=1)
    arrays, args = {}, []
    for name in _INS:
        a = np.ascontiguousarray(inputs[name])
        arrays[f"in_{name}"] = a
        args.append(nc.dram_tensor(f"in_{name}", a.shape, mybir.dt.from_np(a.dtype), kind="ExternalInput").ap())
    out = nc.dram_tensor("out", (1, TX, D), F32, kind="ExternalOutput").ap()
    build(nc, *args, out)
    r = run_bass_kernel_spmd(nc, [arrays], core_ids=[0])
    return r.results[0]["out"]
```

```python
from contextlib import ExitStack

import concourse.bass as bass
from concourse import mybir

P = 128
D = 2048
KC = D // P
TX = 256
NM = 16
T = NM + TX
NT = TX // P
HEADS = 8
DH = 64
CHUNK = 64
LW = 1024
LB = LW // P
CONVW = 4
NG, EPG = 4, 4
NE = NG * EPG
F = 512
FC = F // P
C = 64
MORE = 2 * TX // C
N_TAB = MORE + 2
SLOTS = 12
PARTS = 24
PW = 2 * F
POOL_PARTS = (2, 6, 10, 14, 18, 22)
LO_DVE = PARTS - len(POOL_PARTS)
EPS = 1e-6
LAM_INIT = 0.8 - 0.6
BIG = 4096.0
K0, K1 = NM + P, T
S0, S1 = 0, K0
SW = K0 + K1

N_QKV = 3 * HEADS
N_LRU = 2 * LB
N_OUT = D // P
LRU0 = N_QKV
OUT0 = N_QKV + N_LRU
N_CHUNKS = OUT0 + N_OUT
QKV_RING = 3
RING = 4

F32 = mybir.dt.float32
F32R = mybir.dt.float32r
I32 = mybir.dt.int32
U32 = mybir.dt.uint32
ALU = mybir.AluOpType
ACT = mybir.ActivationFunctionType
AX = mybir.AxisListType

ROW_G1, ROW_G2, ROW_CB, ROW_CW, ROW_BA, ROW_BX, ROW_LA, ROW_SG = 0, 16, 32, 40, 72, 80, 88, 96
N_ROWS = 97


def ds(start, size):
    return bass.ds(start, size)


class Steps:

    def __init__(self, eng, sem):
        self.eng, self.sem, self.base, self.k = eng, sem, 0, 0

    def mark(self, ins):
        self.k += 1
        ins.then_inc(self.sem, 1)

    def wait(self):
        self.eng.wait_ge(self.sem, self.base + self.k)

    def done(self, ins):
        self.mark(ins)
        self.wait()

    def begin(self, base):
        self.base, self.k = base, 0


def looped(eng, steps, first, count, body, per_body, ticks=None):
    start = steps.base + steps.k
    with eng.Fori(first, first + count) as i:
        steps.begin((i - first) * per_body + start)
        body(i)
        assert steps.k == per_body, (steps.k, per_body)
    steps.begin(start + count * per_body)


def at_least(eng, sem, value):
    if isinstance(value, int) and value <= 0:
        return
    eng.wait_ge(sem, value)


def build(nc, x, meta_tokens, norm1_g, w_in, conv_w, conv_b, gate_a_w, gate_a_b, gate_x_w, gate_x_b,
          lru_a_param, lambda_q1, lambda_k1, lambda_q2, lambda_k2, subln_g, w_out, norm2_g,
          router_g_w, router_g_b, router_e_w, router_e_b, exp_w_gate, exp_w_up, exp_w_down,
          final_norm_g, out):
    with ExitStack() as ctx:
        ctx.enter_context(nc.allow_non_contiguous_dma("small parameter loads"))

        def sem(name):
            return ctx.enter_context(nc.semaphore(name))

        base = [(nc.sbuf_base + 31) // 32 * 32]
        arena = nc.alloc_sbuf_tensor("arena", [P, (nc.sbuf_usable_end - base[0] - 64) // 4], F32)
        first_byte = base[0]
        limit = nc.sbuf_usable_end

        def place(name, shape, dt, offset=None):
            n = 4
            for s in shape[1:]:
                n *= s
            n = (n + 31) // 32 * 32
            if offset is None:
                offset = base[0]
                base[0] += n
                assert base[0] <= limit, (name, base[0], limit)
            return nc.alloc_sbuf_tensor_at(name, shape, dt, offset=offset), offset, offset + n

        def region(start, end, *parts):
            o = start
            got = []
            for name, shape, dt in parts:
                t, _, o = place(name, shape, dt, o)
                got.append(t)
            assert o <= end, (parts[-1][0], o, end)
            return got

        h_res, _, _ = place("h_res", [P, NT, D], F32)
        mix_hi, MIX, _ = place("mix_hi", [P, KC, TX], F32R)
        mix_lo, _, MIX_END = place("mix_lo", [P, KC, TX], F32R)
        x_g, x_s, x_hl, y_e = region(MIX, MIX_END, ("x_g", [C, D], F32), ("x_s", [P, D], F32R),
                                     ("x_hl", [P, KC, 2, C], F32R), ("y_e", [C, D], F32))
        xn, metan, junk = region(MIX, MIX_END, ("xn", [P, NT, D], F32), ("metan", [NM, D], F32), ("junk", [P, D], F32))
        STAGE = base[0]
        raw, w_lo, w_hi = [], [], []
        for s in range(RING):
            t, o, _ = place(f"raw{s}", [P, KC, P], F32)
            raw.append(t)
            w_lo.append(place(f"w_lo{s}", [P, KC, P], F32R, o)[0])
            w_hi.append(place(f"w_hi{s}", [P, KC, P], F32R)[0])
        STAGE_END = base[0]
        WREG = base[0]
        m_raw, m_lo, m_hi = [], [], []
        SLOT_BYTES = 4 * PW
        for n in range(SLOTS):
            here = None if n < SLOTS - 2 else STAGE + 2 * SLOT_BYTES * (n - (SLOTS - 2))
            t, o, _ = place(f"m_raw{n}", [P, PW], F32, here)
            m_raw.append(t)
            m_lo.append(place(f"m_lo{n}", [P, PW], F32R, o)[0])
            m_hi.append(place(f"m_hi{n}", [P, PW], F32R, None if here is None else here + SLOT_BYTES)[0])
        WREG_END = base[0]
        g2b, hn_rows, gu_sb, th, h_f, h_hl, sel, ident_r, rt = region(
            STAGE + 4 * SLOT_BYTES, STAGE_END, ("g2b", [P, D], F32), ("hn_rows", [P, NT, KC, P], F32),
            ("gu_sb", [P, 2, F], F32), ("th", [P, FC, C], F32), ("h_f", [P, FC, C], F32),
            ("h_hl", [P, FC, 2, C], F32R), ("sel", [P, NT, C], F32), ("ident_r", [P, P], F32R),
            ("rt", [P, 20, NT, NE], F32))
        (xt_hi, xt_lo, q_t, k_t, v_t, v_tm, v_meta, s_sb, a_sb, at_x, at_m, o_sb, u_pad, yg_t, xc, e_ri, r_ri, a_t, tg,
         lr1, lr2, lr3, gl1, gl2, hs_t, g_w, lru_f, mix_f) = region(
            WREG, WREG_END, ("xt_hi", [P, KC, T], F32R), ("xt_lo", [P, KC, T], F32R),
            ("q_t", [P, TX], F32), ("k_t", [P, T], F32), ("v_t", [P, T], F32), ("v_tm", [P, NT, P], F32),
            ("v_meta", [NM, P], F32), ("s_sb", [P, 2, SW], F32), ("a_sb", [P, SW], F32),
            ("at_x", [P, NT, TX], F32), ("at_m", [NM, TX], F32), ("o_sb", [P, NT, P], F32),
            ("u_pad", [P, CONVW - 1 + T], F32), ("yg_t", [P, TX], F32), ("xc", [P, T], F32),
            ("e_ri", [P, 2, T], F32), ("r_ri", [P, 2, T], F32), ("a_t", [P, T], F32), ("tg", [P, T], F32),
            ("lr1", [P, T], F32), ("lr2", [P, T], F32), ("lr3", [P, T], F32), ("gl1", [P, TX], F32),
            ("gl2", [P, TX], F32), ("hs_t", [P, T], F32), ("g_w", [P, 2, 2, P], F32), ("lru_f", [P, TX], F32),
            ("mix_f", [P, TX], F32))
        y_rows, ysum, yout, fgain = region(WREG, WREG_END, ("y_rows", [P, 2, NT, D], F32), ("ysum", [P, NT, D], F32),
                                           ("yout", [P, NT, D], F32), ("fgain", [P, D], F32))
        def small(name, shape, dt=F32):
            return place(name, shape, dt)[0]

        ident = small("ident", [P, P])
        ltri = small("ltri", [P, P])
        ones = small("ones", [P, P])
        params = small("params", [P, P])
        col = small("col", [P, N_ROWS])
        lam_in = small("lam_in", [P, 4, DH])
        bias = small("bias", [P, SW])
        rw = small("rw", [P, KC, NG + NE])
        rb = small("rb", [P, NG + NE])
        slot_no = small("slot_no", [P, C])
        pair = small("pair", [P, C])
        row_col = small("row_col", [P, NT, 2])
        expert_no = small("expert_no", [P, (TX // C - 1) * NE])
        first_no = small("first_no", [P, (TX // C - 1) * NE])
        unit_no = small("unit_no", [P, N_TAB])
        tab = small("tab", [P, 2, N_TAB])
        tab_i = small("tab_i", [P, N_TAB + 2], I32)
        stat = small("stat", [P, 96])
        negb = small("negb", [P, 3 * LB])
        sp = small("sp", [P, 8, LB])
        o_t = [small(f"o_t{i}", [P, TX]) for i in range(2)]
        idx_n = small("idx_n", [C, 1], I32)
        idx_m = small("idx_m", [C, 1], I32)
        idx_i = small("idx_i", [C, 1], I32)
        idx_g = small("idx_g", [C, 1], I32)
        h_s = [small(f"h_s{i}", [P, NT, P]) for i in range(2)]
        h_tt = [small(f"h_t{i}", [P, TX]) for i in range(2)]
        sg = small("sg", [P, 1])
        junk_a = small("junk_a", [P, NT, P])

        ps = ctx.enter_context(nc.psum_tensor("ps", [P, 8, 512], F32))

        y_dram = nc.dram_tensor("expert_rows", [2 * TX, D], F32, kind="Internal").ap()
        hn_dram = nc.dram_tensor("normed_rows", [TX, D], F32, kind="Internal").ap()
        x_rows = x.rearrange("b (t p) d -> p (b t) d", p=P)
        out_rows = out.rearrange("b (t p) d -> p (b t) d", p=P)
        w_in_rows = w_in[0].rearrange("(c p) n -> p c n", p=P)
        w_out_rows = w_out[0].rearrange("(c p) n -> p c n", p=P)
        wg_rows = exp_w_gate[0].rearrange("e (p c) f -> e p (c f)", c=KC)
        wu_rows = exp_w_up[0].rearrange("e (p c) f -> e p (c f)", c=KC)
        wd_rows = exp_w_down[0].rearrange("e (c p) d -> e c p d", p=P)

        x_in = [sem(f"x_in{i}") for i in range(3)]
        params_in = sem("params_in")
        misc_in = sem("misc_in")
        gates_in = [sem(f"gates_in{i}") for i in range(2)]
        raw_in = [sem(f"raw_in{i}") for i in range(RING)]
        slot_in = [sem(f"slot_in{i}") for i in range(SLOTS)]
        fgain_in, y_in, out_done = sem("fgain_in"), sem("y_in"), sem("out_done")
        carried = sem("carried")
        consts_ready, act_step, dve_step, pool_step = sem("consts_ready"), sem("act_step"), sem("dve_step"), sem("pool_step")
        sq_ready, xn_ready = sem("sq_ready"), sem("xn_ready")
        params_turned, cols_ready = sem("params_turned"), sem("cols_ready")
        xt_turned, xt_hi_ready, xt_lo_ready = sem("xt_turned"), sem("xt_hi_ready"), sem("xt_lo_ready")
        ms_ready, rstd_ready = sem("ms_ready"), sem("rstd_ready")
        sp_e_in, sp_e_out = sem("sp_e_in"), sem("sp_e_out")
        hi_ready, lo_ready, chunk_done, acc_out = sem("hi_ready"), sem("lo_ready"), sem("chunk_done"), sem("acc_out")
        v_turned, v_out = sem("v_turned"), sem("v_out")
        scores_done, biased = sem("scores_done"), sem("biased")
        max_ready, probs_ready, a_ready = sem("max_ready"), sem("probs_ready"), sem("a_ready")
        a_turned, a_out = sem("a_turned"), sem("a_out")
        o_done, o_sq, o_ms, o_rstd, o_out, o_turned = (sem("o_done"), sem("o_sq"), sem("o_ms"), sem("o_rstd"),
                                                       sem("o_out"), sem("o_turned"))
        mix_hi_ready, mix_lo_ready = sem("mix_hi_ready"), sem("mix_lo_ready")
        xc_ready, gates_done, e_ready, r_ready, at_ready = (sem("xc_ready"), sem("gates_done"), sem("e_ready"),
                                                            sem("r_ready"), sem("at_ready"))
        q_ready, sqrt_ready, lru_ready = sem("q_ready"), sem("sqrt_ready"), sem("lru_ready")
        gelu_in, gelu_th, gelu_ready = sem("gelu_in"), sem("gelu_th"), sem("gelu_ready")
        o_back, h_ready, h_kept, h_turned, h_t_ready, logits_done = (
            sem("o_back"), sem("h_ready"), sem("h_kept"), sem("h_turned"), sem("h_t_ready"), sem("logits_done"))
        h_sq = sem("h_sq")
        h_ms, h_rstd, hn_scaled, hn_ready, hn_out, g2b_in = (
            sem("h_ms"), sem("h_rstd"), sem("hn_scaled"), sem("hn_ready"), sem("hn_out"), sem("g2b_in"))
        ident_r_ready = sem("ident_r_ready")
        rt_max, rt_exp = sem("rt_max"), sem("rt_exp")
        members, ranks_done, sel_ready, tab_ready = (
            sem("members"), sem("ranks_done"), sem("sel_ready"), sem("tab_ready"))
        m_hi_ready, m_lo_dve, m_lo_pool = sem("m_hi_ready"), sem("m_lo_dve"), sem("m_lo_pool")
        part_used, gathered, listed, x_hi_ready, x_lo_ready = (
            sem("part_used"), sem("gathered"), sem("listed"), sem("x_hi_ready"), sem("x_lo_ready"))
        x_turned, x_even, x_odd = sem("x_turned"), sem("x_even"), sem("x_odd")
        g_copied, u_copied, g_turned, u_turned, th_ready = (
            sem("g_copied"), sem("u_copied"), sem("g_turned"), sem("u_turned"), sem("th_ready"))
        gated = sem("gated")
        h_f_ready, h_hi_ready, h_ready_e, idx_next, idx_ready = (
            sem("h_f_ready"), sem("h_hi_ready"), sem("h_ready_e"), sem("idx_next"), sem("idx_ready"))
        y_top, y_ready, scattered = sem("y_top"), sem("y_ready"), sem("scattered")
        y_half = sem("y_half")
        ysum_ready, y_sq, y_ms, y_rstd, yout_ready = (sem("ysum_ready"), sem("y_sq"), sem("y_ms"), sem("y_rstd"),
                                                      sem("yout_ready"))

        def chunk_use(n_slot, phase, i):
            before = {"qkv": 0, "lru": HEADS, "out": HEADS + N_LRU // RING}[phase]
            if n_slot == RING - 1 and phase != "qkv":
                before -= HEADS
            return before + i + 1

        def is0(i):
            return isinstance(i, int) and i == 0

        def apart(eng):
            eng.sem_inc(carried, 1)

        SQ, RSTD = 0, 4
        LAM, NLAM = 8, 9
        NMAX, L, RL, CM = 12, 16, 20, 24
        OSQ, ORS = 28, 30
        W12 = 32
        HRS, YSQ, YRS = 36, 38, 40
        HSQ = 48
        NH = 80
        LP = 84

        def qkv_src(h, j):
            return w_in_rows[:, :, ds(2 * LW + j * 1024 + h * P, P)]

        def lru_src(g, j):
            return w_in_rows[:, :, ds(j * LW + g * P, P)]

        block = ctx.enter_context(nc.Block())

        @block.sync
        def _(sp_e):
            eng = sp_e
            eng.dma_start(h_res[:, 0, :], x_rows[:, 0, :]).then_inc(x_in[0], 16)
            eng.dma_start(h_res[:, 1, :], x_rows[:, 1, :]).then_inc(x_in[1], 16)
            eng.dma_start(metan[:, :], meta_tokens).then_inc(x_in[2], 16)

            def load_qkv(h, j, first=False):
                n = 3 * h + j
                if not is0(h):
                    eng.wait_ge(chunk_done, n - QKV_RING + 1)
                eng.dma_start(raw[j][:, :, :], qkv_src(h, j)).then_inc(raw_in[j], 16)

            for j in range(3):
                load_qkv(0, j)
                if j == 0:
                    for r, src in ((ROW_G1, norm1_g[0].rearrange("(c p) -> c p", p=P)),
                                   (ROW_G2, norm2_g[0].rearrange("(c p) -> c p", p=P)),
                                   (ROW_CB, conv_b[0].rearrange("(c p) -> c p", p=P)),
                                   (ROW_CW, conv_w[0].rearrange("k (c p) -> (k c) p", p=P)),
                                   (ROW_BA, gate_a_b[0].rearrange("(c p) -> c p", p=P)),
                                   (ROW_BX, gate_x_b[0].rearrange("(c p) -> c p", p=P)),
                                   (ROW_LA, lru_a_param[0].rearrange("(c p) -> c p", p=P)),
                                   (ROW_SG, subln_g)):
                        eng.dma_start(params[r:r + src.shape[0], :], src).then_inc(params_in, 16)
            for k, lam in enumerate((lambda_q1, lambda_q2, lambda_k1, lambda_k2)):
                eng.dma_start(lam_in[:, k, :], lam.partition_broadcast(P)).then_inc(misc_in, 16)
            eng.dma_start(rw[:, :, 0:NG], router_g_w[0].rearrange("(c p) g -> p c g", p=P)).then_inc(misc_in, 16)
            eng.dma_start(rw[:, :, NG:], router_e_w[0].rearrange("(c p) g -> p c g", p=P)).then_inc(misc_in, 16)
            eng.dma_start(rb[:, 0:NG], router_g_b.partition_broadcast(P)).then_inc(misc_in, 16)
            eng.dma_start(rb[:, NG:], router_e_b.partition_broadcast(P)).then_inc(misc_in, 16)
            with eng.Fori(1, HEADS) as h:
                for j in range(3):
                    load_qkv(h, j)

            def load_lru(i):
                for s in range(RING):
                    if is0(i):
                        if s < QKV_RING:
                            eng.wait_ge(chunk_done, LRU0 - QKV_RING + s + 1)
                    else:
                        eng.wait_ge(chunk_done, LRU0 + RING * i + s - RING + 1)
                    eng.dma_start(raw[s][:, :, :], lru_src(2 * i + s // 2, s % 2)).then_inc(raw_in[s], 16)
                    if s % 2 == 0:
                        g = 2 * i + s // 2
                        if not is0(i):
                            eng.wait_ge(gates_done, g - 1)
                        eng.dma_start(g_w[:, s // 2, 0, :], gate_a_w[0, ds(g, 1)].rearrange("g i j -> i (g j)"))\
                           .then_inc(gates_in[s // 2], 16)
                        eng.dma_start(g_w[:, s // 2, 1, :], gate_x_w[0, ds(g, 1)].rearrange("g i j -> i (g j)"))\
                           .then_inc(gates_in[s // 2], 16)

            load_lru(0)
            with eng.Fori(1, LB // 2) as i:
                load_lru(i)

            def load_out(m, s):
                eng.wait_ge(chunk_done, OUT0 + m - RING + 1)
                eng.dma_start(raw[s][:, :, :], w_out_rows[:, :, ds(m * P, P)]).then_inc(raw_in[s], 16)

            def load_part(e, s):
                if s < 16:
                    rows = (wg_rows if s < 8 else wu_rows)[ds(e, 1), :, (s % 8) * PW:(s % 8 + 1) * PW]
                else:
                    rows = wd_rows[ds(e, 1), (s - 16) // 2, :, (s % 2) * PW:(s % 2 + 1) * PW]
                eng.dma_start(m_raw[s % SLOTS][:, :], rows.rearrange("e p n -> (e p) n")).then_inc(slot_in[s % SLOTS], 16)

            for s in range(RING):
                load_out(s, s)
            eng.wait_ge(mix_hi_ready, KC)
            eng.wait_ge(mix_lo_ready, KC)
            for s in range(RING):
                load_out(RING + s, s)
                load_part(0, 2 * s)
                load_part(0, 2 * s + 1)
            load_part(0, 8)
            load_part(0, 9)
            for i in range(2, N_OUT // RING):
                for s in range(RING):
                    load_out(RING * i + s, s)
            eng.wait_ge(chunk_done, OUT0 + N_OUT - RING + 1)
            load_part(0, 10)
            load_part(0, 11)
            eng.wait_ge(chunk_done, OUT0 + N_OUT - RING + 2)
            eng.dma_start(g2b[:, :], norm2_g[0].partition_broadcast(P)).then_inc(g2b_in, 16)
            hn_out_rows = hn_dram.rearrange("(t p) d -> p t d", p=P)
            for t in range(NT):
                eng.wait_ge(hn_ready, t + 1)
                eng.dma_start(hn_out_rows[:, t, :], hn_rows[:, t, :, :].rearrange("p c q -> p (c q)"))\
                   .then_inc(hn_out, 16)
            for s in range(SLOTS, PARTS):
                eng.wait_ge(part_used, s - SLOTS + 1)
                load_part(0, s)

            def load_unit(k, e):
                for s in range(PARTS):
                    eng.wait_ge(part_used, PARTS * k + s - SLOTS + 1)
                    load_part(e, s)

            with eng.Fori(1, NE) as k:
                load_unit(k, k)
            eng.wait_ge(tab_ready, 1)
            units = eng.value_load(tab_i[0:1, N_TAB:N_TAB + 1], min_val=NE, max_val=NE + MORE)
            with eng.Fori(NE, NE + MORE) as k:
                with eng.If(units > k):
                    e = eng.value_load(tab_i[0:1, ds(k - NE, 1)], min_val=0, max_val=NE - 1)
                    load_unit(k, e)
            eng.wait_ge(scattered, 16 * units)
            apart(eng)
            eng.dma_start(fgain[:, :], final_norm_g.partition_broadcast(P)).then_inc(fgain_in, 16)
            yr = y_dram.rearrange("(k t p) d -> p k t d", p=P, t=NT)
            for t in range(NT):
                eng.dma_start(y_rows[:, :, t, :], yr[:, :, t, :]).then_inc(y_in, 16)
            for t in range(NT):
                eng.wait_ge(yout_ready, t + 1)
                eng.dma_start(out_rows[:, t, :], yout[:, t, :]).then_inc(out_done, 16)
            eng.wait_ge(out_done, 16 * NT)

        @block.gpsimd
        def _(eng):
            step = Steps(eng, pool_step)
            step.done(eng.memset(ident[:, :], 0.0))
            eng.affine_select(out=ident[:, :], in_=ident[:, :], compare_op=ALU.not_equal, fill=1.0, base=0,
                              pattern=[[-1, P]], channel_multiplier=1).then_inc(consts_ready, 1)
            step.done(eng.memset(ones[:, :], 1.0))
            step.mark(eng.affine_select(out=ltri[:, :], in_=ones[:, :], compare_op=ALU.is_gt, fill=0.0, base=0,
                                        pattern=[[1, P]], channel_multiplier=-1))
            step.mark(eng.iota(slot_no[:, :], [[1, C]], base=0, channel_multiplier=0,
                               allow_small_or_imprecise_dtypes=True))
            step.mark(eng.iota(unit_no[:, :], [[1, N_TAB]], base=NE, channel_multiplier=0,
                               allow_small_or_imprecise_dtypes=True))
            step.mark(eng.iota(expert_no[:, :], [[0, TX // C - 1], [1, NE]], base=0, channel_multiplier=0,
                               allow_small_or_imprecise_dtypes=True))
            step.mark(eng.iota(first_no[:, :], [[C, TX // C - 1], [0, NE]], base=C - int(BIG), channel_multiplier=0,
                               allow_small_or_imprecise_dtypes=True))
            step.done(eng.memset(pair[:, :], 0.0))
            step.done(eng.affine_select(out=pair[:, :], in_=pair[:, :], compare_op=ALU.not_equal, fill=1.0, base=0,
                                        pattern=[[-1, C]], channel_multiplier=1))
            step.mark(eng.affine_select(out=pair[:, :], in_=pair[:, :], compare_op=ALU.not_equal, fill=1.0, base=-C,
                                        pattern=[[-1, C]], channel_multiplier=1))
            step.mark(eng.memset(stat[:, NH:NH + 4], -0.5))
            for t, c0, w in ((0, S0, K0), (1, S1, K1)):
                b = bias[:, c0:c0 + w]
                step.done(eng.iota(b, [[1, w]], base=-(NM + P * t), channel_multiplier=-1,
                                   allow_small_or_imprecise_dtypes=True))
            step.done(eng.tensor_scalar(s_sb[:, 0, :], bias[:, :], 0.0, -2.0, ALU.max, ALU.mult))
            step.done(eng.tensor_tensor(bias[:, :], bias[:, :], s_sb[:, 0, :], ALU.add))
            for t, c0 in ((0, S0), (1, S1)):
                late = c0 + NM + P * t + CHUNK
                step.done(eng.memset(bias[0:CHUNK, late:late + CHUNK], -1e30))
            step.mark(eng.memset(u_pad[:, 0:CONVW - 1], 0.0))
            step.mark(eng.iota(stat[:, 86:88], [[P, NT]], base=0, channel_multiplier=1,
                               allow_small_or_imprecise_dtypes=True))
            step.mark(eng.iota(stat[:, 88:92], [[-1, 4]], base=4, channel_multiplier=0,
                               allow_small_or_imprecise_dtypes=True))
            step.wait()
            eng.memset(stat[:, 92:93], 0.0).then_inc(consts_ready, 1)
            eng.wait_ge(ms_ready, 1)
            eng.tensor_tensor(stat[:, RSTD:RSTD + 2], stat[:, RSTD:RSTD + 2], stat[:, NH:NH + 2], ALU.pow)\
               .then_inc(rstd_ready, 1)
            eng.tensor_tensor(stat[0:NM, RSTD + 2:RSTD + 3], stat[0:NM, RSTD + 2:RSTD + 3], stat[0:NM, NH:NH + 1],
                              ALU.pow).then_inc(rstd_ready, 1)

            def o_power(h):
                eng.wait_ge(o_ms, h + 1)
                eng.tensor_tensor(stat[:, ORS:ORS + NT], stat[:, ORS:ORS + NT], stat[:, NH:NH + NT], ALU.pow)\
                   .then_inc(o_rstd, 1)

            with eng.Fori(0, HEADS) as h:
                o_power(h)

            def lru(g):
                yg = yg_t[:, :]
                eng.wait_ge(acc_out, LRU0 + 2 * g + 2)
                at_least(eng, lru_ready, g)
                step.done(eng.tensor_tensor(gl1[:, :], yg, yg, ALU.mult))
                apart(eng)
                step.done(eng.tensor_scalar(gl1[:, :], gl1[:, :], 0.044715, 1.0, ALU.mult, ALU.add))
                eng.tensor_tensor(gl1[:, :], gl1[:, :], yg, ALU.mult).then_inc(gelu_in, 1)
                eng.wait_ge(gelu_th, g + 1)
                apart(eng)
                step.done(eng.tensor_scalar(gl2[:, :], gl2[:, :], 1.0, 0.5, ALU.add, ALU.mult))
                eng.tensor_tensor(gl1[:, :], gl2[:, :], yg, ALU.mult).then_inc(gelu_ready, 1)

            lru(0)
            looped(eng, step, 1, LB - 1, lru, 3)

            def keep(m, b):
                eng.wait_ge(h_ready, m + 1)
                eng.tensor_copy(h_res[:, :, ds(m * P, P)], h_s[b][:, :, :]).then_inc(h_kept, 1)

            with eng.Fori(0, N_OUT // 2) as i:
                for b in range(2):
                    keep(2 * i + b, b)
            eng.wait_ge(h_ms, 1)
            eng.tensor_tensor(stat[:, HRS:HRS + NT], stat[:, HRS:HRS + NT], stat[:, NH:NH + NT], ALU.pow)\
               .then_inc(h_rstd, 1)

            eng.wait_ge(g2b_in, 16)
            for t in range(NT):
                eng.wait_ge(hn_scaled, t + 1)
                eng.tensor_tensor(hn_rows[:, t, :, :], hn_rows[:, t, :, :],
                                  g2b[:, :].rearrange("p (q c) -> p c q", c=KC), ALU.mult).then_inc(hn_ready, 1)

            def gather(k):
                eng.wait_ge(idx_next, k + 1)
                apart(eng)
                eng.indirect_dma_start(out=x_g[:, :], out_offset=None, in_=hn_dram[:, :],
                                       in_offset=bass.IndirectOffsetOnAxis(ap=idx_g[:, 0:1], axis=0),
                                       bounds_check=TX - 1, oob_is_err=False).then_inc(gathered, 16)

            def scatter(k):
                eng.wait_ge(idx_ready, k)
                apart(eng)
                eng.wait_ge(y_ready, k)
                apart(eng)
                eng.indirect_dma_start(out=y_dram[:, :], out_offset=bass.IndirectOffsetOnAxis(ap=idx_i[:, 0:1], axis=0),
                                       in_=y_e[:, :], in_offset=None, bounds_check=2 * TX - 1, oob_is_err=False)\
                   .then_inc(scattered, 16)

            def m_low(k, s):
                eng.wait_ge(m_hi_ready, PARTS * k + s + 1)
                n = s % SLOTS
                eng.tensor_tensor(m_lo[n][:, :], m_raw[n][:, :], m_hi[n][:, :].bitcast(F32), ALU.subtract)\
                   .then_inc(m_lo_pool, 1)

            def unit(k):
                m_low(k, 2)
                m_low(k, 6)
                gather(k + 1)
                m_low(k, 10)
                if not is0(k):
                    scatter(k)
                m_low(k, 14)
                m_low(k, 18)
                m_low(k, 22)

            eng.wait_ge(hn_out, 16 * NT)
            gather(0)
            unit(0)
            with eng.Fori(1, NE) as k:
                unit(k)
            eng.wait_ge(tab_ready, 1)
            units = eng.value_load(tab_i[0:1, N_TAB:N_TAB + 1], min_val=NE, max_val=NE + MORE)
            with eng.Fori(NE, NE + MORE) as k:
                with eng.If(units > k):
                    unit(k)
            scatter(units)
            eng.wait_ge(y_ms, 1)
            eng.tensor_tensor(stat[:, YRS:YRS + NT], stat[:, YRS:YRS + NT], stat[:, NH:NH + NT], ALU.pow)\
               .then_inc(y_rstd, 1)

        @block.scalar
        def _(eng):
            step = Steps(eng, act_step)
            for t in range(NT):
                eng.wait_ge(x_in[t], 16)
                step.mark(eng.activation(junk[:, :], h_res[:, t, :], ACT.Square, accum_out=stat[:, SQ + t:SQ + t + 1]))
                step.wait()
            eng.wait_ge(x_in[2], 16)
            eng.activation(junk[0:NM, :], metan[:, :], ACT.Square, accum_out=stat[0:NM, SQ + 2:SQ + 3])\
               .then_inc(sq_ready, 1)

            def hi(n, s, use):
                eng.wait_ge(raw_in[s], 16 * use)
                eng.activation(w_hi[s][:, :, :], raw[s][:, :, :], ACT.Copy).then_inc(hi_ready, 1)

            hi(0, 0, 1)
            hi(1, 1, 1)
            eng.wait_ge(cols_ready, 1)
            for c in range(KC):
                eng.wait_ge(xt_turned, c + 1)
                eng.activation(xt_hi[:, c, :], ps[:, 3 + c % 4, 0:T], ACT.Copy,
                               scale=col[:, ROW_G1 + c:ROW_G1 + c + 1]).then_inc(xt_hi_ready, 1)
            eng.wait_ge(sp_e_in, 1)
            eng.activation(sp[:, 1, :], sp[:, 0, :], ACT.Exp).then_inc(sp_e_out, 1)
            eng.activation(stat[:, LP:LP + 2], stat[:, LP:LP + 2], ACT.Exp).then_inc(sp_e_out, 1)

            def o_squares(h):
                eng.wait_ge(o_done, h + 1)
                for t in range(NT):
                    ins = eng.activation(junk_a[:, t, :], ps[:, 7, TX + t * P:TX + (t + 1) * P], ACT.Square,
                                         accum_out=stat[:, OSQ + t:OSQ + t + 1])
                    ins.then_inc(o_sq, 1)

            def mix_high(h):
                eng.wait_ge(o_turned, h + 1)
                eng.activation(mix_hi[:, ds(LB + h, 1), :].rearrange("p a t -> p (a t)"), ps[:, 6, 0:TX], ACT.Copy,
                               scale=sg[:, 0:1]).then_inc(mix_hi_ready, 1)

            def probs(h):
                for m in range(2):
                    for t, c0, w in ((0, S0, K0), (1, S1, K1)):
                        eng.wait_ge(max_ready, 2 * h + t + 1)
                        k = 2 * m + t
                        eng.activation(s_sb[:, m, c0:c0 + w], s_sb[:, m, c0:c0 + w], ACT.Exp,
                                       bias=stat[:, NMAX + k:NMAX + k + 1],
                                       accum_out=stat[:, L + k:L + k + 1]).then_inc(probs_ready, 1)

            def qkv(h):
                n = 3 * h
                hi(n + 2, 2, h + 1)
                eng.wait_ge(chunk_done, n + 1)
                eng.activation(q_t[:, :], ps[:, 0, 0:TX], ACT.Copy).then_inc(acc_out, 1)
                if not is0(h):
                    o_squares(h - 1)
                eng.wait_ge(chunk_done, n + 2)
                eng.activation(k_t[:, :], ps[:, 1, 0:T], ACT.Copy).then_inc(acc_out, 1)
                hi(n + 3, 0, h + 2)
                probs(h)
                if not is0(h):
                    mix_high(h - 1)
                hi(n + 4, 1, h + 2)
                eng.wait_ge(chunk_done, n + 3)
                eng.activation(v_t[:, :], ps[:, 2, 0:T], ACT.Copy).then_inc(acc_out, 1)

            qkv(0)
            with eng.Fori(1, HEADS) as h:
                qkv(h)

            def lru(i, b):
                g = 2 * i + b
                n = LRU0 + 2 * g
                s = 2 * b
                eng.wait_ge(chunk_done, n + 1)
                at_least(eng, xc_ready, g)
                eng.activation(u_pad[:, CONVW - 1:], ps[:, 0, 0:T], ACT.Copy).then_inc(acc_out, 1)
                if is0(i) and b == 0:
                    o_squares(HEADS - 1)
                for j in (2, 3):
                    if b == 0:
                        hi(n + j, s + j, chunk_use(s + j, "lru", i))
                    elif isinstance(i, int) and i == LB // 2 - 1:
                        hi(n + j, j - 2, chunk_use(j - 2, "out", 0))
                    else:
                        hi(n + j, j - 2, chunk_use(j - 2, "lru", i + 1))
                    if is0(i) and b == 0 and j == 2:
                        mix_high(HEADS - 1)
                eng.wait_ge(gates_done, g + 1)
                at_least(eng, r_ready, g)
                eng.activation(e_ri[:, 0, :], ps[:, 3, 0:T], ACT.Exp, bias=negb[:, ds(g, 1)], scale=-1.0)\
                   .then_inc(e_ready, 1)
                eng.activation(e_ri[:, 1, :], ps[:, 4, 0:T], ACT.Exp, bias=negb[:, ds(LB + g, 1)], scale=-1.0)\
                   .then_inc(e_ready, 1)
                eng.wait_ge(chunk_done, n + 2)
                at_least(eng, gelu_ready, g)
                eng.activation(yg_t[:, :], ps[:, 1, 0:TX], ACT.Copy).then_inc(acc_out, 1)
                eng.wait_ge(r_ready, g + 1)
                at_least(eng, lru_ready, g)
                eng.activation(a_t[:, :], r_ri[:, 0, :], ACT.Exp, scale=sp[:, 6, ds(g, 1)]).then_inc(at_ready, 1)
                eng.activation(tg[:, :], r_ri[:, 0, :], ACT.Tanh, scale=sp[:, 7, ds(g, 1)]).then_inc(at_ready, 1)
                eng.wait_ge(gelu_in, g + 1)
                eng.activation(gl2[:, :], gl1[:, :], ACT.Tanh, scale=0.7978845608028654).then_inc(gelu_th, 1)
                eng.wait_ge(q_ready, g + 1)
                eng.activation(lr3[:, :], lr2[:, :], ACT.Sqrt).then_inc(sqrt_ready, 1)
                eng.wait_ge(lru_ready, g + 1)
                eng.activation(mix_hi[:, ds(g, 1), :].rearrange("p a t -> p (a t)"), lru_f[:, :], ACT.Copy)\
                   .then_inc(mix_hi_ready, 1)

            lru(0, 0)
            lru(0, 1)
            with eng.Fori(1, LB // 2 - 1) as i:
                lru(i, 0)
                lru(i, 1)
            lru(LB // 2 - 1, 0)
            lru(LB // 2 - 1, 1)

            def h_squares(m, b):
                eng.wait_ge(h_ready, m + 1)
                for t in range(NT):
                    eng.activation(ps[:, 7, (NT * b + t) * P:(NT * b + t + 1) * P], h_s[b][:, t, :], ACT.Square,
                                   accum_out=stat[:, ds(HSQ + t * N_OUT + m, 1)]).then_inc(h_sq, 1)

            def project(i, s, last=False):
                m = RING * i + s
                n = OUT0 + m
                eng.wait_ge(chunk_done, n + 1)
                at_least(eng, o_back, m - 1)
                eng.activation(o_t[s % 2][:, :], ps[:, s % 2, 0:TX], ACT.Copy).then_inc(acc_out, 1)
                if s < 2:
                    hi(n + 2, s + 2, chunk_use(s + 2, "out", i))
                elif not last:
                    hi(n + 2, s - 2, chunk_use(s - 2, "out", i + 1))
                if not (is0(i) and s == 0):
                    h_squares(m - 1, (s - 1) % 2)

            for s in range(RING):
                project(0, s)
            with eng.Fori(1, N_OUT // RING - 1) as i:
                for s in range(RING):
                    project(i, s)
            for s in range(RING):
                project(N_OUT // RING - 1, s, last=True)
            h_squares(N_OUT - 1, 1)
            eng.wait_ge(h_rstd, 1)
            eng.wait_ge(h_kept, N_OUT)
            for t in range(NT):
                eng.activation(hn_rows[:, t, :, :], h_res[:, t, :].rearrange("p (q c) -> p c q", c=KC), ACT.Copy,
                               scale=stat[:, HRS + t:HRS + t + 1]).then_inc(hn_scaled, 1)
            eng.activation(ident_r[:, :], ident[:, :], ACT.Copy).then_inc(ident_r_ready, 1)
            eng.wait_ge(rt_max, 1)
            eng.activation(rt[:, 2, :, 0:NG], rt[:, 1, :, 0:NG], ACT.Exp).then_inc(rt_exp, 1)
            eng.wait_ge(rt_max, 2)
            eng.activation(rt[:, 10, :, 1:2], rt[:, 10, :, 0:1], ACT.Exp).then_inc(rt_exp, 1)

            def m_high(k, *parts):
                for s in parts:
                    eng.wait_ge(slot_in[s % SLOTS], 16 * (PARTS // SLOTS * k + s // SLOTS + 1))
                    eng.activation(m_hi[s % SLOTS][:, :], m_raw[s % SLOTS][:, :], ACT.Copy).then_inc(m_hi_ready, 1)

            def y_copy(k, before=None):
                eng.wait_ge(part_used, PARTS * k)
                if not (isinstance(k, int) and k == 1):
                    eng.wait_ge(scattered, 16 * (k - 1 if before is None else before))
                eng.activation(y_e[:, :].rearrange("p (b d) -> p b d", b=4), ps[0:C, 3:7, :], ACT.Copy)\
                   .then_inc(y_top, 1)

            def x_high(k):
                eng.wait_ge(gathered, 16 * (k + 1))
                at_least(eng, x_turned, 4 * k)
                eng.activation(x_s[0:C, :], x_g[:, :], ACT.Copy).then_inc(x_hi_ready, 1)

            def x_out(k, j):
                eng.wait_ge(x_turned, 4 * k + j + 1)
                eng.activation(x_hl[:, 4 * j:4 * j + 4, :, :].rearrange("p c h s -> p (c h s)"), ps[:, 7, :], ACT.Copy)\
                   .then_inc(x_even, 1)

            def unit(k):
                m_high(k, *range(0, 8))
                if not is0(k):
                    y_copy(k)
                m_high(k, *range(8, 13))
                x_high(k + 1)
                m_high(k, 13)
                eng.wait_ge(part_used, PARTS * k + 8)
                eng.activation(gu_sb[:, 0, :], ps[:, 0, :], ACT.Copy).then_inc(g_copied, 1)
                m_high(k, *range(14, 18))
                eng.wait_ge(g_turned, k + 1)
                eng.activation(th[:, :, :].rearrange("p f c -> p (f c)"), ps[:, 2, 0:FC * C], ACT.Tanh, scale=0.5)\
                   .then_inc(th_ready, 1)
                m_high(k, *range(18, 22))
                eng.wait_ge(part_used, PARTS * k + 16)
                eng.activation(gu_sb[:, 1, :], ps[:, 1, :], ACT.Copy).then_inc(u_copied, 1)
                x_out(k + 1, 0)
                eng.wait_ge(h_f_ready, k + 1)
                eng.activation(h_hl[:, :, 0, :], h_f[:, :, :], ACT.Copy).then_inc(h_hi_ready, 1)
                x_out(k + 1, 2)
                m_high(k, 22, 23)

            x_high(0)
            x_out(0, 0)
            x_out(0, 2)
            unit(0)
            with eng.Fori(1, NE) as k:
                unit(k)
            eng.wait_ge(tab_ready, 1)
            units = eng.value_load(tab_i[0:1, N_TAB:N_TAB + 1], min_val=NE, max_val=NE + MORE)
            with eng.Fori(NE, NE + MORE) as k:
                with eng.If(units > k):
                    unit(k)
            y_copy(units, eng.value_load(tab_i[0:1, N_TAB + 1:N_TAB + 2], min_val=NE - 1, max_val=NE + MORE - 1))
            for t in range(NT):
                eng.wait_ge(ysum_ready, t + 1)
                eng.activation(yout[:, t, :], ysum[:, t, :], ACT.Square,
                               accum_out=stat[:, YSQ + t:YSQ + t + 1]).then_inc(y_sq, 1)

        @block.vector
        def _(eng):
            step = Steps(eng, dve_step)
            eng.wait_ge(sq_ready, 1)
            eng.wait_ge(act_step, 2)
            step.mark(eng.tensor_scalar(stat[:, RSTD:RSTD + 2], stat[:, SQ:SQ + 2], 1.0 / D, EPS, ALU.mult, ALU.add))
            step.mark(eng.tensor_scalar(stat[0:NM, RSTD + 2:RSTD + 3], stat[0:NM, SQ + 2:SQ + 3], 1.0 / D, EPS,
                                        ALU.mult, ALU.add))
            step.wait()
            eng.memset(stat[:, 94:95], 0.0).then_inc(ms_ready, 1)
            eng.wait_ge(params_turned, 1)
            eng.tensor_copy(col[:, :], ps[:, 7, 0:N_ROWS]).then_inc(cols_ready, 1)
            eng.wait_ge(rstd_ready, 2)
            eng.tensor_scalar(metan[:, :], metan[:, :], stat[0:NM, RSTD + 2:RSTD + 3], None, ALU.mult)\
               .then_inc(xn_ready, 1)
            for t in range(NT):
                eng.tensor_scalar(xn[:, t, :], h_res[:, t, :], stat[:, RSTD + t:RSTD + t + 1], None, ALU.mult)\
                   .then_inc(xn_ready, 1)

            def lo(n, s):
                eng.wait_ge(hi_ready, n + 1)
                eng.tensor_tensor(w_lo[s][:, :, :], raw[s][:, :, :], w_hi[s][:, :, :].bitcast(F32), ALU.subtract)\
                   .then_inc(lo_ready, 1)

            lo(0, 0)
            for c in range(KC):
                eng.wait_ge(xt_hi_ready, c + 1)
                eng.wait_ge(cols_ready, 1)
                eng.scalar_tensor_tensor(out=xt_lo[:, c, :], in0=ps[:, 3 + c % 4, 0:T],
                                         scalar=col[:, ROW_G1 + c:ROW_G1 + c + 1],
                                         in1=xt_hi[:, c, :].bitcast(F32), op0=ALU.mult, op1=ALU.subtract)\
                   .then_inc(xt_lo_ready, 1)
            lo(1, 1)
            p = col[:, ROW_LA:ROW_LA + LB]
            step.done(eng.tensor_scalar(sp[:, 5, :], p, -1.0, None, ALU.mult))
            step.done(eng.tensor_tensor(sp[:, 0, :], p, sp[:, 5, :], ALU.min))
            eng.wait_ge(misc_in, 16 * 8)
            step.done(eng.tensor_tensor(lam_in[:, 0:2, :], lam_in[:, 0:2, :], lam_in[:, 2:4, :], ALU.mult))
            step.done(eng.tensor_reduce(stat[:, LP:LP + 2], lam_in[:, 0:2, :], AX.X, ALU.add))
            eng.tensor_scalar(sg[:, 0:1], col[:, ROW_SG:ROW_SG + 1], 1.0 - LAM_INIT, None, ALU.mult).then_inc(sp_e_in, 1)
            step.done(eng.tensor_scalar(negb[:, 0:2 * LB], col[:, ROW_BA:ROW_BA + 2 * LB], -1.0, None, ALU.mult))
            eng.wait_ge(sp_e_out, 2)
            step.done(eng.tensor_tensor(stat[:, LAM:LAM + 1], stat[:, LP + 1:LP + 2], stat[:, LP:LP + 1], ALU.subtract))
            step.done(eng.tensor_scalar(stat[:, NLAM:NLAM + 1], stat[:, LAM:LAM + 1], -LAM_INIT, None, ALU.add))
            step.done(eng.tensor_scalar(sp[:, 2, :], sp[:, 1, :], 2.0, None, ALU.add))
            step.done(eng.reciprocal(sp[:, 3, :], sp[:, 2, :]))
            step.done(eng.tensor_tensor(sp[:, 2, :], sp[:, 1, :], sp[:, 3, :], ALU.mult))
            step.done(eng.tensor_tensor(sp[:, 3, :], sp[:, 2, :], sp[:, 2, :], ALU.mult))
            step.done(eng.tensor_scalar(sp[:, 4, :], sp[:, 3, :], 1.0 / 17, 1.0 / 15, ALU.mult, ALU.add))
            for k in (13, 11, 9, 7, 5, 3, 1):
                step.done(eng.tensor_tensor(sp[:, 4, :], sp[:, 4, :], sp[:, 3, :], ALU.mult))
                step.done(eng.tensor_scalar(sp[:, 4, :], sp[:, 4, :], 1.0 / k, None, ALU.add))
            step.done(eng.tensor_tensor(sp[:, 4, :], sp[:, 4, :], sp[:, 2, :], ALU.mult))
            step.done(eng.tensor_scalar(sp[:, 5, :], sp[:, 5, :], 0.0, None, ALU.max))
            step.done(eng.scalar_tensor_tensor(out=sp[:, 5, :], in0=sp[:, 4, :], scalar=2.0, in1=sp[:, 5, :],
                                               op0=ALU.mult, op1=ALU.add))
            step.done(eng.tensor_scalar(sp[:, 6, :], sp[:, 5, :], -8.0, None, ALU.mult))
            step.done(eng.tensor_scalar(sp[:, 7, :], sp[:, 5, :], 8.0, None, ALU.mult))
            eng.wait_ge(consts_ready, 2)

            def v_rows(h):
                eng.wait_ge(v_turned, h + 1)
                eng.tensor_copy(v_tm[:, :, :], ps[:, 6, 0:TX].rearrange("p (t d) -> p t d", t=NT)).then_inc(v_out, 1)
                eng.tensor_copy(v_meta[:, :], ps[0:NM, 6, TX:TX + P]).then_inc(v_out, 1)

            def a_turn(h):
                eng.wait_ge(a_turned, h + 1)
                eng.tensor_copy(at_x[:, 0, :], ps[:, 5, 0:TX]).then_inc(a_out, 1)
                eng.tensor_copy(at_x[:, 1, P:TX], ps[:, 5, TX + P:2 * TX]).then_inc(a_out, 1)
                eng.tensor_copy(at_m[:, :], ps[0:NM, 7, 0:TX]).then_inc(a_out, 1)

            def o_norm(h):
                eng.wait_ge(o_sq, 2 * h + 2)
                eng.tensor_scalar(stat[:, ORS:ORS + NT], stat[:, OSQ:OSQ + NT], 1.0 / P, EPS, ALU.mult, ALU.add)\
                   .then_inc(o_ms, 1)
                eng.wait_ge(o_rstd, h + 1)
                eng.tensor_tensor(o_sb[:, :, :], ps[:, 7, TX:2 * TX].rearrange("p (t d) -> p t d", t=NT),
                                  stat[:, ORS:ORS + NT].unsqueeze(2).to_broadcast([P, NT, P]), ALU.mult)\
                   .then_inc(o_out, 1)

            def softmax_in(h):
                step.done(eng.tensor_scalar(bias[:, :], bias[:, :], 0.5, None, ALU.mult))
                eng.wait_ge(scores_done, h + 1)
                eng.scalar_tensor_tensor(out=s_sb[:, :, :], in0=ps[:, 3:5, 0:SW], scalar=DH ** -0.5,
                                         in1=bias[:, :].unsqueeze(1).to_broadcast([P, 2, SW]), op0=ALU.mult,
                                         op1=ALU.add).then_inc(biased, 1)
                eng.wait_ge(biased, h + 1)
                for t, c0, w in ((0, S0, K0), (1, S1, K1)):
                    eng.tensor_reduce(stat[:, NMAX + t:NMAX + t + 3:2], s_sb[:, :, c0:c0 + w], AX.X, ALU.max,
                                      negate=True).then_inc(max_ready, 1)

            def softmax_out(h):
                eng.wait_ge(probs_ready, 4 * h + 4)
                step.done(eng.reciprocal(stat[:, RL:RL + 4], stat[:, L:L + 4]))
                step.done(eng.tensor_scalar(stat[:, CM:CM + 2], stat[:, RL + 2:RL + 4], stat[:, NLAM:NLAM + 1], None,
                                            ALU.mult))
                for t, c0, w in ((0, S0, K0), (1, S1, K1)):
                    step.mark(eng.tensor_scalar(a_sb[:, c0:c0 + w], s_sb[:, 0, c0:c0 + w],
                                                stat[:, RL + t:RL + t + 1], None, ALU.mult))
                step.wait()
                for t, c0, w in ((0, S0, K0), (1, S1, K1)):
                    eng.scalar_tensor_tensor(out=a_sb[:, c0:c0 + w], in0=s_sb[:, 1, c0:c0 + w],
                                             scalar=stat[:, CM + t:CM + t + 1], in1=a_sb[:, c0:c0 + w],
                                             op0=ALU.mult, op1=ALU.add).then_inc(a_ready, 1)

            def mix_low(h):
                eng.wait_ge(mix_hi_ready, h + 1)
                eng.scalar_tensor_tensor(out=mix_lo[:, ds(LB + h, 1), :].rearrange("p a t -> p (a t)"),
                                         in0=ps[:, 6, 0:TX], scalar=sg[:, 0:1],
                                         in1=mix_hi[:, ds(LB + h, 1), :].rearrange("p a t -> p (a t)").bitcast(F32),
                                         op0=ALU.mult, op1=ALU.subtract).then_inc(mix_lo_ready, 1)

            def qkv(h):
                n = 3 * h
                if not is0(h):
                    v_rows(h - 1)
                lo(n + 2, 2)
                if not is0(h):
                    a_turn(h - 1)
                    o_norm(h - 1)
                lo(n + 3, 0)
                softmax_in(h)
                if not is0(h):
                    mix_low(h - 1)
                lo(n + 4, 1)
                softmax_out(h)

            qkv(0)
            looped(eng, step, 1, HEADS - 1, qkv, 5)

            def lru(i, b):
                g = 2 * i + b
                n = LRU0 + 2 * g
                s = 2 * b
                if is0(i) and b == 0:
                    v_rows(HEADS - 1)
                eng.wait_ge(acc_out, n + 1)
                for k in range(CONVW):
                    src = u_pad[:, CONVW - 1 - k:CONVW - 1 - k + T]
                    tap = col[:, ds(ROW_CW + k * LB + g, 1)]
                    if k == 0:
                        step.done(eng.tensor_scalar(xc[:, :], src, tap, col[:, ds(ROW_CB + g, 1)], ALU.mult, ALU.add))
                    else:
                        ins = eng.scalar_tensor_tensor(out=xc[:, :], in0=src, scalar=tap, in1=xc[:, :], op0=ALU.mult,
                                                       op1=ALU.add)
                        if k < CONVW - 1:
                            step.done(ins)
                ins.then_inc(xc_ready, 1)
                if is0(i) and b == 0:
                    a_turn(HEADS - 1)
                    o_norm(HEADS - 1)
                lo(n + 2, (s + 2) % RING)
                if is0(i) and b == 0:
                    mix_low(HEADS - 1)
                eng.wait_ge(e_ready, 2 * g + 2)
                at_least(eng, at_ready, 2 * g)
                step.done(eng.tensor_scalar(r_ri[:, :, :], e_ri[:, :, :], 1.0, None, ALU.add))
                eng.reciprocal(r_ri[:, :, :], r_ri[:, :, :]).then_inc(r_ready, 1)
                lo(n + 3, (s + 3) % RING)
                eng.wait_ge(r_ready, g + 1)
                step.done(eng.tensor_tensor(lr1[:, :], r_ri[:, 1, :], xc[:, :], ALU.mult))
                eng.wait_ge(at_ready, 2 * g + 2)
                step.done(eng.tensor_scalar(lr2[:, :], tg[:, :], 1.0, None, ALU.add))
                step.done(eng.reciprocal(lr2[:, :], lr2[:, :]))
                eng.scalar_tensor_tensor(out=lr2[:, :], in0=tg[:, :], scalar=2.0, in1=lr2[:, :], op0=ALU.mult,
                                         op1=ALU.mult).then_inc(q_ready, 1)
                eng.wait_ge(sqrt_ready, g + 1)
                step.done(eng.tensor_tensor(lr3[:, :], lr3[:, :], lr1[:, :], ALU.mult))
                step.done(eng.tensor_tensor_scan(hs_t[:, :], a_t[:, :], lr3[:, :], 0.0, ALU.mult, ALU.add))
                eng.wait_ge(gelu_ready, g + 1)
                eng.tensor_tensor(lru_f[:, :], hs_t[:, NM:T], gl1[:, :], ALU.mult).then_inc(lru_ready, 1)
                eng.wait_ge(mix_hi_ready, HEADS + g + 1)
                eng.tensor_tensor(mix_lo[:, ds(g, 1), :].rearrange("p a t -> p (a t)"), lru_f[:, :],
                                  mix_hi[:, ds(g, 1), :].rearrange("p a t -> p (a t)").bitcast(F32),
                                  ALU.subtract).then_inc(mix_lo_ready, 1)

            lru(0, 0)
            lru(0, 1)

            def lru2(i):
                lru(i, 0)
                lru(i, 1)

            looped(eng, step, 1, LB // 2 - 1, lru2, 18)

            def residual(m, b):
                eng.wait_ge(o_back, m + 1)
                at_least(eng, h_kept, m - 1)
                at_least(eng, h_sq, 2 * (m - 1))
                at_least(eng, h_turned, m - 1)
                eng.tensor_tensor(h_s[b][:, :, :], ps[:, 3, 0:TX].rearrange("p (t d) -> p t d", t=NT),
                                  h_res[:, :, ds(m * P, P)], ALU.add).then_inc(h_ready, 1)
                eng.wait_ge(h_turned, m + 1)
                at_least(eng, logits_done, m - 1)
                eng.tensor_scalar(h_tt[b][:, :], ps[:, 4, 0:TX], col[:, ds(ROW_G2 + m, 1)], None, ALU.mult)\
                   .then_inc(h_t_ready, 1)

            def project(i, s, last=False):
                m = RING * i + s
                if not (is0(i) and s == 0):
                    residual(m - 1, (s - 1) % 2)
                if not (last and s >= 2):
                    lo(OUT0 + m + 2, (s + 2) % RING)

            for s in range(RING):
                project(0, s)
            with eng.Fori(1, N_OUT // RING - 1) as i:
                for s in range(RING):
                    project(i, s)
            for s in range(RING):
                project(N_OUT // RING - 1, s, last=True)
            residual(N_OUT - 1, 1)

            eng.wait_ge(h_sq, 2 * N_OUT)
            step.done(eng.tensor_reduce(stat[:, HRS:HRS + NT],
                                        stat[:, HSQ:HSQ + NT * N_OUT].rearrange("p (t m) -> p t m", t=NT), AX.X, ALU.add))
            eng.tensor_scalar(stat[:, HRS:HRS + NT], stat[:, HRS:HRS + NT], 1.0 / D, EPS, ALU.mult, ALU.add)\
               .then_inc(h_ms, 1)
            eng.wait_ge(h_rstd, 1)
            eng.wait_ge(logits_done, N_OUT)
            lg = rt[:, 0, :, 0:NG]
            le = rt[:, 3, :, :]
            for t in range(NT):
                step.mark(eng.scalar_tensor_tensor(out=rt[:, 0, t, 0:NG], in0=ps[:, 5 + t, 0:NG],
                                                   scalar=stat[:, HRS + t:HRS + t + 1], in1=rb[:, 0:NG],
                                                   op0=ALU.mult, op1=ALU.add))
                step.mark(eng.scalar_tensor_tensor(out=rt[:, 3, t, :], in0=ps[:, 5 + t, NG:NG + NE],
                                                   scalar=stat[:, HRS + t:HRS + t + 1], in1=rb[:, NG:NG + NE],
                                                   op0=ALU.mult, op1=ALU.add))
            step.wait()
            prio = stat[:, 88:92].unsqueeze(1).to_broadcast([P, NT, 4])

            def first_max(v, m, hot, work):
                step.done(eng.tensor_reduce(m, v, AX.X, ALU.max))
                step.done(eng.tensor_tensor(work, v, m.to_broadcast([P, NT, 4]), ALU.is_equal))
                step.done(eng.tensor_tensor(work, work, prio, ALU.mult))
                step.done(eng.tensor_reduce(rt[:, 17, :, 0:1], work, AX.X, ALU.max))
                step.done(eng.tensor_tensor(hot, prio, rt[:, 17, :, 0:1].to_broadcast([P, NT, 4]), ALU.is_equal))

            gmax = rt[:, 4, :, 0:1]
            ghot = rt[:, 5, :, 0:NG]
            first_max(lg, gmax, ghot, rt[:, 6, :, 0:NG])
            eng.tensor_tensor(rt[:, 1, :, 0:NG], lg, gmax.to_broadcast([P, NT, NG]), ALU.subtract).then_inc(rt_max, 1)
            for t in range(NT):
                step.mark(eng.tensor_tensor(rt[:, 7, t, :].rearrange("p (g j) -> p g j", g=NG),
                                            rt[:, 3, t, :].rearrange("p (g j) -> p g j", g=NG),
                                            rt[:, 5, t, 0:NG].unsqueeze(2).to_broadcast([P, NG, EPG]), ALU.mult))
            step.wait()
            lin = rt[:, 8, :, 0:EPG]
            for t in range(NT):
                step.mark(eng.tensor_reduce(rt[:, 8, t, 0:EPG], rt[:, 7, t, :].rearrange("p (g j) -> p j g", g=NG),
                                            AX.X, ALU.add))
            step.wait()
            hot1, hot2 = rt[:, 9, :, 0:EPG], rt[:, 11, :, 0:EPG]
            m1, m2 = rt[:, 12, :, 0:1], rt[:, 12, :, 1:2]
            first_max(lin, m1, hot1, rt[:, 6, :, 0:EPG])
            step.done(eng.scalar_tensor_tensor(out=rt[:, 13, :, 0:EPG], in0=hot1, scalar=-1e30, in1=lin,
                                               op0=ALU.mult, op1=ALU.add))
            first_max(rt[:, 13, :, 0:EPG], m2, hot2, rt[:, 6, :, 0:EPG])
            eng.tensor_tensor(rt[:, 10, :, 0:1], m2, m1, ALU.subtract).then_inc(rt_max, 1)
            for t in range(NT):
                for k, hot in ((14, 9), (15, 11)):
                    step.mark(eng.tensor_tensor(rt[:, k, t, :].rearrange("p (g j) -> p g j", g=NG),
                                                rt[:, 5, t, 0:NG].unsqueeze(2).to_broadcast([P, NG, EPG]),
                                                rt[:, hot, t, 0:EPG].unsqueeze(1).to_broadcast([P, NG, EPG]),
                                                ALU.mult))
            step.wait()
            member = rt[:, 16, :, :]
            eng.tensor_tensor(member, rt[:, 14, :, :], rt[:, 15, :, :], ALU.add).then_inc(members, 1)
            eng.wait_ge(members, 1)
            for t in range(NT):
                step.mark(eng.tensor_scalar(rt[:, 18, t, :], rt[:, 16, t, :], stat[:, 86 + t:87 + t], None, ALU.mult))
            step.wait()
            step.done(eng.scalar_tensor_tensor(out=rt[:, 18, :, :], in0=rt[:, 15, :, :], scalar=float(TX),
                                               in1=rt[:, 18, :, :], op0=ALU.mult, op1=ALU.add))
            step.done(eng.scalar_tensor_tensor(out=rt[:, 18, :, :], in0=member, scalar=-BIG, in1=rt[:, 18, :, :],
                                               op0=ALU.mult, op1=ALU.add))
            eng.wait_ge(ranks_done, 1)
            rank = rt[:, 19, :, :]
            step.done(eng.scalar_tensor_tensor(out=rank, in0=ps[:, 3, 0:NT * NE].rearrange("p (t e) -> p t e", t=NT),
                                               scalar=1.0, in1=member, op0=ALU.add, op1=ALU.mult))
            step.done(eng.tensor_scalar(rank, rank, -1.0, None, ALU.add))
            step.done(eng.tensor_copy(row_col[:, :, 1], stat[:, 86:88]))

            def select(e, first):
                for t in range(NT):
                    eng.tensor_scalar(sel[:, t, :], slot_no[:, :], first, rank[:, t, ds(e, 1)], ALU.add, ALU.is_equal)\
                       .then_inc(sel_ready, 1)
                eng.tensor_copy(row_col[:, :, 0:1], rt[:, 18, :, ds(e, 1)]).then_inc(sel_ready, 1)

            def list_out(k):
                eng.wait_ge(listed, k + 1)
                step.mark(eng.tensor_scalar(idx_n[:, :], ps[0:C, 7, 0:1], BIG, None, ALU.add))
                eng.tensor_copy(idx_g[:, :], ps[0:C, 7, 1:2]).then_inc(idx_next, 1)

            def x_low(k):
                eng.wait_ge(x_hi_ready, k + 1)
                eng.tensor_tensor(x_s[C:2 * C, :], x_g[:, :], x_s[0:C, :].bitcast(F32), ALU.subtract)\
                   .then_inc(x_lo_ready, 1)

            def x_out(k, j):
                eng.wait_ge(x_turned, 4 * k + j + 1)
                eng.tensor_copy(x_hl[:, 4 * j:4 * j + 4, :, :].rearrange("p c h s -> p (c h s)"), ps[:, 0, :])\
                   .then_inc(x_odd, 1)

            zero = stat[:, 92:93]
            select(0, zero)
            list_out(0)
            step.wait()
            step.done(eng.tensor_copy(idx_m[:, :], idx_n[:, :]))
            select(1, zero)

            def m_low(k, *parts):
                for s in parts:
                    n = s % SLOTS
                    eng.wait_ge(m_hi_ready, PARTS * k + s + 1)
                    eng.tensor_tensor(m_lo[n][:, :], m_raw[n][:, :], m_hi[n][:, :].bitcast(F32), ALU.subtract)\
                       .then_inc(m_lo_dve, 1)

            def y_add(k):
                eng.wait_ge(y_top, k)
                y = y_e[:, :].rearrange("p (b d) -> p b d", b=4)
                eng.tensor_tensor(y, ps[C:2 * C, 3:7, :], y, ALU.add).then_inc(y_ready, 1)

            x_low(0)
            x_out(0, 1)
            x_out(0, 3)
            eng.wait_ge(rt_exp, 2)
            step.done(eng.tensor_reduce(rt[:, 17, :, 1:2], rt[:, 2, :, 0:NG], AX.X, ALU.add))
            step.done(eng.tensor_scalar(rt[:, 17, :, 2:3], rt[:, 10, :, 1:2], 1.0, None, ALU.add))
            step.done(eng.tensor_tensor(rt[:, 17, :, 3:4], rt[:, 17, :, 1:2], rt[:, 17, :, 2:3], ALU.mult))
            w12 = stat[:, W12:W12 + 4].rearrange("p (t k) -> p t k", k=2)
            step.done(eng.reciprocal(w12[:, :, 0:1], rt[:, 17, :, 3:4]))
            step.done(eng.tensor_tensor(w12[:, :, 1:2], w12[:, :, 0:1], rt[:, 10, :, 1:2], ALU.mult))
            w = rt[:, :, :, :].rearrange("p a b c -> p (a b c)")
            n_over = (TX // C - 1) * NE
            flags, upto, unit_of, junk_w, none = (w[:, j * n_over:(j + 1) * n_over] for j in range(5))
            totals = w[:, 5 * n_over:5 * n_over + NE]
            step.done(eng.tensor_copy(totals, ps[:, 4, 0:NE]))

            def further_units():
                for r in range(TX // C - 1):
                    step.mark(eng.tensor_scalar(flags[:, r * NE:(r + 1) * NE], totals, float(C * (r + 1)), None,
                                                ALU.is_gt))
                step.mark(eng.memset(none, 0.0))
                step.wait()
                step.done(eng.tensor_tensor_scan(upto, flags, none, 0.0, ALU.add, ALU.add))
                step.done(eng.scalar_tensor_tensor(out=unit_of, in0=upto, scalar=float(NE - 1), in1=flags, op0=ALU.add,
                                                   op1=ALU.mult))
                for j in range(N_TAB):
                    for k, row in ((0, expert_no), (1, first_no)):
                        step.done(eng.scalar_tensor_tensor(out=junk_w, in0=unit_of, scalar=unit_no[:, j:j + 1],
                                                           in1=row[:, :], op0=ALU.is_equal, op1=ALU.mult,
                                                           accum_out=tab[:, k, j:j + 1]))
                step.done(eng.tensor_scalar(tab[:, 1, :], tab[:, 1, :], BIG, None, ALU.add))
                step.mark(eng.tensor_copy(tab_i[:, 0:N_TAB], tab[:, 0, :]))
                for j in range(2):
                    step.mark(eng.tensor_scalar(tab_i[:, N_TAB + j:N_TAB + j + 1], upto[:, n_over - 1:n_over],
                                                float(NE - j), None, ALU.add))
                step.wait()
                eng.memset(stat[:, 94:95], 0.0).then_inc(tab_ready, 1)

            flat_t = th[:, :, :].rearrange("p f c -> p (f c)")
            flat_h = h_f[:, :, :].rearrange("p f c -> p (f c)")

            def unit(k, following):
                m_low(k, 0, 1, 3, 4, 5)
                list_out(k + 1)
                m_low(k, 7, 8)
                if not is0(k):
                    y_add(k)
                m_low(k, 9, 11)
                following()
                m_low(k, 12, 13)
                x_low(k + 1)
                m_low(k, 15, 16, 17)
                eng.wait_ge(th_ready, k + 1)
                eng.scalar_tensor_tensor(out=flat_t, in0=flat_t, scalar=1.0, in1=ps[:, 2, 0:FC * C],
                                         op0=ALU.add, op1=ALU.mult).then_inc(gated, 1)
                if not is0(k):
                    eng.wait_ge(scattered, 16 * k)
                eng.tensor_copy(idx_i[:, :], idx_m[:, :]).then_inc(idx_ready, 1)
                eng.wait_ge(idx_ready, k + 1)
                step.mark(eng.tensor_copy(idx_m[:, :], idx_n[:, :]))
                m_low(k, 19, 20, 21)
                x_out(k + 1, 1)
                step.wait()
                eng.wait_ge(gated, k + 1)
                eng.wait_ge(u_turned, k + 1)
                eng.scalar_tensor_tensor(out=flat_h, in0=flat_t, scalar=0.5, in1=ps[:, 2, FC * C:2 * FC * C],
                                         op0=ALU.mult, op1=ALU.mult).then_inc(h_f_ready, 1)
                eng.wait_ge(h_hi_ready, k + 1)
                eng.tensor_tensor(h_hl[:, :, 1, :], h_f[:, :, :], h_hl[:, :, 0, :].bitcast(F32), ALU.subtract)\
                   .then_inc(h_ready_e, 1)
                x_out(k + 1, 3)
                m_low(k, 23)

            unit(0, lambda: select(2, zero))
            further_units()
            looped(eng, step, 1, NE - 3, lambda k: unit(k, lambda: select(k + 2, zero)), 2)
            for j in range(2):
                expert = eng.value_load(tab_i[0:1, j:j + 1], min_val=0, max_val=NE - 1)
                unit(NE - 2 + j, lambda: select(expert, tab[:, 1, j:j + 1]))
            k0 = step.base + step.k
            units = eng.value_load(tab_i[0:1, N_TAB:N_TAB + 1], min_val=NE, max_val=NE + MORE)
            with eng.Fori(NE, NE + MORE) as k:
                with eng.If(units > k):
                    step.begin(k0 + (k - NE) * 2)
                    expert = eng.value_load(tab_i[0:1, ds(k - NE + 2, 1)], min_val=0, max_val=NE - 1)
                    unit(k, lambda: select(expert, tab[:, 1, ds(k - NE + 2, 1)]))
            y_add(units)

            for t in range(NT):
                eng.wait_ge(y_in, 16 * NT)
                eng.scalar_tensor_tensor(out=ysum[:, t, :], in0=y_rows[:, 0, t, :],
                                         scalar=stat[:, W12 + 2 * t:W12 + 2 * t + 1], in1=h_res[:, t, :],
                                         op0=ALU.mult, op1=ALU.add).then_inc(y_half, 1)
                eng.wait_ge(y_half, t + 1)
                eng.scalar_tensor_tensor(out=ysum[:, t, :], in0=y_rows[:, 1, t, :],
                                         scalar=stat[:, W12 + 2 * t + 1:W12 + 2 * t + 2], in1=ysum[:, t, :],
                                         op0=ALU.mult, op1=ALU.add).then_inc(ysum_ready, 1)
            eng.wait_ge(y_sq, NT)
            eng.tensor_scalar(stat[:, YRS:YRS + NT], stat[:, YSQ:YSQ + NT], 1.0 / D, EPS, ALU.mult, ALU.add)\
               .then_inc(y_ms, 1)
            eng.wait_ge(y_rstd, 1)
            eng.wait_ge(fgain_in, 16)
            for t in range(NT):
                eng.scalar_tensor_tensor(out=yout[:, t, :], in0=ysum[:, t, :], scalar=stat[:, YRS + t:YRS + t + 1],
                                         in1=fgain[:, :], op0=ALU.mult, op1=ALU.mult).then_inc(yout_ready, 1)

        @block.tensor
        def _(eng):
            eng.wait_ge(consts_ready, 1)
            eng.wait_ge(params_in, 16 * 8)
            eng.transpose(ps[:, 7, 0:N_ROWS], params[0:N_ROWS, :], ident[0:N_ROWS, 0:N_ROWS]).then_inc(params_turned, 1)
            eng.wait_ge(xn_ready, 3)
            for c in range(KC):
                if c >= 4:
                    eng.wait_ge(xt_lo_ready, c - 3)
                cs = slice(c * P, (c + 1) * P)
                eng.transpose(ps[:, 3 + c % 4, 0:NM], metan[:, cs], ident[0:NM, 0:NM])
                eng.transpose(ps[:, 3 + c % 4, NM:NM + P], xn[:, 0, cs], ident[:, :])
                eng.transpose(ps[:, 3 + c % 4, NM + P:T], xn[:, 1, cs], ident[:, :]).then_inc(xt_turned, 1)

            def chunk(n, s, acc, act_hi, act_lo, t0, extras=(), order=range(KC), ready=None, freed=2):
                eng.wait_ge(lo_ready, n + 1)
                at_least(eng, acc_out, n - freed + 1)
                w = act_hi.shape[2] - t0
                for k, c in enumerate(order):
                    if k in dict(extras):
                        dict(extras)[k]()
                    if ready:
                        ready(c)
                    o = ps[:, acc, 0:w]
                    eng.matmul(o, w_hi[s][:, c, :], act_hi[:, c, t0:], start=(k == 0), stop=False,
                               skip_group_check=True)
                    eng.matmul(o, w_hi[s][:, c, :], act_lo[:, c, t0:], start=False, stop=False, skip_group_check=True)
                    ins = eng.matmul(o, w_lo[s][:, c, :], act_hi[:, c, t0:], start=False, stop=(k == KC - 1),
                                     skip_group_check=True)
                ins.then_inc(chunk_done, 1)

            def turn_v(h):
                eng.wait_ge(acc_out, 3 * h + 3)
                if not is0(h):
                    eng.wait_ge(mix_lo_ready, h)
                eng.transpose(ps[:, 6, 0:P], v_t[:, NM:NM + P], ident[:, :])
                eng.transpose(ps[:, 6, P:TX], v_t[:, NM + P:T], ident[:, :])
                eng.transpose(ps[0:NM, 6, TX:TX + P], v_t[:, 0:NM], ident[:, :]).then_inc(v_turned, 1)

            def score(h):
                eng.wait_ge(acc_out, 3 * h + 2)
                at_least(eng, biased, h)
                for m in range(2):
                    rows = slice(DH * m, DH * (m + 1))
                    for t, c0, w in ((0, S0, K0), (1, S1, K1)):
                        ins = eng.matmul(ps[:, 3 + m, c0:c0 + w], q_t[rows, t * P:(t + 1) * P], k_t[rows, 0:w],
                                         start=True, stop=True)
                ins.then_inc(scores_done, 1)

            def turn_a(h):
                eng.wait_ge(a_ready, 2 * h + 2)
                at_least(eng, a_out, 3 * h)
                eng.transpose(ps[:, 5, 0:P], a_sb[:, S0 + NM:S0 + NM + P], ident[:, :])
                eng.transpose(ps[:, 5, P:TX], a_sb[:, S1 + NM:S1 + NM + P], ident[:, :])
                eng.transpose(ps[:, 5, TX + P:2 * TX], a_sb[:, S1 + NM + P:S1 + T], ident[:, :])
                eng.transpose(ps[0:NM, 7, 0:P], a_sb[:, S0:S0 + NM], ident[:, :])
                eng.transpose(ps[0:NM, 7, P:TX], a_sb[:, S1:S1 + NM], ident[:, :]).then_inc(a_turned, 1)

            def attend(h):
                eng.wait_ge(a_out, 3 * h + 3)
                eng.wait_ge(v_out, 2 * h + 2)
                at_least(eng, o_out, h)
                for t in range(NT):
                    o = ps[:, 7, TX + t * P:TX + (t + 1) * P]
                    q = slice(t * P, (t + 1) * P)
                    eng.matmul(o, at_m[:, q], v_meta[:, :], start=True, stop=False)
                    for k in range(t + 1):
                        ins = eng.matmul(o, at_x[:, k, q], v_tm[:, k, :], start=False, stop=(k == t))
                ins.then_inc(o_done, 1)

            def turn_o(h):
                eng.wait_ge(o_out, h + 1)
                eng.transpose(ps[:, 6, 0:P], o_sb[:, 0, :], ident[:, :])
                eng.transpose(ps[:, 6, P:TX], o_sb[:, 1, :], ident[:, :]).then_inc(o_turned, 1)

            def qkv(h):
                n = 3 * h
                if is0(h):
                    chunk(0, 0, 0, xt_hi, xt_lo, NM, ready=lambda c: eng.wait_ge(xt_lo_ready, c + 1), freed=3)
                    chunk(1, 1, 1, xt_hi, xt_lo, 0, freed=3)
                    chunk(2, 2, 2, xt_hi, xt_lo, 0, extras=[(6, lambda: score(0))], freed=3)
                    return
                chunk(n, 0, 0, xt_hi, xt_lo, NM, extras=[(4, lambda: turn_v(h - 1))], freed=3)
                chunk(n + 1, 1, 1, xt_hi, xt_lo, 0, extras=[(4, lambda: turn_a(h - 1)), (12, lambda: attend(h - 1))],
                      freed=3)
                chunk(n + 2, 2, 2, xt_hi, xt_lo, 0, extras=[(6, lambda: score(h)), (12, lambda: turn_o(h - 1))],
                      freed=3)

            qkv(0)
            qkv(1)
            with eng.Fori(2, HEADS) as h:
                qkv(h)

            def gates(g, b, i):
                eng.wait_ge(xc_ready, g + 1)
                eng.wait_ge(gates_in[b], 32 * (i + 1))
                at_least(eng, e_ready, 2 * g)
                if is0(i) and b == 0:
                    eng.wait_ge(biased, HEADS)
                eng.matmul(ps[:, 3, 0:T], g_w[:, b, 0, :], xc[:, :], start=True, stop=True)
                eng.matmul(ps[:, 4, 0:T], g_w[:, b, 1, :], xc[:, :], start=True, stop=True).then_inc(gates_done, 1)

            def lru(i, b):
                g = 2 * i + b
                n = LRU0 + 2 * g
                h = HEADS - 1
                first = is0(i) and b == 0
                chunk(n, 2 * b, 0, xt_hi, xt_lo, 0, extras=[(4, lambda: turn_v(h)), (12, lambda: turn_a(h))]
                      if first else ())
                chunk(n + 1, 2 * b + 1, 1, xt_hi, xt_lo, NM,
                      extras=[(3, lambda: attend(h)), (12, lambda: gates(g, b, i)), (15, lambda: turn_o(h))]
                      if first else [(12, lambda: gates(g, b, i))])

            lru(0, 0)
            lru(0, 1)
            with eng.Fori(1, LB // 2) as i:
                lru(i, 0)
                lru(i, 1)

            def turn_back(m, b):
                eng.wait_ge(acc_out, OUT0 + m + 1)
                at_least(eng, h_ready, m)
                for t in range(NT):
                    ins = eng.transpose(ps[:, 3, t * P:(t + 1) * P], o_t[b][:, t * P:(t + 1) * P], ident[:, :])
                ins.then_inc(o_back, 1)

            def turn_h(m, b):
                eng.wait_ge(h_ready, m + 1)
                at_least(eng, h_t_ready, m)
                for t in range(NT):
                    ins = eng.transpose(ps[:, 4, t * P:(t + 1) * P], h_s[b][:, t, :], ident[:, :])
                ins.then_inc(h_turned, 1)

            def logits(m, b, last=False):
                eng.wait_ge(h_t_ready, m + 1)
                for t in range(NT):
                    ins = eng.matmul(ps[:, 5 + t, 0:NG + NE], h_tt[b][:, t * P:(t + 1) * P],
                                     rw[:, ds(m, 1), :].rearrange("p a e -> p (a e)"), start=is0(m), stop=last,
                                     skip_group_check=True)
                ins.then_inc(logits_done, 1)

            heads_first = list(range(LB, KC)) + list(range(LB))

            def mix_ready(c):
                k = HEADS + c + 1 if c < LB else c - LB + 1
                eng.wait_ge(mix_hi_ready, k)
                eng.wait_ge(mix_lo_ready, k)

            def project(i, s):
                m = RING * i + s
                extras = ()
                if not (is0(i) and s == 0):
                    b = (s - 1) % 2
                    extras = [(2, lambda: turn_back(m - 1, b)), (7, lambda: turn_h(m - 1, b)),
                              (13, lambda: logits(m - 1, b))]
                chunk(OUT0 + m, s, s % 2, mix_hi, mix_lo, 0, extras=extras, order=heads_first,
                      ready=mix_ready if (is0(i) and s == 0) else None)

            for s in range(RING):
                project(0, s)
            with eng.Fori(1, N_OUT // RING) as i:
                for s in range(RING):
                    project(i, s)
            turn_back(N_OUT - 1, 1)
            turn_h(N_OUT - 1, 1)
            logits(N_OUT - 1, 1, last=True)

            eng.wait_ge(members, 1)
            m0, m1 = rt[:, 16, 0, :], rt[:, 16, 1, :]
            eng.matmul(ps[:, 3, 0:NE], ltri[:, :], m0, start=True, stop=True)
            eng.matmul(ps[:, 3, NE:2 * NE], ones[:, :], m0, start=True, stop=False)
            eng.matmul(ps[:, 3, NE:2 * NE], ltri[:, :], m1, start=False, stop=True)
            eng.matmul(ps[:, 4, 0:NE], ones[:, :], m0, start=True, stop=False)
            eng.matmul(ps[:, 4, 0:NE], ones[:, :], m1, start=False, stop=True).then_inc(ranks_done, 1)

            def lists(k):
                eng.wait_ge(sel_ready, 3 * (k + 1))
                for t in range(NT):
                    ins = eng.matmul(ps[0:C, 7, 0:2], sel[:, t, :], row_col[:, t, :], start=(t == 0), stop=(t == NT - 1))
                ins.then_inc(listed, 1)

            def turn_x(k, j):
                if j < 2:
                    eng.wait_ge(x_lo_ready, k + 1)
                else:
                    eng.wait_ge((x_even, x_odd)[j % 2], 2 * k + 1)
                for c in range(4):
                    ins = eng.matmul(ps[:, 7 - 7 * (j % 2), c * P:(c + 1) * P], x_s[:, (4 * j + c) * P:(4 * j + c + 1) * P],
                                     ident_r[:, :], start=True, stop=True)
                ins.then_inc(x_turned, 1)

            def split_ready(k, s):
                if s in POOL_PARTS:
                    eng.wait_ge(m_lo_pool, len(POOL_PARTS) * k + POOL_PARTS.index(s) + 1)
                else:
                    done = sum(1 for q in range(s) if q not in POOL_PARTS)
                    eng.wait_ge(m_lo_dve, LO_DVE * k + done + 1)

            def hidden(k, acc, parts):
                for s in parts:
                    split_ready(k, s)
                    n = s % SLOTS
                    for c in range(2):
                        kc = 2 * (s % 8) + c
                        for w in (m_hi, m_lo):
                            ins = eng.matmul(ps[:, acc, :], x_hl[:, kc, :, :], w[n][:, c * F:(c + 1) * F],
                                             start=(kc == 0 and w is m_hi), stop=(kc == KC - 1 and w is m_lo))
                    ins.then_inc(part_used, 1)

            def turn(k, j):
                for f in range(FC):
                    ins = eng.matmul(ps[:, 2, (j * FC + f) * C:(j * FC + f + 1) * C], gu_sb[:, j, f * P:(f + 1) * P],
                                     pair[:, :], start=True, stop=True)
                ins.then_inc((g_turned, u_turned)[j], 1)

            def unit(k):
                eng.wait_ge(x_even, 2 * (k + 1))
                eng.wait_ge(x_odd, 2 * (k + 1))
                lists(k + 1)
                hidden(k, 0, range(0, 8))
                hidden(k, 1, range(8, 12))
                eng.wait_ge(g_copied, k + 1)
                turn(k, 0)
                hidden(k, 1, range(12, 16))
                eng.wait_ge(idx_next, k + 2)
                turn_x(k + 1, 0)
                turn_x(k + 1, 1)
                eng.wait_ge(u_copied, k + 1)
                eng.wait_ge(gated, k + 1)
                turn(k, 1)
                turn_x(k + 1, 2)
                turn_x(k + 1, 3)
                eng.wait_ge(h_ready_e, k + 1)
                at_least(eng, y_ready, k)
                for s in range(16, 24):
                    f = (s - 16) // 2
                    split_ready(k, s)
                    for b in range(2):
                        for w in (m_hi, m_lo):
                            ins = eng.matmul(ps[:, 3 + 2 * (s % 2) + b, :], h_hl[:, f, :, :],
                                             w[s % SLOTS][:, b * F:(b + 1) * F],
                                             start=(f == 0 and w is m_hi), stop=(f == FC - 1 and w is m_lo))
                    ins.then_inc(part_used, 1)

            lists(0)
            eng.wait_ge(ident_r_ready, 1)
            for j in range(4):
                turn_x(0, j)
            unit(0)
            with eng.Fori(1, NE) as k:
                unit(k)
            eng.wait_ge(tab_ready, 1)
            units = eng.value_load(tab_i[0:1, N_TAB:N_TAB + 1], min_val=NE, max_val=NE + MORE)
            with eng.Fori(NE, NE + MORE) as k:
                with eng.If(units > k):
                    unit(k)

    return nc


_INS = ["x", "meta_tokens", "norm1_g", "w_in", "conv_w", "conv_b", "gate_a_w", "gate_a_b", "gate_x_w", "gate_x_b",
        "lru_a_param", "lambda_q1", "lambda_k1", "lambda_q2", "lambda_k2", "subln_g", "w_out", "norm2_g",
        "router_g_w", "router_g_b", "router_e_w", "router_e_b", "exp_w_gate", "exp_w_up", "exp_w_down",
        "final_norm_g"]


def kernel(**inputs):
    import numpy as np
    import concourse.bacc as bacc
    from concourse.bass_utils import run_bass_kernel_spmd

    nc = bacc.Bacc("TRN2", target_bir_lowering=False, num_devices=1)
    arrays, args = {}, []
    for name in _INS:
        a = np.ascontiguousarray(inputs[name])
        arrays[f"in_{name}"] = a
        args.append(nc.dram_tensor(f"in_{name}", a.shape, mybir.dt.from_np(a.dtype), kind="ExternalInput").ap())
    out = nc.dram_tensor("out", (1, TX, D), F32, kind="ExternalOutput").ap()
    build(nc, *args, out)
    r = run_bass_kernel_spmd(nc, [arrays], core_ids=[0])
    return r.results[0]["out"]
```

```python
from contextlib import ExitStack

import concourse.bass as bass
from concourse import mybir

P = 128
D = 2048
KC = D // P
TX = 256
NM = 16
T = NM + TX
NT = TX // P
HEADS = 8
DH = 64
CHUNK = 64
LW = 1024
LB = LW // P
CONVW = 4
NG, EPG = 4, 4
NE = NG * EPG
F = 512
FC = F // P
C = 64
MORE = 2 * TX // C
N_TAB = MORE + 2
SLOTS = 12
PARTS = 24
PW = 2 * F
POOL_PARTS = (1, 4, 7, 10, 13, 16, 19, 22)
LO_DVE = PARTS - len(POOL_PARTS)
EPS = 1e-6
LAM_INIT = 0.8 - 0.6
BIG = 4096.0
K0, K1 = NM + P, T
S0, S1 = 0, K0
SW = K0 + K1

N_QKV = 3 * HEADS
N_LRU = 2 * LB
N_OUT = D // P
LRU0 = N_QKV
OUT0 = N_QKV + N_LRU
N_CHUNKS = OUT0 + N_OUT
QKV_RING = 3
TURN_BANKS = 6
RING = 4

F32 = mybir.dt.float32
F32R = mybir.dt.float32r
I32 = mybir.dt.int32
ALU = mybir.AluOpType
ACT = mybir.ActivationFunctionType
AX = mybir.AxisListType

ROW_G1, ROW_G2, ROW_CB, ROW_CW, ROW_BA, ROW_BX, ROW_LA, ROW_SG = 0, 16, 32, 40, 72, 80, 88, 96
N_ROWS = 97


def ds(start, size):
    return bass.ds(start, size)


class Steps:

    def __init__(self, eng, sem):
        self.eng, self.sem, self.base, self.k = eng, sem, 0, 0

    def mark(self, ins):
        self.k += 1
        ins.then_inc(self.sem, 1)

    def wait(self):
        self.eng.wait_ge(self.sem, self.base + self.k)

    def done(self, ins):
        self.mark(ins)
        self.wait()

    def begin(self, base):
        self.base, self.k = base, 0


def looped(eng, steps, first, count, body, per_body):
    start = steps.base + steps.k
    with eng.Fori(first, first + count) as i:
        steps.begin((i - first) * per_body + start)
        body(i)
        assert steps.k == per_body, (steps.k, per_body)
    steps.begin(start + count * per_body)


def at_least(eng, sem, value):
    if isinstance(value, int) and value <= 0:
        return
    eng.wait_ge(sem, value)


def build(nc, x, meta_tokens, norm1_g, w_in, conv_w, conv_b, gate_a_w, gate_a_b, gate_x_w, gate_x_b,
          lru_a_param, lambda_q1, lambda_k1, lambda_q2, lambda_k2, subln_g, w_out, norm2_g,
          router_g_w, router_g_b, router_e_w, router_e_b, exp_w_gate, exp_w_up, exp_w_down,
          final_norm_g, out):
    with ExitStack() as ctx:
        ctx.enter_context(nc.allow_non_contiguous_dma("small parameter loads"))

        def sem(name):
            return ctx.enter_context(nc.semaphore(name))

        base = [(nc.sbuf_base + 31) // 32 * 32]
        arena = nc.alloc_sbuf_tensor("arena", [P, (nc.sbuf_usable_end - base[0] - 64) // 4], F32)
        limit = nc.sbuf_usable_end

        def place(name, shape, dt, offset=None):
            n = 4
            for s in shape[1:]:
                n *= s
            n = (n + 31) // 32 * 32
            if offset is None:
                offset = base[0]
                base[0] += n
                assert base[0] <= limit, (name, base[0], limit)
            return nc.alloc_sbuf_tensor_at(name, shape, dt, offset=offset), offset, offset + n

        def region(start, end, *parts):
            o = start
            got = []
            for name, shape, dt in parts:
                t, _, o = place(name, shape, dt, o)
                got.append(t)
            assert o <= end, (parts[-1][0], o, end)
            return got

        h_res, _, _ = place("h_res", [P, NT, D], F32)
        mix_hi, MIX, _ = place("mix_hi", [P, KC, TX], F32R)
        mix_lo, _, MIX_END = place("mix_lo", [P, KC, TX], F32R)
        x_s, x_hl, y_hi, y_lo = region(MIX, MIX_END, ("x_s", [P, D], F32R), ("x_hl", [P, KC, 2, C], F32R),
                                       ("y_hi", [P, 4, F], F32R), ("y_lo", [P, 4, F], F32R))
        hn_0, = region(MIX + 3 * 4 * D, MIX_END, ("hn_0", [P, KC, P], F32))
        xn, metan, junk = region(MIX, MIX_END, ("xn", [P, NT, D], F32), ("metan", [NM, D], F32), ("junk", [P, D], F32))
        STAGE = base[0]
        raw, w_lo, w_hi = [], [], []
        for s in range(RING):
            t, o, _ = place(f"raw{s}", [P, KC, P], F32)
            raw.append(t)
            w_lo.append(place(f"w_lo{s}", [P, KC, P], F32R, o)[0])
            w_hi.append(place(f"w_hi{s}", [P, KC, P], F32R)[0])
        STAGE_END = base[0]
        WREG = base[0]
        m_raw, m_lo, m_hi = [], [], []
        SLOT_BYTES = 4 * PW
        for n in range(SLOTS):
            here = None if n < SLOTS - 2 else STAGE + 2 * SLOT_BYTES * (n - (SLOTS - 2))
            t, o, _ = place(f"m_raw{n}", [P, PW], F32, here)
            m_raw.append(t)
            m_lo.append(place(f"m_lo{n}", [P, PW], F32R, o)[0])
            m_hi.append(place(f"m_hi{n}", [P, PW], F32R, None if here is None else here + SLOT_BYTES)[0])
        WREG_END = base[0]
        hn_lo, hn_hi, gu_sb, th, h_f, h_hl, sel, ident_r, rt, back, gates, tok = region(
            STAGE + 4 * SLOT_BYTES, STAGE_END, ("hn_lo", [P, NT, KC, P], F32R), ("hn_hi", [P, NT, KC, P], F32R),
            ("gu_sb", [P, 2, F], F32), ("th", [P, FC, C], F32), ("h_f", [P, FC, C], F32),
            ("h_hl", [P, FC, 2, C], F32R), ("sel", [P, NT, 4 * C], F32R), ("ident_r", [P, P], F32R),
            ("rt", [P, 20, NT, NE], F32), ("back", [P, TX], F32R), ("gates", [P, NT, NE + MORE], F32),
            ("tok", [P, 1], F32))
        g2b, hg = region(WREG + 14 * SLOT_BYTES, WREG_END, ("g2b", [P, D], F32), ("hg", [P, NT, D], F32))
        (xt_hi, xt_lo, q_t, k_t, v_t, v_tm, v_meta, s_sb, a_sb, at_x, at_m, o_sb, u_pad, yg_t, xc, th_ri, a_t, tg,
         lr1, lr2, lr3, gl1, gl2, hs_t, g_w, lru_f, junk_a) = region(
            WREG, WREG_END, ("xt_hi", [P, KC, T], F32R), ("xt_lo", [P, KC, T], F32R),
            ("q_t", [P, TX], F32), ("k_t", [P, T], F32), ("v_t", [P, T], F32), ("v_tm", [P, NT, P], F32),
            ("v_meta", [NM, P], F32), ("s_sb", [P, 2, SW], F32), ("a_sb", [P, SW], F32),
            ("at_x", [P, NT, TX], F32), ("at_m", [NM, TX], F32), ("o_sb", [P, NT, P], F32),
            ("u_pad", [P, CONVW - 1 + T], F32), ("yg_t", [P, 2, TX], F32), ("xc", [P, T], F32),
            ("th_ri", [P, 2, T], F32), ("a_t", [P, T], F32), ("tg", [P, T], F32),
            ("lr1", [P, T], F32), ("lr2", [P, T], F32), ("lr3", [P, T], F32), ("gl1", [P, 2, TX], F32),
            ("gl2", [P, 2, TX], F32), ("hs_t", [P, 2, T], F32), ("g_w", [P, 2, 2, P], F32), ("lru_f", [P, TX], F32),
            ("junk_a", [P, NT, P], F32))
        yout, fgain = region(WREG, WREG_END, ("yout", [P, NT, D], F32), ("fgain", [P, D], F32))

        def small(name, shape, dt=F32):
            return place(name, shape, dt)[0]

        ident = small("ident", [P, P])
        ltri = small("ltri", [P, P])
        ones = small("ones", [P, P])
        params = small("params", [P, P])
        col = small("col", [P, N_ROWS])
        lam_in = small("lam_in", [P, 4, DH])
        bias = small("bias", [P, SW])
        rw = small("rw", [P, KC, NG + NE])
        rb = small("rb", [P, NG + NE])
        slot_no = small("slot_no", [P, C])
        pair = small("pair", [P, C])
        tok_no = small("tok_no", [P, TX])
        expert_no = small("expert_no", [P, (TX // C - 1) * NE])
        first_no = small("first_no", [P, (TX // C - 1) * NE])
        unit_no = small("unit_no", [P, N_TAB])
        tab = small("tab", [P, 2, N_TAB])
        tab_i = small("tab_i", [P, N_TAB + 2], I32)
        stat = small("stat", [P, 96])
        halfb = small("halfb", [P, 2 * LB])
        sp = small("sp", [P, 8, LB])
        o_t = [small(f"o_t{i}", [P, TX]) for i in range(2)]
        h_s = [small(f"h_s{i}", [P, NT, P]) for i in range(2)]
        h_tt = [small(f"h_t{i}", [P, TX]) for i in range(2)]
        sg = small("sg", [P, 1])

        ps = ctx.enter_context(nc.psum_tensor("ps", [P, 8, 512], F32))

        x_rows = x.rearrange("b (t p) d -> p (b t) d", p=P)
        out_rows = out.rearrange("b (t p) d -> p (b t) d", p=P)
        w_in_rows = w_in[0].rearrange("(c p) n -> p c n", p=P)
        w_out_rows = w_out[0].rearrange("(c p) n -> p c n", p=P)
        wg_rows = exp_w_gate[0].rearrange("e (p c) f -> e p (c f)", c=KC)
        wu_rows = exp_w_up[0].rearrange("e (p c) f -> e p (c f)", c=KC)
        wd_rows = exp_w_down[0].rearrange("e (c p) d -> e c p d", p=P)

        x_in = [sem(f"x_in{i}") for i in range(3)]
        params_in = sem("params_in")
        misc_in = sem("misc_in")
        gates_in = [sem(f"gates_in{i}") for i in range(2)]
        raw_in = [sem(f"raw_in{i}") for i in range(RING)]
        slot_in = [sem(f"slot_in{i}") for i in range(SLOTS)]
        fgain_in, out_done = sem("fgain_in"), sem("out_done")
        carried = sem("carried")
        consts_ready, dve_step, pool_step = sem("consts_ready"), sem("dve_step"), sem("pool_step")
        sq_ready, xn_ready, xn1_ready = sem("sq_ready"), sem("xn_ready"), sem("xn1_ready")
        params_turned, cols_ready = sem("params_turned"), sem("cols_ready")
        xt_turned, xt_hi_ready, xt_lo_ready = sem("xt_turned"), sem("xt_hi_ready"), sem("xt_lo_ready")
        ms_ready, rstd_ready = sem("ms_ready"), sem("rstd_ready")
        sp_e_in, sp_e_out = sem("sp_e_in"), sem("sp_e_out")
        hi_ready, lo_ready, chunk_done, acc_out = sem("hi_ready"), sem("lo_ready"), sem("chunk_done"), sem("acc_out")
        v_turned, v_out = sem("v_turned"), sem("v_out")
        scores_done, biased = sem("scores_done"), sem("biased")
        max_ready, probs_ready, a_ready = sem("max_ready"), sem("probs_ready"), sem("a_ready")
        a_turned, a_out = sem("a_turned"), sem("a_out")
        o_done, o_sq, o_ms, o_rstd, o_out, o_turned = (sem("o_done"), sem("o_sq"), sem("o_ms"), sem("o_rstd"),
                                                       sem("o_out"), sem("o_turned"))
        mix_hi_ready, mix_lo_ready = sem("mix_hi_ready"), sem("mix_lo_ready")
        xc_ready, gates_done, th_ri_ready, ix_ready, at_ready = (
            sem("xc_ready"), sem("gates_done"), sem("th_ri_ready"), sem("ix_ready"), sem("at_ready"))
        q_ready, sqrt_ready, scanned, lru_ready = sem("q_ready"), sem("sqrt_ready"), sem("scanned"), sem("lru_ready")
        gelu_in, gelu_th, gelu_ready = sem("gelu_in"), sem("gelu_th"), sem("gelu_ready")
        o_back, h_ready, h_kept, h_turned, h_t_ready, logits_done = (
            sem("o_back"), sem("h_ready"), sem("h_kept"), sem("h_turned"), sem("h_t_ready"), sem("logits_done"))
        h_sq = sem("h_sq")
        h_ms, h_rstd, hn_scaled, g2b_in = sem("h_ms"), sem("h_rstd"), sem("hn_scaled"), sem("g2b_in")
        hn_hi_ready, hn_lo_ready = sem("hn_hi_ready"), sem("hn_lo_ready")
        ident_r_ready = sem("ident_r_ready")
        rt_max, rt_exp = sem("rt_max"), sem("rt_exp")
        members, ranks_done, sel_ready, tab_ready = (
            sem("members"), sem("ranks_done"), sem("sel_ready"), sem("tab_ready"))
        m_hi_ready, m_lo_dve, m_lo_pool = sem("m_hi_ready"), sem("m_lo_dve"), sem("m_lo_pool")
        part_used, gathered, listed, x_rows_left, x_rows_right = (
            sem("part_used"), sem("gathered"), sem("listed"), sem("x_rows_left"), sem("x_rows_right"))
        x_turned, x_even, x_odd = sem("x_turned"), sem("x_even"), sem("x_odd")
        g_copied, u_copied, g_turned, u_turned, th_ready = (
            sem("g_copied"), sem("u_copied"), sem("g_turned"), sem("u_turned"), sem("th_ready"))
        gated = sem("gated")
        h_f_ready, h_hi_ready, h_ready_e = sem("h_f_ready"), sem("h_hi_ready"), sem("h_ready_e")
        tok_ready, back_ready = sem("tok_ready"), sem("back_ready")
        gates_kept = sem("gates_kept")
        y_hi_ready, y_lo_ready, combined, added = sem("y_hi_ready"), sem("y_lo_ready"), sem("combined"), sem("added")
        y_sq, y_ms, y_rstd, yout_ready = sem("y_sq"), sem("y_ms"), sem("y_rstd"), sem("yout_ready")

        def chunk_use(n_slot, phase, i):
            before = {"qkv": 0, "lru": HEADS, "out": HEADS + N_LRU // RING}[phase]
            if n_slot == RING - 1 and phase != "qkv":
                before -= HEADS
            return before + i + 1

        def is0(i):
            return isinstance(i, int) and i == 0

        def apart(eng):
            eng.sem_inc(carried, 1)

        SQ, RSTD = 0, 4
        LAM, NLAM = 8, 9
        NMAX, L, RL, CM = 12, 16, 20, 24
        OSQ, ORS = 28, 30
        W12 = 32
        HRS, YSQ, YRS = 36, 38, 40
        HSQ = 48
        NH = 80
        LP = 84

        def qkv_src(h, j):
            return w_in_rows[:, :, ds(2 * LW + j * 1024 + h * P, P)]

        def lru_src(g, j):
            return w_in_rows[:, :, ds(j * LW + g * P, P)]

        block = ctx.enter_context(nc.Block())

        @block.sync
        def _(sp_e):
            eng = sp_e
            eng.dma_start(metan[:, :], meta_tokens).then_inc(x_in[2], 16)
            eng.dma_start(h_res[:, 0, :], x_rows[:, 0, :]).then_inc(x_in[0], 16)
            eng.dma_start(h_res[:, 1, :], x_rows[:, 1, :]).then_inc(x_in[1], 16)

            def load_qkv(h, j, first=False):
                n = 3 * h + j
                if not is0(h):
                    eng.wait_ge(chunk_done, n - QKV_RING + 1)
                eng.dma_start(raw[j][:, :, :], qkv_src(h, j)).then_inc(raw_in[j], 16)

            for j in range(3):
                load_qkv(0, j)
                if j == 0:
                    for r, src in ((ROW_G1, norm1_g[0].rearrange("(c p) -> c p", p=P)),
                                   (ROW_G2, norm2_g[0].rearrange("(c p) -> c p", p=P)),
                                   (ROW_CB, conv_b[0].rearrange("(c p) -> c p", p=P)),
                                   (ROW_CW, conv_w[0].rearrange("k (c p) -> (k c) p", p=P)),
                                   (ROW_BA, gate_a_b[0].rearrange("(c p) -> c p", p=P)),
                                   (ROW_BX, gate_x_b[0].rearrange("(c p) -> c p", p=P)),
                                   (ROW_LA, lru_a_param[0].rearrange("(c p) -> c p", p=P)),
                                   (ROW_SG, subln_g)):
                        eng.dma_start(params[r:r + src.shape[0], :], src).then_inc(params_in, 16)
            for k, lam in enumerate((lambda_q1, lambda_q2, lambda_k1, lambda_k2)):
                eng.dma_start(lam_in[:, k, :], lam.partition_broadcast(P)).then_inc(misc_in, 16)
            eng.dma_start(rw[:, :, 0:NG], router_g_w[0].rearrange("(c p) g -> p c g", p=P)).then_inc(misc_in, 16)
            eng.dma_start(rw[:, :, NG:], router_e_w[0].rearrange("(c p) g -> p c g", p=P)).then_inc(misc_in, 16)
            eng.dma_start(rb[:, 0:NG], router_g_b.partition_broadcast(P)).then_inc(misc_in, 16)
            eng.dma_start(rb[:, NG:], router_e_b.partition_broadcast(P)).then_inc(misc_in, 16)
            with eng.Fori(1, HEADS) as h:
                for j in range(3):
                    load_qkv(h, j)

            def load_lru(i):
                for s in range(RING):
                    if is0(i):
                        if s < QKV_RING:
                            eng.wait_ge(chunk_done, LRU0 - QKV_RING + s + 1)
                    else:
                        eng.wait_ge(chunk_done, LRU0 + RING * i + s - RING + 1)
                    eng.dma_start(raw[s][:, :, :], lru_src(2 * i + s // 2, s % 2)).then_inc(raw_in[s], 16)
                    if s % 2 == 0:
                        g = 2 * i + s // 2
                        if not is0(i):
                            eng.wait_ge(gates_done, g - 1)
                        eng.dma_start(g_w[:, s // 2, 0, :], gate_a_w[0, ds(g, 1)].rearrange("g i j -> i (g j)"))\
                           .then_inc(gates_in[s // 2], 16)
                        eng.dma_start(g_w[:, s // 2, 1, :], gate_x_w[0, ds(g, 1)].rearrange("g i j -> i (g j)"))\
                           .then_inc(gates_in[s // 2], 16)

            load_lru(0)
            with eng.Fori(1, LB // 2) as i:
                load_lru(i)

            def load_out(m, s):
                eng.wait_ge(chunk_done, OUT0 + m - RING + 1)
                eng.dma_start(raw[s][:, :, :], w_out_rows[:, :, ds(m * P, P)]).then_inc(raw_in[s], 16)

            def load_part(e, s):
                if s < 16:
                    rows = (wg_rows if s < 8 else wu_rows)[ds(e, 1), :, (s % 8) * PW:(s % 8 + 1) * PW]
                else:
                    rows = wd_rows[ds(e, 1), (s - 16) // 2, :, (s % 2) * PW:(s % 2 + 1) * PW]
                eng.dma_start(m_raw[s % SLOTS][:, :], rows.rearrange("e p n -> (e p) n")).then_inc(slot_in[s % SLOTS], 16)

            for s in range(RING):
                load_out(s, s)
            eng.wait_ge(mix_hi_ready, KC)
            eng.wait_ge(mix_lo_ready, KC)
            eng.dma_start(g2b[:, :], norm2_g[0].partition_broadcast(P)).then_inc(g2b_in, 16)
            for s in range(RING):
                load_out(RING + s, s)
                for j in (2 * s, 2 * s + 1):
                    if j < 7:
                        load_part(0, j)
            for i in range(2, N_OUT // RING):
                for s in range(RING):
                    load_out(RING * i + s, s)
            eng.wait_ge(chunk_done, OUT0 + N_OUT - RING + 1)
            load_part(0, 10)
            load_part(0, 11)
            eng.wait_ge(h_kept, N_OUT)
            load_part(0, 7)
            eng.wait_ge(hn_scaled, 1)
            eng.wait_ge(hn_hi_ready, NT)
            eng.wait_ge(hn_lo_ready, NT)
            load_part(0, 8)
            load_part(0, 9)
            for s in range(SLOTS, PARTS):
                eng.wait_ge(part_used, s - SLOTS + 1)
                load_part(0, s)

            def load_unit(k, e):
                for s in range(PARTS):
                    eng.wait_ge(part_used, PARTS * k + s - SLOTS + 1)
                    load_part(e, s)

            with eng.Fori(1, NE) as k:
                load_unit(k, k)
            eng.wait_ge(tab_ready, 1)
            units = eng.value_load(tab_i[0:1, N_TAB:N_TAB + 1], min_val=NE, max_val=NE + MORE)
            with eng.Fori(NE, NE + MORE) as k:
                with eng.If(units > k):
                    e = eng.value_load(tab_i[0:1, ds(k - NE, 1)], min_val=0, max_val=NE - 1)
                    load_unit(k, e)
            eng.wait_ge(part_used, PARTS * units)
            apart(eng)
            eng.dma_start(fgain[:, :], final_norm_g.partition_broadcast(P)).then_inc(fgain_in, 16)
            for t in range(NT):
                for j in range(2):
                    eng.wait_ge(yout_ready, 2 * t + j + 1)
                    cs = slice(j * D // 2, (j + 1) * D // 2)
                    eng.dma_start(out_rows[:, t, cs], yout[:, t, cs]).then_inc(out_done, 16)
            eng.wait_ge(out_done, 16 * 2 * NT)

        @block.gpsimd
        def _(eng):
            step = Steps(eng, pool_step)
            step.done(eng.memset(ident[:, :], 0.0))
            eng.affine_select(out=ident[:, :], in_=ident[:, :], compare_op=ALU.not_equal, fill=1.0, base=0,
                              pattern=[[-1, P]], channel_multiplier=1).then_inc(consts_ready, 1)
            step.done(eng.memset(ones[:, :], 1.0))
            step.mark(eng.affine_select(out=ltri[:, :], in_=ones[:, :], compare_op=ALU.is_gt, fill=0.0, base=0,
                                        pattern=[[1, P]], channel_multiplier=-1))
            step.mark(eng.iota(slot_no[:, :], [[1, C]], base=0, channel_multiplier=0,
                               allow_small_or_imprecise_dtypes=True))
            step.mark(eng.iota(unit_no[:, :], [[1, N_TAB]], base=NE, channel_multiplier=0,
                               allow_small_or_imprecise_dtypes=True))
            step.mark(eng.iota(expert_no[:, :], [[0, TX // C - 1], [1, NE]], base=0, channel_multiplier=0,
                               allow_small_or_imprecise_dtypes=True))
            step.mark(eng.iota(first_no[:, :], [[C, TX // C - 1], [0, NE]], base=C - int(BIG), channel_multiplier=0,
                               allow_small_or_imprecise_dtypes=True))
            step.done(eng.memset(pair[:, :], 0.0))
            step.done(eng.affine_select(out=pair[:, :], in_=pair[:, :], compare_op=ALU.not_equal, fill=1.0, base=0,
                                        pattern=[[-1, C]], channel_multiplier=1))
            step.mark(eng.affine_select(out=pair[:, :], in_=pair[:, :], compare_op=ALU.not_equal, fill=1.0, base=-C,
                                        pattern=[[-1, C]], channel_multiplier=1))
            step.mark(eng.memset(stat[:, NH:NH + 4], -0.5))
            for t, c0, w in ((0, S0, K0), (1, S1, K1)):
                b = bias[:, c0:c0 + w]
                step.done(eng.iota(b, [[1, w]], base=-(NM + P * t), channel_multiplier=-1,
                                   allow_small_or_imprecise_dtypes=True))
            step.done(eng.tensor_scalar(s_sb[:, 0, :], bias[:, :], 0.0, -2.0, ALU.max, ALU.mult))
            step.done(eng.tensor_tensor(bias[:, :], bias[:, :], s_sb[:, 0, :], ALU.add))
            for t, c0 in ((0, S0), (1, S1)):
                late = c0 + NM + P * t + CHUNK
                step.done(eng.memset(bias[0:CHUNK, late:late + CHUNK], -1e30))
            step.mark(eng.memset(u_pad[:, 0:CONVW - 1], 0.0))
            step.mark(eng.iota(stat[:, 86:88], [[P, NT]], base=1, channel_multiplier=1,
                               allow_small_or_imprecise_dtypes=True))
            step.mark(eng.iota(tok_no[:, :], [[1, TX]], base=1, channel_multiplier=0,
                               allow_small_or_imprecise_dtypes=True))
            step.mark(eng.iota(stat[:, 88:92], [[-1, 4]], base=4, channel_multiplier=0,
                               allow_small_or_imprecise_dtypes=True))
            step.wait()
            eng.memset(stat[:, 92:93], 0.0).then_inc(consts_ready, 1)
            eng.wait_ge(ms_ready, 1)
            eng.tensor_tensor(stat[:, RSTD:RSTD + 2], stat[:, RSTD:RSTD + 2], stat[:, NH:NH + 2], ALU.pow)\
               .then_inc(rstd_ready, 1)
            eng.tensor_tensor(stat[0:NM, RSTD + 2:RSTD + 3], stat[0:NM, RSTD + 2:RSTD + 3], stat[0:NM, NH:NH + 1],
                              ALU.pow).then_inc(rstd_ready, 1)

            def o_power(h):
                eng.wait_ge(o_ms, h + 1)
                eng.tensor_tensor(stat[:, ORS:ORS + NT], stat[:, ORS:ORS + NT], stat[:, NH:NH + NT], ALU.pow)\
                   .then_inc(o_rstd, 1)

            with eng.Fori(0, HEADS) as h:
                o_power(h)

            def lru(i, b):
                g = 2 * i + b
                yg = yg_t[:, b, :]
                eng.wait_ge(acc_out, LRU0 + 2 * g + 2)
                at_least(eng, lru_ready, g - 1)
                step.done(eng.tensor_tensor(gl1[:, b, :], yg, yg, ALU.mult))
                apart(eng)
                step.done(eng.tensor_scalar(gl1[:, b, :], gl1[:, b, :], 0.044715, 1.0, ALU.mult, ALU.add))
                eng.tensor_tensor(gl1[:, b, :], gl1[:, b, :], yg, ALU.mult).then_inc(gelu_in, 1)
                eng.wait_ge(gelu_th, g + 1)
                apart(eng)
                step.done(eng.tensor_scalar(gl2[:, b, :], gl2[:, b, :], 1.0, 0.5, ALU.add, ALU.mult))
                eng.tensor_tensor(gl1[:, b, :], gl2[:, b, :], yg, ALU.mult).then_inc(gelu_ready, 1)

            def lru_pair(i):
                lru(i, 0)
                lru(i, 1)

            lru_pair(0)
            looped(eng, step, 1, LB // 2 - 1, lru_pair, 6)

            def keep(m, b):
                eng.wait_ge(h_ready, m + 1)
                eng.tensor_tensor(hg[:, :, ds(m * P, P)], h_s[b][:, :, :],
                                  g2b[:, ds(m * P, P)].unsqueeze(1).to_broadcast([P, NT, P]), ALU.mult)
                eng.tensor_copy(h_res[:, :, ds(m * P, P)], h_s[b][:, :, :]).then_inc(h_kept, 1)

            eng.wait_ge(mix_hi_ready, KC)
            eng.wait_ge(mix_lo_ready, KC)
            eng.wait_ge(g2b_in, 16)
            with eng.Fori(0, N_OUT // 2) as i:
                for b in range(2):
                    keep(2 * i + b, b)
            eng.wait_ge(h_ms, 1)
            eng.tensor_tensor(stat[:, HRS:HRS + NT], stat[:, HRS:HRS + NT], stat[:, NH:NH + NT], ALU.pow)\
               .then_inc(h_rstd, 1)

            eng.wait_ge(hn_scaled, 1)
            eng.tensor_tensor(hn_lo[:, 0, :, :], hn_0[:, :, :], hn_hi[:, 0, :, :].bitcast(F32), ALU.subtract)\
               .then_inc(hn_lo_ready, 1)

            def m_low(k, s):
                eng.wait_ge(m_hi_ready, PARTS * k + s + 1)
                n = s % SLOTS
                eng.tensor_tensor(m_lo[n][:, :], m_raw[n][:, :], m_hi[n][:, :].bitcast(F32), ALU.subtract)\
                   .then_inc(m_lo_pool, 1)

            def unit(k):
                for s in POOL_PARTS:
                    m_low(k, s)

            unit(0)
            with eng.Fori(1, NE) as k:
                unit(k)
            eng.wait_ge(tab_ready, 1)
            units = eng.value_load(tab_i[0:1, N_TAB:N_TAB + 1], min_val=NE, max_val=NE + MORE)
            with eng.Fori(NE, NE + MORE) as k:
                with eng.If(units > k):
                    unit(k)
            for t in range(NT):
                eng.wait_ge(y_ms, t + 1)
                eng.tensor_tensor(stat[:, YRS + t:YRS + t + 1], stat[:, YRS + t:YRS + t + 1], stat[:, NH:NH + 1], ALU.pow)\
                   .then_inc(y_rstd, 1)

        @block.scalar
        def _(eng):
            for t in range(NT):
                eng.wait_ge(x_in[t], 16)
                eng.activation(junk[:, :], h_res[:, t, :], ACT.Square, accum_out=stat[:, SQ + t:SQ + t + 1])\
                   .then_inc(sq_ready, 1)
                eng.wait_ge(sq_ready, t + 1)

            def hi(n, s, use):
                eng.wait_ge(raw_in[s], 16 * use)
                eng.activation(w_hi[s][:, :, :], raw[s][:, :, :], ACT.Copy).then_inc(hi_ready, 1)

            hi(0, 0, 1)
            eng.wait_ge(rstd_ready, 2)
            eng.activation(xn[:, 1, :], h_res[:, 1, :], ACT.Copy, scale=stat[:, RSTD + 1:RSTD + 2]).then_inc(xn1_ready, 1)
            eng.wait_ge(cols_ready, 1)
            for c in range(KC):
                eng.wait_ge(xt_turned, c + 1)
                eng.activation(xt_hi[:, c, :], ps[:, 1 + c % TURN_BANKS, 0:T], ACT.Copy,
                               scale=col[:, ROW_G1 + c:ROW_G1 + c + 1]).then_inc(xt_hi_ready, 1)
                if c == 9:
                    hi(1, 1, 1)
            hi(2, 2, 1)
            eng.wait_ge(sp_e_in, 1)
            eng.activation(sp[:, 1, :], sp[:, 0, :], ACT.Exp).then_inc(sp_e_out, 1)
            eng.activation(stat[:, LP:LP + 2], stat[:, LP:LP + 2], ACT.Exp).then_inc(sp_e_out, 1)

            def o_squares(h):
                eng.wait_ge(o_done, h + 1)
                for t in range(NT):
                    ins = eng.activation(junk_a[:, t, :], ps[:, 7, TX + t * P:TX + (t + 1) * P], ACT.Square,
                                         accum_out=stat[:, OSQ + t:OSQ + t + 1])
                    ins.then_inc(o_sq, 1)

            def mix_high(h):
                eng.wait_ge(o_turned, h + 1)
                eng.activation(mix_hi[:, ds(LB + h, 1), :].rearrange("p a t -> p (a t)"), ps[:, 6, 0:TX], ACT.Copy,
                               scale=sg[:, 0:1]).then_inc(mix_hi_ready, 1)

            def probs(h):
                for m in range(2):
                    for t, c0, w in ((0, S0, K0), (1, S1, K1)):
                        eng.wait_ge(max_ready, 2 * h + t + 1)
                        k = 2 * m + t
                        eng.activation(s_sb[:, m, c0:c0 + w], s_sb[:, m, c0:c0 + w], ACT.Exp,
                                       bias=stat[:, NMAX + k:NMAX + k + 1],
                                       accum_out=stat[:, L + k:L + k + 1]).then_inc(probs_ready, 1)

            def qkv(h):
                n = 3 * h
                if not is0(h):
                    hi(n + 2, 2, h + 1)
                eng.wait_ge(chunk_done, n + 1)
                eng.activation(q_t[:, :], ps[:, 0, 0:TX], ACT.Copy).then_inc(acc_out, 1)
                if not is0(h):
                    o_squares(h - 1)
                eng.wait_ge(chunk_done, n + 2)
                eng.activation(k_t[:, :], ps[:, 1, 0:T], ACT.Copy).then_inc(acc_out, 1)
                hi(n + 3, 0, h + 2)
                hi(n + 4, 1, h + 2)
                probs(h)
                if not is0(h):
                    mix_high(h - 1)
                eng.wait_ge(chunk_done, n + 3)
                eng.activation(v_t[:, :], ps[:, 2, 0:T], ACT.Copy).then_inc(acc_out, 1)

            qkv(0)
            with eng.Fori(1, HEADS) as h:
                qkv(h)

            def gelu_tanh(g, b):
                eng.wait_ge(gelu_in, g + 1)
                eng.activation(gl2[:, b, :], gl1[:, b, :], ACT.Tanh, scale=0.7978845608028654).then_inc(gelu_th, 1)

            def mix_lru(g):
                eng.wait_ge(lru_ready, g + 1)
                eng.activation(mix_hi[:, ds(g, 1), :].rearrange("p a t -> p (a t)"), lru_f[:, :], ACT.Copy)\
                   .then_inc(mix_hi_ready, 1)

            def lru(i, b):
                g = 2 * i + b
                n = LRU0 + 2 * g
                peeled = is0(i)

                def split(j):
                    if b == 0:
                        hi(n + 2 + j, 2 + j, chunk_use(2 + j, "lru", i))
                    elif isinstance(i, int) and i == LB // 2 - 1:
                        hi(n + 2 + j, j, chunk_use(j, "out", 0))
                    else:
                        hi(n + 2 + j, j, chunk_use(j, "lru", i + 1))

                split(0)
                if not peeled:
                    mix_lru(g - 2)
                eng.wait_ge(chunk_done, n + 1)
                at_least(eng, xc_ready, g)
                eng.activation(u_pad[:, CONVW - 1:], ps[:, 0, 0:T], ACT.Copy).then_inc(acc_out, 1)
                if peeled and b == 0:
                    o_squares(HEADS - 1)
                split(1)
                eng.wait_ge(gates_done, g + 1)
                at_least(eng, ix_ready, g)
                for k in range(2):
                    eng.activation(th_ri[:, k, :], ps[:, 3 + k, 0:T], ACT.Tanh, bias=halfb[:, ds(k * LB + g, 1)],
                                   scale=0.5).then_inc(th_ri_ready, 1)
                eng.wait_ge(th_ri_ready, 2 * g + 1)
                at_least(eng, scanned, g)
                eng.activation(a_t[:, :], th_ri[:, 0, :], ACT.Exp, bias=sp[:, 6, ds(g, 1)], scale=sp[:, 6, ds(g, 1)])\
                   .then_inc(at_ready, 1)
                eng.activation(tg[:, :], th_ri[:, 0, :], ACT.Tanh, bias=sp[:, 7, ds(g, 1)], scale=sp[:, 7, ds(g, 1)])\
                   .then_inc(at_ready, 1)
                if not (peeled and b == 0):
                    gelu_tanh(g - 1, 1 - b)
                eng.wait_ge(q_ready, g + 1)
                eng.activation(lr3[:, :], lr2[:, :], ACT.Sqrt, scale=0.25).then_inc(sqrt_ready, 1)
                if peeled and b == 0:
                    mix_high(HEADS - 1)
                eng.wait_ge(chunk_done, n + 2)
                at_least(eng, gelu_ready, g - 1)
                eng.activation(yg_t[:, b, :], ps[:, 1, 0:TX], ACT.Copy).then_inc(acc_out, 1)

            lru(0, 0)
            lru(0, 1)
            with eng.Fori(1, LB // 2 - 1) as i:
                lru(i, 0)
                lru(i, 1)
            lru(LB // 2 - 1, 0)
            lru(LB // 2 - 1, 1)

            def h_squares(m, b):
                eng.wait_ge(h_ready, m + 1)
                for t in range(NT):
                    eng.activation(ps[:, 7, (NT * b + t) * P:(NT * b + t + 1) * P], h_s[b][:, t, :], ACT.Square,
                                   accum_out=stat[:, ds(HSQ + t * N_OUT + m, 1)]).then_inc(h_sq, 1)

            def project(i, s, last=False):
                m = RING * i + s
                n = OUT0 + m
                eng.wait_ge(chunk_done, n + 1)
                at_least(eng, o_back, m - 1)
                eng.activation(o_t[s % 2][:, :], ps[:, s % 2, 0:TX], ACT.Copy).then_inc(acc_out, 1)
                if s == 0:
                    hi(n + 3, 3, chunk_use(3, "out", i))
                elif not last:
                    hi(n + 3, s - 1, chunk_use(s - 1, "out", i + 1))
                if not (is0(i) and s == 0):
                    h_squares(m - 1, (s - 1) % 2)

            mix_lru(LB - 2)
            gelu_tanh(LB - 1, 1)
            hi(OUT0 + 2, 2, chunk_use(2, "out", 0))
            mix_lru(LB - 1)
            for s in range(RING):
                project(0, s)
            with eng.Fori(1, N_OUT // RING - 1) as i:
                for s in range(RING):
                    project(i, s)
            for s in range(RING):
                project(N_OUT // RING - 1, s, last=True)
            h_squares(N_OUT - 1, 1)
            eng.wait_ge(h_rstd, 1)
            eng.wait_ge(h_kept, N_OUT)

            def normed(out, t, signal):
                eng.activation(out, hg[:, t, :].rearrange("p (q c) -> p c q", c=KC), ACT.Copy,
                               scale=stat[:, HRS + t:HRS + t + 1]).then_inc(signal, 1)

            normed(hn_hi[:, 0, :, :], 0, hn_hi_ready)
            normed(hn_0[:, :, :], 0, hn_scaled)
            normed(hn_hi[:, 1, :, :], 1, hn_hi_ready)
            eng.activation(ident_r[:, :], ident[:, :], ACT.Copy).then_inc(ident_r_ready, 1)
            eng.wait_ge(rt_max, 1)
            eng.activation(rt[:, 2, :, 0:NG], rt[:, 1, :, 0:NG], ACT.Exp).then_inc(rt_exp, 1)
            eng.wait_ge(rt_max, 2)
            eng.activation(rt[:, 10, :, 1:2], rt[:, 10, :, 0:1], ACT.Exp).then_inc(rt_exp, 1)

            def m_high(k, *parts):
                for s in parts:
                    eng.wait_ge(slot_in[s % SLOTS], 16 * (PARTS // SLOTS * k + s // SLOTS + 1))
                    eng.activation(m_hi[s % SLOTS][:, :], m_raw[s % SLOTS][:, :], ACT.Copy).then_inc(m_hi_ready, 1)

            def y_high(k):
                eng.wait_ge(part_used, PARTS * k)
                for j in range(2):
                    eng.activation(y_hi[:, 2 * j:2 * j + 2, :], ps[:, 3 + 2 * j:5 + 2 * j, :], ACT.Copy)\
                       .then_inc(y_hi_ready, 1)

            def x_rows_out(k):
                eng.wait_ge(gathered, 2 * k + 1)
                at_least(eng, x_turned, 4 * k)
                eng.activation(x_s[:, 0:D // 2].rearrange("p (b n) -> p b n", b=2), ps[:, 3:5, :], ACT.Copy)\
                   .then_inc(x_rows_left, 1)

            def x_out(k, j):
                eng.wait_ge(x_turned, 4 * k + j + 1)
                eng.activation(x_hl[:, 4 * j:4 * j + 4, :, :].rearrange("p c h s -> p (c h s)"), ps[:, 7, :], ACT.Copy)\
                   .then_inc(x_even, 1)

            def unit(k):
                if not is0(k):
                    m_high(k, *range(0, 6))
                    y_high(k)
                    m_high(k, 6, 7)
                m_high(k, *range(8, 14))
                eng.wait_ge(part_used, PARTS * k + 8)
                eng.activation(gu_sb[:, 0, :], ps[:, 0, :], ACT.Copy).then_inc(g_copied, 1)
                m_high(k, *range(14, 18))
                eng.wait_ge(g_turned, k + 1)
                eng.activation(th[:, :, :].rearrange("p f c -> p (f c)"), ps[:, 2, 0:FC * C], ACT.Tanh, scale=0.5)\
                   .then_inc(th_ready, 1)
                x_rows_out(k + 1)
                m_high(k, *range(18, 21))
                eng.wait_ge(part_used, PARTS * k + 16)
                eng.activation(gu_sb[:, 1, :], ps[:, 1, :], ACT.Copy).then_inc(u_copied, 1)
                x_out(k + 1, 0)
                eng.wait_ge(h_f_ready, k + 1)
                eng.activation(h_hl[:, :, 0, :], h_f[:, :, :], ACT.Copy).then_inc(h_hi_ready, 1)
                x_out(k + 1, 2)
                m_high(k, 21, 22, 23)

            m_high(0, *range(0, 5))
            x_rows_out(0)
            x_out(0, 0)
            x_out(0, 2)
            m_high(0, 5, 6, 7)
            unit(0)
            with eng.Fori(1, NE) as k:
                unit(k)
            eng.wait_ge(tab_ready, 1)
            units = eng.value_load(tab_i[0:1, N_TAB:N_TAB + 1], min_val=NE, max_val=NE + MORE)
            with eng.Fori(NE, NE + MORE) as k:
                with eng.If(units > k):
                    unit(k)
            y_high(units)
            final = eng.value_load(tab_i[0:1, N_TAB + 1:N_TAB + 2], min_val=NE - 1, max_val=NE + MORE - 1)
            for t in range(NT):
                eng.wait_ge(added, 4 * final + 2 * t + 2)
                apart(eng)
                eng.activation(yout[:, t, :], h_res[:, t, :], ACT.Square,
                               accum_out=stat[:, YSQ + t:YSQ + t + 1]).then_inc(y_sq, 1)

        @block.vector
        def _(eng):
            step = Steps(eng, dve_step)
            eng.wait_ge(x_in[2], 16)
            step.done(eng.scalar_tensor_tensor(out=xn[0:NM, 0, :], in0=metan[:, :], scalar=1.0, in1=metan[:, :],
                                               op0=ALU.mult, op1=ALU.mult, accum_out=stat[0:NM, SQ + 2:SQ + 3]))
            step.done(eng.tensor_scalar(stat[0:NM, RSTD + 2:RSTD + 3], stat[0:NM, SQ + 2:SQ + 3], 1.0 / D, EPS,
                                        ALU.mult, ALU.add))
            eng.wait_ge(sq_ready, NT)
            eng.tensor_scalar(stat[:, RSTD:RSTD + 2], stat[:, SQ:SQ + 2], 1.0 / D, EPS, ALU.mult, ALU.add)\
               .then_inc(ms_ready, 1)
            eng.wait_ge(params_turned, 1)
            eng.tensor_copy(col[:, :], ps[:, 7, 0:N_ROWS]).then_inc(cols_ready, 1)
            eng.wait_ge(rstd_ready, 2)
            eng.tensor_scalar(metan[:, :], metan[:, :], stat[0:NM, RSTD + 2:RSTD + 3], None, ALU.mult)\
               .then_inc(xn_ready, 1)
            eng.tensor_scalar(xn[:, 0, :], h_res[:, 0, :], stat[:, RSTD:RSTD + 1], None, ALU.mult).then_inc(xn_ready, 1)

            def lo(n, s):
                eng.wait_ge(hi_ready, n + 1)
                eng.tensor_tensor(w_lo[s][:, :, :], raw[s][:, :, :], w_hi[s][:, :, :].bitcast(F32), ALU.subtract)\
                   .then_inc(lo_ready, 1)

            lo(0, 0)
            for c in range(KC):
                eng.wait_ge(xt_hi_ready, c + 1)
                eng.wait_ge(cols_ready, 1)
                eng.scalar_tensor_tensor(out=xt_lo[:, c, :], in0=ps[:, 1 + c % TURN_BANKS, 0:T],
                                         scalar=col[:, ROW_G1 + c:ROW_G1 + c + 1],
                                         in1=xt_hi[:, c, :].bitcast(F32), op0=ALU.mult, op1=ALU.subtract)\
                   .then_inc(xt_lo_ready, 1)
                if c == 12:
                    lo(1, 1)
            lo(2, 2)
            p = col[:, ROW_LA:ROW_LA + LB]
            step.done(eng.tensor_scalar(sp[:, 5, :], p, -1.0, None, ALU.mult))
            step.done(eng.tensor_tensor(sp[:, 0, :], p, sp[:, 5, :], ALU.min))
            eng.wait_ge(misc_in, 16 * 8)
            step.done(eng.tensor_tensor(lam_in[:, 0:2, :], lam_in[:, 0:2, :], lam_in[:, 2:4, :], ALU.mult))
            step.done(eng.tensor_reduce(stat[:, LP:LP + 2], lam_in[:, 0:2, :], AX.X, ALU.add))
            eng.tensor_scalar(sg[:, 0:1], col[:, ROW_SG:ROW_SG + 1], 1.0 - LAM_INIT, None, ALU.mult).then_inc(sp_e_in, 1)
            step.done(eng.tensor_scalar(halfb[:, :], col[:, ROW_BA:ROW_BA + 2 * LB], 0.5, None, ALU.mult))
            eng.wait_ge(sp_e_out, 2)
            step.done(eng.tensor_tensor(stat[:, LAM:LAM + 1], stat[:, LP + 1:LP + 2], stat[:, LP:LP + 1], ALU.subtract))
            step.done(eng.tensor_scalar(stat[:, NLAM:NLAM + 1], stat[:, LAM:LAM + 1], -LAM_INIT, None, ALU.add))
            step.done(eng.tensor_scalar(sp[:, 2, :], sp[:, 1, :], 2.0, None, ALU.add))
            step.done(eng.reciprocal(sp[:, 3, :], sp[:, 2, :]))
            step.done(eng.tensor_tensor(sp[:, 2, :], sp[:, 1, :], sp[:, 3, :], ALU.mult))
            step.done(eng.tensor_tensor(sp[:, 3, :], sp[:, 2, :], sp[:, 2, :], ALU.mult))
            step.done(eng.tensor_scalar(sp[:, 4, :], sp[:, 3, :], 1.0 / 17, 1.0 / 15, ALU.mult, ALU.add))
            for k in (13, 11, 9, 7, 5, 3, 1):
                step.done(eng.tensor_tensor(sp[:, 4, :], sp[:, 4, :], sp[:, 3, :], ALU.mult))
                step.done(eng.tensor_scalar(sp[:, 4, :], sp[:, 4, :], 1.0 / k, None, ALU.add))
            step.done(eng.tensor_tensor(sp[:, 4, :], sp[:, 4, :], sp[:, 2, :], ALU.mult))
            step.done(eng.tensor_scalar(sp[:, 5, :], sp[:, 5, :], 0.0, None, ALU.max))
            step.done(eng.scalar_tensor_tensor(out=sp[:, 5, :], in0=sp[:, 4, :], scalar=2.0, in1=sp[:, 5, :],
                                               op0=ALU.mult, op1=ALU.add))
            step.done(eng.tensor_scalar(sp[:, 6, :], sp[:, 5, :], -4.0, None, ALU.mult))
            step.done(eng.tensor_scalar(sp[:, 7, :], sp[:, 5, :], 4.0, None, ALU.mult))
            eng.wait_ge(consts_ready, 2)

            def v_rows(h):
                eng.wait_ge(v_turned, h + 1)
                eng.tensor_copy(v_tm[:, :, :], ps[:, 6, 0:TX].rearrange("p (t d) -> p t d", t=NT)).then_inc(v_out, 1)
                eng.tensor_copy(v_meta[:, :], ps[0:NM, 6, TX:TX + P]).then_inc(v_out, 1)

            def a_turn(h):
                eng.wait_ge(a_turned, h + 1)
                eng.tensor_copy(at_x[:, 0, :], ps[:, 5, 0:TX]).then_inc(a_out, 1)
                eng.tensor_copy(at_x[:, 1, P:TX], ps[:, 5, TX + P:2 * TX]).then_inc(a_out, 1)
                eng.tensor_copy(at_m[:, :], ps[0:NM, 7, 0:TX]).then_inc(a_out, 1)

            def o_norm(h):
                eng.wait_ge(o_sq, 2 * h + 2)
                eng.tensor_scalar(stat[:, ORS:ORS + NT], stat[:, OSQ:OSQ + NT], 1.0 / P, EPS, ALU.mult, ALU.add)\
                   .then_inc(o_ms, 1)
                eng.wait_ge(o_rstd, h + 1)
                eng.tensor_tensor(o_sb[:, :, :], ps[:, 7, TX:2 * TX].rearrange("p (t d) -> p t d", t=NT),
                                  stat[:, ORS:ORS + NT].unsqueeze(2).to_broadcast([P, NT, P]), ALU.mult)\
                   .then_inc(o_out, 1)

            def softmax_in(h):
                step.done(eng.tensor_scalar(bias[:, :], bias[:, :], 0.5, None, ALU.mult))
                eng.wait_ge(scores_done, h + 1)
                eng.scalar_tensor_tensor(out=s_sb[:, :, :], in0=ps[:, 3:5, 0:SW], scalar=DH ** -0.5,
                                         in1=bias[:, :].unsqueeze(1).to_broadcast([P, 2, SW]), op0=ALU.mult,
                                         op1=ALU.add).then_inc(biased, 1)
                eng.wait_ge(biased, h + 1)
                for t, c0, w in ((0, S0, K0), (1, S1, K1)):
                    eng.tensor_reduce(stat[:, NMAX + t:NMAX + t + 3:2], s_sb[:, :, c0:c0 + w], AX.X, ALU.max,
                                      negate=True).then_inc(max_ready, 1)

            def softmax_out(h):
                eng.wait_ge(probs_ready, 4 * h + 4)
                step.done(eng.reciprocal(stat[:, RL:RL + 4], stat[:, L:L + 4]))
                step.done(eng.tensor_scalar(stat[:, CM:CM + 2], stat[:, RL + 2:RL + 4], stat[:, NLAM:NLAM + 1], None,
                                            ALU.mult))
                for t, c0, w in ((0, S0, K0), (1, S1, K1)):
                    step.mark(eng.tensor_scalar(a_sb[:, c0:c0 + w], s_sb[:, 0, c0:c0 + w],
                                                stat[:, RL + t:RL + t + 1], None, ALU.mult))
                step.wait()
                for t, c0, w in ((0, S0, K0), (1, S1, K1)):
                    eng.scalar_tensor_tensor(out=a_sb[:, c0:c0 + w], in0=s_sb[:, 1, c0:c0 + w],
                                             scalar=stat[:, CM + t:CM + t + 1], in1=a_sb[:, c0:c0 + w],
                                             op0=ALU.mult, op1=ALU.add).then_inc(a_ready, 1)

            def mix_low(h):
                eng.wait_ge(mix_hi_ready, h + 1)
                eng.scalar_tensor_tensor(out=mix_lo[:, ds(LB + h, 1), :].rearrange("p a t -> p (a t)"),
                                         in0=ps[:, 6, 0:TX], scalar=sg[:, 0:1],
                                         in1=mix_hi[:, ds(LB + h, 1), :].rearrange("p a t -> p (a t)").bitcast(F32),
                                         op0=ALU.mult, op1=ALU.subtract).then_inc(mix_lo_ready, 1)

            def qkv(h):
                n = 3 * h
                if not is0(h):
                    v_rows(h - 1)
                    lo(n + 2, 2)
                    a_turn(h - 1)
                    o_norm(h - 1)
                lo(n + 3, 0)
                softmax_in(h)
                lo(n + 4, 1)
                if not is0(h):
                    mix_low(h - 1)
                softmax_out(h)

            qkv(0)
            looped(eng, step, 1, HEADS - 1, qkv, 5)

            def finish(g, b):
                eng.wait_ge(gelu_ready, g + 1)
                eng.wait_ge(mix_lo_ready, HEADS + g)
                eng.tensor_tensor(lru_f[:, :], hs_t[:, b, NM:T], gl1[:, b, :], ALU.mult).then_inc(lru_ready, 1)

            def mix_lru_low(g):
                eng.wait_ge(mix_hi_ready, HEADS + g + 1)
                eng.tensor_tensor(mix_lo[:, ds(g, 1), :].rearrange("p a t -> p (a t)"), lru_f[:, :],
                                  mix_hi[:, ds(g, 1), :].rearrange("p a t -> p (a t)").bitcast(F32),
                                  ALU.subtract).then_inc(mix_lo_ready, 1)

            def lru(i, b):
                g = 2 * i + b
                n = LRU0 + 2 * g
                s = 2 * b
                peeled = is0(i)
                if peeled and b == 0:
                    v_rows(HEADS - 1)
                    lo(n + 2, 2)
                    a_turn(HEADS - 1)
                eng.wait_ge(acc_out, n + 1)
                for k in range(CONVW):
                    src = u_pad[:, CONVW - 1 - k:CONVW - 1 - k + T]
                    tap = col[:, ds(ROW_CW + k * LB + g, 1)]
                    if k == 0:
                        step.done(eng.tensor_scalar(xc[:, :], src, tap, col[:, ds(ROW_CB + g, 1)], ALU.mult, ALU.add))
                    else:
                        ins = eng.scalar_tensor_tensor(out=xc[:, :], in0=src, scalar=tap, in1=xc[:, :], op0=ALU.mult,
                                                       op1=ALU.add)
                        if k < CONVW - 1:
                            step.done(ins)
                ins.then_inc(xc_ready, 1)
                if peeled and b == 0:
                    o_norm(HEADS - 1)
                else:
                    lo(n + 2, (s + 2) % RING)
                if not peeled:
                    mix_lru_low(g - 2)
                lo(n + 3, (s + 3) % RING)
                eng.wait_ge(th_ri_ready, 2 * g + 2)
                eng.scalar_tensor_tensor(out=lr1[:, :], in0=th_ri[:, 1, :], scalar=1.0, in1=xc[:, :], op0=ALU.add,
                                         op1=ALU.mult).then_inc(ix_ready, 1)
                eng.wait_ge(at_ready, 2 * g + 2)
                step.done(eng.tensor_tensor(lr2[:, :], a_t[:, :], a_t[:, :], ALU.mult))
                eng.scalar_tensor_tensor(out=lr2[:, :], in0=lr2[:, :], scalar=1.0, in1=tg[:, :], op0=ALU.add,
                                         op1=ALU.mult).then_inc(q_ready, 1)
                if not (peeled and b == 0):
                    finish(g - 1, 1 - b)
                else:
                    mix_low(HEADS - 1)
                eng.wait_ge(sqrt_ready, g + 1)
                eng.wait_ge(ix_ready, g + 1)
                step.done(eng.tensor_tensor(lr3[:, :], lr3[:, :], lr1[:, :], ALU.mult))
                eng.tensor_tensor_scan(hs_t[:, b, :], a_t[:, :], lr3[:, :], 0.0, ALU.mult, ALU.add).then_inc(scanned, 1)
                eng.wait_ge(scanned, g + 1)

            def lru_pair(i):
                lru(i, 0)
                lru(i, 1)

            lru_pair(0)
            looped(eng, step, 1, LB // 2 - 1, lru_pair, 10)
            mix_lru_low(LB - 2)
            finish(LB - 1, 1)
            mix_lru_low(LB - 1)
            lo(OUT0 + 2, 2)

            def residual(m, b):
                eng.wait_ge(o_back, m + 1)
                at_least(eng, h_kept, m - 1)
                at_least(eng, h_sq, 2 * (m - 1))
                at_least(eng, h_turned, m - 1)
                eng.tensor_tensor(h_s[b][:, :, :], ps[:, 3, 0:TX].rearrange("p (t d) -> p t d", t=NT),
                                  h_res[:, :, ds(m * P, P)], ALU.add).then_inc(h_ready, 1)
                eng.wait_ge(h_turned, m + 1)
                at_least(eng, logits_done, m - 1)
                eng.tensor_scalar(h_tt[b][:, :], ps[:, 4, 0:TX], col[:, ds(ROW_G2 + m, 1)], None, ALU.mult)\
                   .then_inc(h_t_ready, 1)

            def project(i, s, last=False):
                m = RING * i + s
                if not (is0(i) and s == 0):
                    residual(m - 1, (s - 1) % 2)
                if not (last and s >= 2) and not (is0(i) and s == 0):
                    lo(OUT0 + m + 2, (s + 2) % RING)

            for s in range(RING):
                project(0, s)
            with eng.Fori(1, N_OUT // RING - 1) as i:
                for s in range(RING):
                    project(i, s)
            for s in range(RING):
                project(N_OUT // RING - 1, s, last=True)
            residual(N_OUT - 1, 1)

            eng.wait_ge(h_sq, 2 * N_OUT)
            step.done(eng.tensor_reduce(stat[:, HRS:HRS + NT],
                                        stat[:, HSQ:HSQ + NT * N_OUT].rearrange("p (t m) -> p t m", t=NT), AX.X, ALU.add))
            eng.tensor_scalar(stat[:, HRS:HRS + NT], stat[:, HRS:HRS + NT], 1.0 / D, EPS, ALU.mult, ALU.add)\
               .then_inc(h_ms, 1)
            eng.wait_ge(h_rstd, 1)
            eng.wait_ge(logits_done, N_OUT)
            lg = rt[:, 0, :, 0:NG]
            le = rt[:, 3, :, :]
            for t in range(NT):
                step.mark(eng.scalar_tensor_tensor(out=rt[:, 0, t, 0:NG], in0=ps[:, 5 + t, 0:NG],
                                                   scalar=stat[:, HRS + t:HRS + t + 1], in1=rb[:, 0:NG],
                                                   op0=ALU.mult, op1=ALU.add))
                step.mark(eng.scalar_tensor_tensor(out=rt[:, 3, t, :], in0=ps[:, 5 + t, NG:NG + NE],
                                                   scalar=stat[:, HRS + t:HRS + t + 1], in1=rb[:, NG:NG + NE],
                                                   op0=ALU.mult, op1=ALU.add))
            step.wait()
            prio = stat[:, 88:92].unsqueeze(1).to_broadcast([P, NT, 4])

            def first_max(v, m, hot, work):
                step.done(eng.tensor_reduce(m, v, AX.X, ALU.max))
                for t in range(NT):
                    step.mark(eng.scalar_tensor_tensor(out=work[:, t, :], in0=v[:, t, :], scalar=m[:, t, :],
                                                       in1=stat[:, 88:92], op0=ALU.is_equal, op1=ALU.mult))
                step.wait()
                step.done(eng.tensor_reduce(rt[:, 17, :, 0:1], work, AX.X, ALU.max))
                step.done(eng.tensor_tensor(hot, prio, rt[:, 17, :, 0:1].to_broadcast([P, NT, 4]), ALU.is_equal))

            gmax = rt[:, 4, :, 0:1]
            ghot = rt[:, 5, :, 0:NG]
            first_max(lg, gmax, ghot, rt[:, 6, :, 0:NG])
            eng.tensor_tensor(rt[:, 1, :, 0:NG], lg, gmax.to_broadcast([P, NT, NG]), ALU.subtract).then_inc(rt_max, 1)
            for t in range(NT):
                step.mark(eng.tensor_tensor(rt[:, 7, t, :].rearrange("p (g j) -> p g j", g=NG),
                                            rt[:, 3, t, :].rearrange("p (g j) -> p g j", g=NG),
                                            rt[:, 5, t, 0:NG].unsqueeze(2).to_broadcast([P, NG, EPG]), ALU.mult))
            step.wait()
            lin = rt[:, 8, :, 0:EPG]
            for t in range(NT):
                step.mark(eng.tensor_reduce(rt[:, 8, t, 0:EPG], rt[:, 7, t, :].rearrange("p (g j) -> p j g", g=NG),
                                            AX.X, ALU.add))
            step.wait()
            hot1, hot2 = rt[:, 9, :, 0:EPG], rt[:, 11, :, 0:EPG]
            m1, m2 = rt[:, 12, :, 0:1], rt[:, 12, :, 1:2]
            first_max(lin, m1, hot1, rt[:, 6, :, 0:EPG])
            step.done(eng.scalar_tensor_tensor(out=rt[:, 13, :, 0:EPG], in0=hot1, scalar=-1e30, in1=lin,
                                               op0=ALU.mult, op1=ALU.add))
            first_max(rt[:, 13, :, 0:EPG], m2, hot2, rt[:, 6, :, 0:EPG])
            eng.tensor_tensor(rt[:, 10, :, 0:1], m2, m1, ALU.subtract).then_inc(rt_max, 1)
            for t in range(NT):
                for k, hot in ((14, 9), (15, 11)):
                    step.mark(eng.tensor_tensor(rt[:, k, t, :].rearrange("p (g j) -> p g j", g=NG),
                                                rt[:, 5, t, 0:NG].unsqueeze(2).to_broadcast([P, NG, EPG]),
                                                rt[:, hot, t, 0:EPG].unsqueeze(1).to_broadcast([P, NG, EPG]),
                                                ALU.mult))
            step.wait()
            member = rt[:, 16, :, :]
            eng.tensor_tensor(member, rt[:, 14, :, :], rt[:, 15, :, :], ALU.add).then_inc(members, 1)
            eng.wait_ge(members, 1)
            eng.wait_ge(hn_hi_ready, NT)
            eng.scalar_tensor_tensor(out=hn_lo[:, 1, :, :], in0=hg[:, 1, :].rearrange("p (q c) -> p c q", c=KC),
                                     scalar=stat[:, HRS + 1:HRS + 2], in1=hn_hi[:, 1, :, :].bitcast(F32),
                                     op0=ALU.mult, op1=ALU.subtract).then_inc(hn_lo_ready, 1)
            eng.wait_ge(ranks_done, 1)
            rank = rt[:, 19, :, :]
            step.done(eng.scalar_tensor_tensor(out=rank, in0=ps[:, 3, 0:NT * NE].rearrange("p (t e) -> p t e", t=NT),
                                               scalar=1.0, in1=member, op0=ALU.add, op1=ALU.mult))
            step.done(eng.tensor_scalar(rank, rank, -1.0, None, ALU.add))
            for t in range(NT):
                for side in (0, 3):
                    step.mark(eng.tensor_scalar(sel[:, t, side * C:(side + 1) * C], slot_no[:, :], -1.0, None,
                                                ALU.is_equal))
            n_over = (TX // C - 1) * NE
            w = rt[:, :, :, :].rearrange("p a b c -> p (a b c)")
            totals = w[:, 5 * n_over:5 * n_over + NE]
            step.mark(eng.tensor_copy(totals, ps[:, 4, 0:NE]))
            step.wait()

            def select(e, first):
                for t in range(NT):
                    eng.tensor_scalar(sel[:, t, C:3 * C].rearrange("p (a s) -> p a s", a=2),
                                      slot_no[:, :].unsqueeze(1).to_broadcast([P, 2, C]), first,
                                      rank[:, t, ds(e, 1)], ALU.add, ALU.is_equal).then_inc(sel_ready, 1)

            def list_out(k):
                eng.wait_ge(listed, k + 1)
                at_least(eng, back_ready, k)
                eng.tensor_copy(tok[:, :], ps[:, 7, 0:1]).then_inc(tok_ready, 1)

            def turn_back_list(k):
                eng.wait_ge(tok_ready, k + 1)
                eng.tensor_scalar(back[:, :], tok_no[:, :], tok[:, 0:1], None, ALU.is_equal).then_inc(back_ready, 1)

            def x_rows_out(k):
                eng.wait_ge(gathered, 2 * k + 2)
                at_least(eng, x_turned, 4 * k)
                eng.tensor_copy(x_s[:, D // 2:].rearrange("p (b n) -> p b n", b=2), ps[:, 5:7, :])\
                   .then_inc(x_rows_right, 1)

            def x_out(k, j):
                eng.wait_ge(x_turned, 4 * k + j + 1)
                eng.tensor_copy(x_hl[:, 4 * j:4 * j + 4, :, :].rearrange("p c h s -> p (c h s)"), ps[:, 0, :])\
                   .then_inc(x_odd, 1)

            zero = stat[:, 92:93]
            select(0, zero)
            list_out(0)

            def m_low(k, *parts):
                for s in parts:
                    n = s % SLOTS
                    eng.wait_ge(m_hi_ready, PARTS * k + s + 1)
                    eng.tensor_tensor(m_lo[n][:, :], m_raw[n][:, :], m_hi[n][:, :].bitcast(F32), ALU.subtract)\
                       .then_inc(m_lo_dve, 1)

            def y_low(k):
                for j in range(2):
                    eng.wait_ge(y_hi_ready, 2 * k + j + 1)
                    eng.tensor_tensor(y_lo[:, 2 * j:2 * j + 2, :], ps[:, 3 + 2 * j:5 + 2 * j, :],
                                      y_hi[:, 2 * j:2 * j + 2, :].bitcast(F32), ALU.subtract).then_inc(y_lo_ready, 1)

            def add(k, t):
                for j in range(2):
                    eng.wait_ge(combined, 4 * k + 2 * t + j + 1)
                    h = h_res[:, t, j * D // 2:(j + 1) * D // 2].rearrange("p (b n) -> p b n", b=2)
                    eng.scalar_tensor_tensor(out=h, in0=ps[:, 3 + 2 * j:5 + 2 * j, :], scalar=gates[:, t, ds(k, 1)],
                                             in1=h, op0=ALU.mult, op1=ALU.add).then_inc(added, 1)

            m_low(0, 0, 2, 3)
            x_rows_out(0)
            select(1, zero)
            x_out(0, 1)
            x_out(0, 3)
            eng.wait_ge(rt_exp, 2)
            step.done(eng.tensor_reduce(rt[:, 17, :, 1:2], rt[:, 2, :, 0:NG], AX.X, ALU.add))
            step.done(eng.tensor_scalar(rt[:, 17, :, 2:3], rt[:, 10, :, 1:2], 1.0, None, ALU.add))
            step.done(eng.tensor_tensor(rt[:, 17, :, 3:4], rt[:, 17, :, 1:2], rt[:, 17, :, 2:3], ALU.mult))
            w12 = stat[:, W12:W12 + 4].rearrange("p (t k) -> p t k", k=2)
            step.done(eng.reciprocal(w12[:, :, 0:1], rt[:, 17, :, 3:4]))
            step.done(eng.tensor_tensor(w12[:, :, 1:2], w12[:, :, 0:1], rt[:, 10, :, 1:2], ALU.mult))
            for t in range(NT):
                step.mark(eng.tensor_scalar(gates[:, t, 0:NE], rt[:, 15, t, :], stat[:, W12 + 2 * t + 1:W12 + 2 * t + 2],
                                            None, ALU.mult))
            step.wait()
            for t in range(NT):
                step.mark(eng.scalar_tensor_tensor(out=gates[:, t, 0:NE], in0=rt[:, 14, t, :],
                                                   scalar=stat[:, W12 + 2 * t:W12 + 2 * t + 1],
                                                   in1=gates[:, t, 0:NE], op0=ALU.mult, op1=ALU.add))
            step.wait()
            flags, upto, unit_of, junk_w, none = (w[:, j * n_over:(j + 1) * n_over] for j in range(5))

            def number_units():
                for r in range(TX // C - 1):
                    step.mark(eng.tensor_scalar(flags[:, r * NE:(r + 1) * NE], totals, float(C * (r + 1)), None,
                                                ALU.is_gt))
                step.mark(eng.memset(none, 0.0))
                step.wait()
                step.done(eng.tensor_tensor_scan(upto, flags, none, 0.0, ALU.add, ALU.add))
                step.done(eng.scalar_tensor_tensor(out=unit_of, in0=upto, scalar=float(NE - 1), in1=flags, op0=ALU.add,
                                                   op1=ALU.mult))

            def further_units(*units):
                for j in units:
                    for k, row in ((0, expert_no), (1, first_no)):
                        step.done(eng.scalar_tensor_tensor(out=junk_w, in0=unit_of, scalar=unit_no[:, j:j + 1],
                                                           in1=row[:, :], op0=ALU.is_equal, op1=ALU.mult,
                                                           accum_out=tab[:, k, j:j + 1]))

            def close_table():
                step.done(eng.tensor_scalar(tab[:, 1, :], tab[:, 1, :], BIG, None, ALU.add))
                step.mark(eng.tensor_copy(tab_i[:, 0:N_TAB], tab[:, 0, :]))
                for j in range(2):
                    step.mark(eng.tensor_scalar(tab_i[:, N_TAB + j:N_TAB + j + 1], upto[:, n_over - 1:n_over],
                                                float(NE - j), None, ALU.add))
                step.wait()
                eng.memset(stat[:, 94:95], 0.0).then_inc(tab_ready, 1)

            flat_t = th[:, :, :].rearrange("p f c -> p (f c)")
            flat_h = h_f[:, :, :].rearrange("p f c -> p (f c)")

            def unit(k, following):
                if not is0(k):
                    m_low(k, 0, 2, 3)
                m_low(k, 5)
                if not is0(k):
                    y_low(k - 1)
                m_low(k, 6, 8, 9)
                if not is0(k):
                    add(k - 1, 0)
                m_low(k, 11)
                if not is0(k):
                    add(k - 1, 1)
                turn_back_list(k)
                m_low(k, 12, 14, 15, 17)
                eng.wait_ge(th_ready, k + 1)
                eng.scalar_tensor_tensor(out=flat_t, in0=flat_t, scalar=1.0, in1=ps[:, 2, 0:FC * C],
                                         op0=ALU.add, op1=ALU.mult).then_inc(gated, 1)
                x_rows_out(k + 1)
                list_out(k + 1)
                following()
                m_low(k, 18, 20)
                x_out(k + 1, 1)
                eng.wait_ge(gated, k + 1)
                eng.wait_ge(u_turned, k + 1)
                eng.scalar_tensor_tensor(out=flat_h, in0=flat_t, scalar=0.5, in1=ps[:, 2, FC * C:2 * FC * C],
                                         op0=ALU.mult, op1=ALU.mult).then_inc(h_f_ready, 1)
                eng.wait_ge(h_hi_ready, k + 1)
                eng.tensor_tensor(h_hl[:, :, 1, :], h_f[:, :, :], h_hl[:, :, 0, :].bitcast(F32), ALU.subtract)\
                   .then_inc(h_ready_e, 1)
                x_out(k + 1, 3)
                m_low(k, 21, 23)

            unit(0, lambda: select(2, zero))
            number_units()
            further_units(0, 1)
            unit(1, lambda: select(3, zero))
            further_units(2, 3, 4, 5)
            unit(2, lambda: select(4, zero))
            further_units(*range(6, N_TAB))
            close_table()
            looped(eng, step, 3, NE - 5, lambda k: unit(k, lambda: select(k + 2, zero)), 0)
            for j in range(2):
                expert = eng.value_load(tab_i[0:1, j:j + 1], min_val=0, max_val=NE - 1)
                unit(NE - 2 + j, lambda: select(expert, tab[:, 1, j:j + 1]))
            units = eng.value_load(tab_i[0:1, N_TAB:N_TAB + 1], min_val=NE, max_val=NE + MORE)
            with eng.Fori(NE, NE + MORE) as k:
                with eng.If(units > k):
                    expert = eng.value_load(tab_i[0:1, ds(k - NE, 1)], min_val=0, max_val=NE - 1)
                    eng.tensor_copy(gates[:, :, ds(k, 1)], gates[:, :, ds(expert, 1)]).then_inc(gates_kept, 1)
                    eng.wait_ge(gates_kept, k - NE + 1)
                    expert = eng.value_load(tab_i[0:1, ds(k - NE + 2, 1)], min_val=0, max_val=NE - 1)
                    unit(k, lambda: select(expert, tab[:, 1, ds(k - NE + 2, 1)]))
            final = eng.value_load(tab_i[0:1, N_TAB + 1:N_TAB + 2], min_val=NE - 1, max_val=NE + MORE - 1)
            y_low(final)
            add(final, 0)
            add(final, 1)
            for t in range(NT):
                eng.wait_ge(y_sq, t + 1)
                eng.tensor_scalar(stat[:, YRS + t:YRS + t + 1], stat[:, YSQ + t:YSQ + t + 1], 1.0 / D, EPS, ALU.mult, ALU.add)\
                   .then_inc(y_ms, 1)
            eng.wait_ge(fgain_in, 16)
            for t in range(NT):
                eng.wait_ge(y_rstd, t + 1)
                for j in range(2):
                    cs = slice(j * D // 2, (j + 1) * D // 2)
                    eng.scalar_tensor_tensor(out=yout[:, t, cs], in0=h_res[:, t, cs],
                                             scalar=stat[:, YRS + t:YRS + t + 1], in1=fgain[:, cs], op0=ALU.mult,
                                             op1=ALU.mult).then_inc(yout_ready, 1)

        @block.tensor
        def _(eng):
            eng.wait_ge(consts_ready, 1)
            eng.wait_ge(params_in, 16 * 8)
            eng.transpose(ps[:, 7, 0:N_ROWS], params[0:N_ROWS, :], ident[0:N_ROWS, 0:N_ROWS]).then_inc(params_turned, 1)
            def products(s, acc, act_hi, act_lo, t0, k, c):
                o = ps[:, acc, 0:act_hi.shape[2] - t0]
                eng.matmul(o, w_hi[s][:, c, :], act_hi[:, c, t0:], start=(k == 0), stop=False, skip_group_check=True)
                eng.matmul(o, w_hi[s][:, c, :], act_lo[:, c, t0:], start=False, stop=False, skip_group_check=True)
                return eng.matmul(o, w_lo[s][:, c, :], act_hi[:, c, t0:], start=False, stop=(k == KC - 1),
                                  skip_group_check=True)

            eng.wait_ge(xn_ready, 2)
            eng.wait_ge(xn1_ready, 1)
            LAG = 3
            for c in range(KC + LAG):
                if c < KC:
                    if c >= TURN_BANKS:
                        eng.wait_ge(xt_lo_ready, c - TURN_BANKS + 1)
                    cs = slice(c * P, (c + 1) * P)
                    eng.transpose(ps[:, 1 + c % TURN_BANKS, 0:NM], metan[:, cs], ident[0:NM, 0:NM])
                    eng.transpose(ps[:, 1 + c % TURN_BANKS, NM:NM + P], xn[:, 0, cs], ident[:, :])
                    eng.transpose(ps[:, 1 + c % TURN_BANKS, NM + P:T], xn[:, 1, cs], ident[:, :]).then_inc(xt_turned, 1)
                if c >= LAG:
                    if c == LAG:
                        eng.wait_ge(lo_ready, 1)
                    eng.wait_ge(xt_lo_ready, c - LAG + 1)
                    ins = products(0, 0, xt_hi, xt_lo, NM, c - LAG, c - LAG)
            ins.then_inc(chunk_done, 1)

            def chunk(n, s, acc, act_hi, act_lo, t0, extras=(), order=range(KC), freed=2):
                eng.wait_ge(lo_ready, n + 1)
                at_least(eng, acc_out, n - freed + 1)
                for k, c in enumerate(order):
                    if k in dict(extras):
                        dict(extras)[k]()
                    ins = products(s, acc, act_hi, act_lo, t0, k, c)
                ins.then_inc(chunk_done, 1)

            def turn_v(h):
                eng.wait_ge(acc_out, 3 * h + 3)
                if not is0(h):
                    eng.wait_ge(mix_lo_ready, h)
                eng.transpose(ps[:, 6, 0:P], v_t[:, NM:NM + P], ident[:, :])
                eng.transpose(ps[:, 6, P:TX], v_t[:, NM + P:T], ident[:, :])
                eng.transpose(ps[0:NM, 6, TX:TX + P], v_t[:, 0:NM], ident[:, :]).then_inc(v_turned, 1)

            def score(h):
                eng.wait_ge(acc_out, 3 * h + 2)
                at_least(eng, biased, h)
                for m in range(2):
                    rows = slice(DH * m, DH * (m + 1))
                    for t, c0, w in ((0, S0, K0), (1, S1, K1)):
                        ins = eng.matmul(ps[:, 3 + m, c0:c0 + w], q_t[rows, t * P:(t + 1) * P], k_t[rows, 0:w],
                                         start=True, stop=True)
                ins.then_inc(scores_done, 1)

            def turn_a(h):
                eng.wait_ge(a_ready, 2 * h + 2)
                at_least(eng, a_out, 3 * h)
                eng.transpose(ps[:, 5, 0:P], a_sb[:, S0 + NM:S0 + NM + P], ident[:, :])
                eng.transpose(ps[:, 5, P:TX], a_sb[:, S1 + NM:S1 + NM + P], ident[:, :])
                eng.transpose(ps[:, 5, TX + P:2 * TX], a_sb[:, S1 + NM + P:S1 + T], ident[:, :])
                eng.transpose(ps[0:NM, 7, 0:P], a_sb[:, S0:S0 + NM], ident[:, :])
                eng.transpose(ps[0:NM, 7, P:TX], a_sb[:, S1:S1 + NM], ident[:, :]).then_inc(a_turned, 1)

            def attend(h):
                eng.wait_ge(a_out, 3 * h + 3)
                eng.wait_ge(v_out, 2 * h + 2)
                at_least(eng, o_out, h)
                for t in range(NT):
                    o = ps[:, 7, TX + t * P:TX + (t + 1) * P]
                    q = slice(t * P, (t + 1) * P)
                    eng.matmul(o, at_m[:, q], v_meta[:, :], start=True, stop=False)
                    for k in range(t + 1):
                        ins = eng.matmul(o, at_x[:, k, q], v_tm[:, k, :], start=False, stop=(k == t))
                ins.then_inc(o_done, 1)

            def turn_o(h):
                eng.wait_ge(o_out, h + 1)
                eng.transpose(ps[:, 6, 0:P], o_sb[:, 0, :], ident[:, :])
                eng.transpose(ps[:, 6, P:TX], o_sb[:, 1, :], ident[:, :]).then_inc(o_turned, 1)

            def qkv(h):
                n = 3 * h
                if is0(h):
                    chunk(1, 1, 1, xt_hi, xt_lo, 0, freed=3)
                    chunk(2, 2, 2, xt_hi, xt_lo, 0, extras=[(6, lambda: score(0))], freed=3)
                    return
                chunk(n, 0, 0, xt_hi, xt_lo, NM, extras=[(7, lambda: turn_v(h - 1))], freed=3)
                chunk(n + 1, 1, 1, xt_hi, xt_lo, 0, extras=[(4, lambda: turn_a(h - 1)), (12, lambda: attend(h - 1))],
                      freed=3)
                chunk(n + 2, 2, 2, xt_hi, xt_lo, 0, extras=[(6, lambda: score(h)), (12, lambda: turn_o(h - 1))],
                      freed=3)

            qkv(0)
            qkv(1)
            with eng.Fori(2, HEADS) as h:
                qkv(h)

            def gates(g, b, i):
                eng.wait_ge(xc_ready, g + 1)
                eng.wait_ge(gates_in[b], 32 * (i + 1))
                at_least(eng, th_ri_ready, 2 * g)
                if is0(i) and b == 0:
                    eng.wait_ge(biased, HEADS)
                eng.matmul(ps[:, 3, 0:T], g_w[:, b, 0, :], xc[:, :], start=True, stop=True)
                eng.matmul(ps[:, 4, 0:T], g_w[:, b, 1, :], xc[:, :], start=True, stop=True).then_inc(gates_done, 1)

            def lru(i, b):
                g = 2 * i + b
                n = LRU0 + 2 * g
                h = HEADS - 1
                first = is0(i) and b == 0
                chunk(n, 2 * b, 0, xt_hi, xt_lo, 0, extras=[(4, lambda: turn_v(h)), (12, lambda: turn_a(h))]
                      if first else ())
                chunk(n + 1, 2 * b + 1, 1, xt_hi, xt_lo, NM,
                      extras=[(3, lambda: attend(h)), (10, lambda: gates(g, b, i)), (15, lambda: turn_o(h))]
                      if first else [(9, lambda: gates(g, b, i))])

            lru(0, 0)
            lru(0, 1)
            with eng.Fori(1, LB // 2) as i:
                lru(i, 0)
                lru(i, 1)

            def turn_back(m, b):
                eng.wait_ge(acc_out, OUT0 + m + 1)
                at_least(eng, h_ready, m)
                for t in range(NT):
                    ins = eng.transpose(ps[:, 3, t * P:(t + 1) * P], o_t[b][:, t * P:(t + 1) * P], ident[:, :])
                ins.then_inc(o_back, 1)

            def turn_h(m, b):
                eng.wait_ge(h_ready, m + 1)
                at_least(eng, h_t_ready, m)
                for t in range(NT):
                    ins = eng.transpose(ps[:, 4, t * P:(t + 1) * P], h_s[b][:, t, :], ident[:, :])
                ins.then_inc(h_turned, 1)

            def logits(m, b, last=False):
                eng.wait_ge(h_t_ready, m + 1)
                for t in range(NT):
                    ins = eng.matmul(ps[:, 5 + t, 0:NG + NE], h_tt[b][:, t * P:(t + 1) * P],
                                     rw[:, ds(m, 1), :].rearrange("p a e -> p (a e)"), start=is0(m), stop=last,
                                     skip_group_check=True)
                ins.then_inc(logits_done, 1)

            heads_first = list(range(LB, KC)) + list(range(LB))

            def mix_ready(c):
                k = HEADS + c + 1 if c < LB else c - LB + 1
                eng.wait_ge(mix_hi_ready, k)
                eng.wait_ge(mix_lo_ready, k)

            def project(i, s):
                m = RING * i + s
                extras = ()
                if not (is0(i) and s == 0):
                    b = (s - 1) % 2
                    extras = [(2, lambda: turn_back(m - 1, b)), (7, lambda: turn_h(m - 1, b)),
                              (13, lambda: logits(m - 1, b))]
                chunk(OUT0 + m, s, s % 2, mix_hi, mix_lo, 0, extras=extras, order=heads_first)

            eng.wait_ge(lo_ready, OUT0 + 1)
            eng.wait_ge(acc_out, OUT0 - 1)
            for k, c in enumerate(heads_first[:-1]):
                mix_ready(c)
                products(0, 0, mix_hi, mix_lo, 0, k, c)
            eng.wait_ge(lo_ready, OUT0 + 2)
            eng.wait_ge(acc_out, OUT0)
            for k, c in enumerate(heads_first[:KC // 2]):
                products(1, 1, mix_hi, mix_lo, 0, k, c)
            mix_ready(heads_first[-1])
            products(0, 0, mix_hi, mix_lo, 0, KC - 1, heads_first[-1]).then_inc(chunk_done, 1)
            for k, c in list(enumerate(heads_first))[KC // 2:]:
                if k == KC // 2 + 2:
                    turn_back(0, 0)
                if k == KC - 3:
                    turn_h(0, 0)
                ins = products(1, 1, mix_hi, mix_lo, 0, k, c)
            ins.then_inc(chunk_done, 1)
            logits(0, 0)
            for s in range(2, RING):
                project(0, s)
            with eng.Fori(1, N_OUT // RING) as i:
                for s in range(RING):
                    project(i, s)
            turn_back(N_OUT - 1, 1)
            turn_h(N_OUT - 1, 1)
            logits(N_OUT - 1, 1, last=True)

            eng.wait_ge(members, 1)
            m0, m1 = rt[:, 16, 0, :], rt[:, 16, 1, :]
            eng.matmul(ps[:, 3, 0:NE], ltri[:, :], m0, start=True, stop=True)
            eng.matmul(ps[:, 3, NE:2 * NE], ones[:, :], m0, start=True, stop=False)
            eng.matmul(ps[:, 3, NE:2 * NE], ltri[:, :], m1, start=False, stop=True)
            eng.matmul(ps[:, 4, 0:NE], ones[:, :], m0, start=True, stop=False)
            eng.matmul(ps[:, 4, 0:NE], ones[:, :], m1, start=False, stop=True).then_inc(ranks_done, 1)

            def gather(k):
                at_least(eng, added, 4 * (k - 1))
                for j in range(4):
                    for part, c0 in ((hn_hi, 2 * C), (hn_lo, 0)):
                        for t in range(NT):
                            ins = eng.matmul(ps[:, 3 + j, :], sel[:, t, c0:c0 + P],
                                             part[:, t, 4 * j:4 * j + 4, :].rearrange("p c q -> p (c q)"),
                                             start=(part is hn_hi and t == 0), stop=(part is hn_lo and t == NT - 1))
                    if j % 2 == 1:
                        ins.then_inc(gathered, 1)

            def lists(k):
                at_least(eng, x_even, 2 * k)
                for t in range(NT):
                    ins = eng.matmul(ps[:, 7, 0:1], sel[:, t, C:3 * C].bitcast(F32), stat[:, 86 + t:87 + t],
                                     start=(t == 0), stop=(t == NT - 1))
                ins.then_inc(listed, 1)

            def turn_x(k, j):
                eng.wait_ge((x_rows_left, x_rows_right)[j // 2], k + 1)
                if j >= 2:
                    eng.wait_ge((x_even, x_odd)[j % 2], 2 * k + 1)
                for c in range(4):
                    ins = eng.matmul(ps[:, 7 - 7 * (j % 2), c * P:(c + 1) * P], x_s[:, (4 * j + c) * P:(4 * j + c + 1) * P],
                                     ident_r[:, :], start=True, stop=True)
                ins.then_inc(x_turned, 1)

            def combine(k, t):
                for j in range(2):
                    if t == 0:
                        eng.wait_ge(y_lo_ready, 2 * k + j + 1)
                        eng.wait_ge(back_ready, k + 1)
                    else:
                        eng.wait_ge(added, 4 * k + j + 1)
                    for b in (2 * j, 2 * j + 1):
                        for y in (y_hi, y_lo):
                            ins = eng.matmul(ps[:, 3 + b, :], back[:, t * P:(t + 1) * P], y[:, b, :],
                                             start=(y is y_hi), stop=(y is y_lo))
                    ins.then_inc(combined, 1)

            def split_ready(k, s):
                if s in POOL_PARTS:
                    eng.wait_ge(m_lo_pool, len(POOL_PARTS) * k + POOL_PARTS.index(s) + 1)
                else:
                    done = sum(1 for q in range(s) if q not in POOL_PARTS)
                    eng.wait_ge(m_lo_dve, LO_DVE * k + done + 1)

            def hidden(k, acc, parts):
                for s in parts:
                    split_ready(k, s)
                    n = s % SLOTS
                    for c in range(2):
                        kc = 2 * (s % 8) + c
                        for w in (m_hi, m_lo):
                            ins = eng.matmul(ps[:, acc, :], x_hl[:, kc, :, :], w[n][:, c * F:(c + 1) * F],
                                             start=(kc == 0 and w is m_hi), stop=(kc == KC - 1 and w is m_lo))
                    ins.then_inc(part_used, 1)

            def turn(k, j):
                for f in range(FC):
                    ins = eng.matmul(ps[:, 2, (j * FC + f) * C:(j * FC + f + 1) * C], gu_sb[:, j, f * P:(f + 1) * P],
                                     pair[:, :], start=True, stop=True)
                ins.then_inc((g_turned, u_turned)[j], 1)

            def unit(k):
                eng.wait_ge(x_even, 2 * (k + 1))
                eng.wait_ge(x_odd, 2 * (k + 1))
                hidden(k, 0, range(0, 6))
                if not is0(k):
                    combine(k - 1, 0)
                hidden(k, 0, range(6, 8))
                hidden(k, 1, range(8, 9))
                if not is0(k):
                    combine(k - 1, 1)
                hidden(k, 1, range(9, 12))
                eng.wait_ge(g_copied, k + 1)
                turn(k, 0)
                eng.wait_ge(sel_ready, 2 * (k + 2))
                gather(k + 1)
                lists(k + 1)
                hidden(k, 1, range(12, 16))
                eng.wait_ge(tok_ready, k + 2)
                turn_x(k + 1, 0)
                turn_x(k + 1, 1)
                eng.wait_ge(u_copied, k + 1)
                eng.wait_ge(gated, k + 1)
                turn(k, 1)
                turn_x(k + 1, 2)
                turn_x(k + 1, 3)
                eng.wait_ge(h_ready_e, k + 1)
                for s in range(16, 24):
                    f = (s - 16) // 2
                    split_ready(k, s)
                    for b in range(2):
                        for w in (m_hi, m_lo):
                            ins = eng.matmul(ps[:, 3 + 2 * (s % 2) + b, :], h_hl[:, f, :, :],
                                             w[s % SLOTS][:, b * F:(b + 1) * F],
                                             start=(f == 0 and w is m_hi), stop=(f == FC - 1 and w is m_lo))
                    ins.then_inc(part_used, 1)

            eng.wait_ge(sel_ready, NT)
            lists(0)
            eng.wait_ge(hn_hi_ready, NT)
            eng.wait_ge(hn_lo_ready, NT)
            gather(0)
            eng.wait_ge(ident_r_ready, 1)
            eng.wait_ge(tok_ready, 1)
            for j in range(4):
                turn_x(0, j)
            unit(0)
            with eng.Fori(1, NE) as k:
                unit(k)
            eng.wait_ge(tab_ready, 1)
            units = eng.value_load(tab_i[0:1, N_TAB:N_TAB + 1], min_val=NE, max_val=NE + MORE)
            with eng.Fori(NE, NE + MORE) as k:
                with eng.If(units > k):
                    unit(k)
            final = eng.value_load(tab_i[0:1, N_TAB + 1:N_TAB + 2], min_val=NE - 1, max_val=NE + MORE - 1)
            combine(final, 0)
            combine(final, 1)

    return nc


_INS = ["x", "meta_tokens", "norm1_g", "w_in", "conv_w", "conv_b", "gate_a_w", "gate_a_b", "gate_x_w", "gate_x_b",
        "lru_a_param", "lambda_q1", "lambda_k1", "lambda_q2", "lambda_k2", "subln_g", "w_out", "norm2_g",
        "router_g_w", "router_g_b", "router_e_w", "router_e_b", "exp_w_gate", "exp_w_up", "exp_w_down",
        "final_norm_g"]


def kernel(**inputs):
    import numpy as np
    import concourse.bacc as bacc
    from concourse.bass_utils import run_bass_kernel_spmd

    nc = bacc.Bacc("TRN2", target_bir_lowering=False, num_devices=1)
    arrays, args = {}, []
    for name in _INS:
        a = np.ascontiguousarray(inputs[name])
        arrays[f"in_{name}"] = a
        args.append(nc.dram_tensor(f"in_{name}", a.shape, mybir.dt.from_np(a.dtype), kind="ExternalInput").ap())
    out = nc.dram_tensor("out", (1, TX, D), F32, kind="ExternalOutput").ap()
    build(nc, *args, out)
    r = run_bass_kernel_spmd(nc, [arrays], core_ids=[0])
    return r.results[0]["out"]
```
